# Optimizing a Trainium2 kernel written in Bass

```python
import jax, jax.numpy as jnp
from jax import lax
import numpy as np

D_MODEL = 1024
BATCH = 1
SEQ = 512
DEPTH = 2

GRID_W = 64
CTX_LEN = 256
N_MIXERS = 2
RET_HEADS = 4
RET_QK_DIM = D_MODEL // RET_HEADS
RET_V_DIM = 2 * D_MODEL // RET_HEADS
RET_CHUNK = 128
DECAY_EXP_FWD = 5.0
DECAY_EXP_BWD = 5.5
ROPE_BASE = 10000.0
CONV_WIDTH = 3
FFN_HIDDEN = -(-8 * D_MODEL // (3 * 256)) * 256
N_RET_LAYERS = (DEPTH + N_MIXERS - 1) // N_MIXERS
N_CONV_LAYERS = DEPTH // N_MIXERS
EPS = 1e-6


def rms_norm(x, gain=None):
    xf = x.astype(jnp.float32)
    y = xf * lax.rsqrt(jnp.mean(xf * xf, axis=-1, keepdims=True) + EPS)
    if gain is not None:
        y = y * gain.astype(jnp.float32)
    return y.astype(x.dtype)

def ada_params(cond, w, b):
    return jnp.split(jax.nn.silu(cond) @ w + b, 6, axis=-1)

def modulate(x, shift, scale):
    return x * (1 + scale) + shift

def rope_1d(x, pos):
    n = x.shape[-1] // 2
    freqs = ROPE_BASE ** (-jnp.arange(n, dtype=jnp.float32) / n)
    ang = pos.astype(jnp.float32)[:, None] * freqs[None, :]
    cos, sin = jnp.cos(ang).astype(x.dtype), jnp.sin(ang).astype(x.dtype)
    x1, x2 = x[..., :n], x[..., n:]
    return jnp.concatenate([x1 * cos - x2 * sin, x1 * sin + x2 * cos], axis=-1)

def rope_2d(x, row, col):
    half = x.shape[-1] // 2
    return jnp.concatenate([rope_1d(x[..., :half], row), rope_1d(x[..., half:], col)], axis=-1)

def retention_log_decays():
    h = jnp.arange(RET_HEADS, dtype=jnp.float32)
    lg_f = jnp.log1p(-jnp.exp2(-DECAY_EXP_FWD - h))
    lg_b = jnp.log1p(-jnp.exp2(-DECAY_EXP_BWD - h))
    return lg_f, lg_b

def retention_chunk_scan(q, k, v, log_g, s0):
    bsz, nh, L, _ = q.shape
    dv = v.shape[-1]
    n_chunks = L // RET_CHUNK

    def to_chunks(t):
        return t.reshape(bsz, nh, n_chunks, RET_CHUNK, t.shape[-1]).transpose(2, 0, 1, 3, 4)

    idx = jnp.arange(RET_CHUNK, dtype=jnp.float32)
    diff = idx[:, None] - idx[None, :]
    decay_mat = jnp.where(diff[None] >= 0,
                          jnp.exp(jnp.maximum(diff, 0.0)[None] * log_g[:, None, None]), 0.0)
    q_dec = jnp.exp((idx[None, :] + 1.0) * log_g[:, None])[None, :, :, None]
    k_dec = jnp.exp((RET_CHUNK - 1.0 - idx[None, :]) * log_g[:, None])[None, :, :, None]
    chunk_dec = jnp.exp(RET_CHUNK * log_g)[None, :, None, None]

    def step(s, inp):
        qc, kc, vc = inp
        scores = jnp.einsum('bhid,bhjd->bhij', qc, kc) * decay_mat[None]
        intra = jnp.einsum('bhij,bhje->bhie', scores, vc)
        cross = jnp.einsum('bhid,bhde->bhie', qc * q_dec, s)
        s_new = s * chunk_dec + jnp.einsum('bhjd,bhje->bhde', kc * k_dec, vc)
        return s_new, intra + cross

    _, out = lax.scan(step, s0, (to_chunks(q), to_chunks(k), to_chunks(v)))
    return out.transpose(1, 2, 0, 3, 4).reshape(bsz, nh, L, dv)

def context_state(k, v, log_g, reverse):
    L = k.shape[2]
    j = jnp.arange(L, dtype=jnp.float32)
    dist = j if reverse else (L - 1.0) - j
    w = jnp.exp(dist[None, :] * log_g[:, None])
    return jnp.einsum('bhld,bhle->bhde', k * w[None, :, :, None], v)

def context_parallel(q, k, v, lg_f, lg_b):
    L = q.shape[2]
    idx = jnp.arange(L, dtype=jnp.float32)
    diff = idx[:, None] - idx[None, :]
    d_f = jnp.where(diff[None] >= 0, jnp.exp(jnp.maximum(diff, 0.0)[None] * lg_f[:, None, None]), 0.0)
    d_b = jnp.where(diff[None] <= 0, jnp.exp(jnp.maximum(-diff, 0.0)[None] * lg_b[:, None, None]), 0.0)
    scores = jnp.einsum('bhid,bhjd->bhij', q, k) * (d_f + d_b)[None]
    return jnp.einsum('bhij,bhje->bhie', scores, v)

def retention_output(o, g, w_o):
    bsz, nh, L, dv = o.shape
    o = o * lax.rsqrt(jnp.mean(o * o, axis=-1, keepdims=True) + EPS)
    o = o.transpose(0, 2, 1, 3).reshape(bsz, L, nh * dv).astype(g.dtype)
    return (jax.nn.silu(g) * o) @ w_o

def retention_mixer(ax, ac, w_qkvg, w_o, row, col, with_ctx_out):
    D = D_MODEL
    scale = RET_QK_DIM ** -0.5

    def heads(t, d):
        return t.reshape(t.shape[0], t.shape[1], RET_HEADS, d).transpose(0, 2, 1, 3).astype(jnp.float32)

    qx, kx, vx, gx = jnp.split(ax @ w_qkvg, [D, 2 * D, 4 * D], axis=-1)
    qx = rope_2d(heads(qx, RET_QK_DIM), row, col)
    kx = rope_2d(heads(kx, RET_QK_DIM), row, col) * scale
    vx = heads(vx, RET_V_DIM)

    if with_ctx_out:
        qc, kc, vc, gc = jnp.split(ac @ w_qkvg, [D, 2 * D, 4 * D], axis=-1)
    else:
        kc, vc = jnp.split(ac @ w_qkvg[:, D:4 * D], [D], axis=-1)
    kc = heads(kc, RET_QK_DIM) * scale
    vc = heads(vc, RET_V_DIM)

    lg_f, lg_b = retention_log_decays()
    s_f = context_state(kc, vc, lg_f, reverse=False)
    s_b = context_state(kc, vc, lg_b, reverse=True)

    o_f = retention_chunk_scan(qx, kx, vx, lg_f, s_f)
    o_b = jnp.flip(retention_chunk_scan(jnp.flip(qx, 2), jnp.flip(kx, 2), jnp.flip(vx, 2), lg_b, s_b), 2)
    yx = retention_output(o_f + o_b, gx, w_o)

    yc = None
    if with_ctx_out:
        yc = retention_output(context_parallel(heads(qc, RET_QK_DIM), kc, vc, lg_f, lg_b), gc, w_o)
    return yx, yc

def short_conv(u, w):
    return lax.conv_general_dilated(
        u, w[:, None, :].astype(u.dtype), window_strides=(1,),
        padding=[(CONV_WIDTH // 2, CONV_WIDTH // 2)],
        dimension_numbers=('NWC', 'WIO', 'NWC'), feature_group_count=u.shape[-1])

def conv_mixer(h, w_in, w_conv, w_out):
    b_gate, c_gate, xv = jnp.split(h @ w_in, 3, axis=-1)
    return (b_gate * short_conv(c_gate * xv, w_conv)) @ w_out

def swiglu(h, w1, w3, w2):
    return (jax.nn.silu(h @ w1) * (h @ w3)) @ w2

def first_inputs(seed: int = 0) -> dict:
    key = jax.random.key(seed)
    ks = jax.random.split(key, 20)
    D, F = D_MODEL, FFN_HIDDEN
    nrm = jax.random.normal
    f32 = jnp.float32
    return {
        "x": nrm(ks[0], (BATCH, SEQ, D), f32),
        "c": nrm(ks[1], (BATCH, D), f32),
        "ctx": nrm(ks[2], (BATCH, CTX_LEN, D), f32),
        "c_ctx": nrm(ks[3], (D,), f32),
        "ada_w": nrm(ks[4], (DEPTH, D, 6 * D), f32) * (0.5 * D ** -0.5),
        "ada_b": nrm(ks[5], (DEPTH, 6 * D), f32) * 0.02,
        "norm_mix": 1.0 + 0.02 * nrm(ks[6], (DEPTH, D), f32),
        "norm_ffn": 1.0 + 0.02 * nrm(ks[7], (DEPTH, D), f32),
        "ret_w_qkvg": nrm(ks[8], (N_RET_LAYERS, D, 6 * D), f32) * D ** -0.5,
        "ret_w_o": nrm(ks[9], (N_RET_LAYERS, 2 * D, D), f32) * (2 * D) ** -0.5,
        "conv_w_in": nrm(ks[10], (N_CONV_LAYERS, D, 3 * D), f32) * D ** -0.5,
        "conv_w": nrm(ks[11], (N_CONV_LAYERS, CONV_WIDTH, D), f32) * CONV_WIDTH ** -0.5,
        "conv_w_out": nrm(ks[12], (N_CONV_LAYERS, D, D), f32) * D ** -0.5,
        "ffn_w1": nrm(ks[13], (DEPTH, D, F), f32) * D ** -0.5,
        "ffn_w3": nrm(ks[14], (DEPTH, D, F), f32) * D ** -0.5,
        "ffn_w2": nrm(ks[15], (DEPTH, F, D), f32) * F ** -0.5,
        "final_norm": 1.0 + 0.02 * nrm(ks[16], (D,), f32),
    }

def first_block(x, c, ctx, c_ctx, ada_w, ada_b, norm_mix, norm_ffn, ret_w_qkvg, ret_w_o,
              conv_w_in, conv_w, conv_w_out, ffn_w1, ffn_w3, ffn_w2, final_norm):
    T = x.shape[1]
    rows = T // GRID_W
    row = jnp.repeat(jnp.arange(rows, dtype=jnp.int32), GRID_W)
    col = jnp.tile(jnp.arange(GRID_W, dtype=jnp.int32), rows)

    hx, hc = x, ctx
    for i in range(DEPTH):
        mixer = i % N_MIXERS
        ctx_needed = any(j % N_MIXERS == 0 for j in range(i + 1, DEPTH))
        sh1, sc1, g1, sh2, sc2, g2 = [t[:, None, :] for t in ada_params(c, ada_w[i], ada_b[i])]
        ax = modulate(rms_norm(hx, norm_mix[i]), sh1, sc1)
        if mixer == 0 or ctx_needed:
            csh1, csc1, cg1, csh2, csc2, cg2 = ada_params(c_ctx, ada_w[i], ada_b[i])
            ac = modulate(rms_norm(hc, norm_mix[i]), csh1, csc1)

        if mixer == 0:
            r = i // N_MIXERS
            yx, yc = retention_mixer(ax, ac, ret_w_qkvg[r], ret_w_o[r], row, col, ctx_needed)
        else:
            r = i // N_MIXERS
            yx = conv_mixer(ax, conv_w_in[r], conv_w[r], conv_w_out[r])
            yc = conv_mixer(ac, conv_w_in[r], conv_w[r], conv_w_out[r]) if ctx_needed else None

        hx = hx + g1 * yx
        fx = modulate(rms_norm(hx, norm_ffn[i]), sh2, sc2)
        hx = hx + g2 * swiglu(fx, ffn_w1[i], ffn_w3[i], ffn_w2[i])

        if ctx_needed:
            hc = hc + cg1 * yc
            fc = modulate(rms_norm(hc, norm_ffn[i]), csh2, csc2)
            hc = hc + cg2 * swiglu(fc, ffn_w1[i], ffn_w3[i], ffn_w2[i])

    return rms_norm(hx, final_norm)


DEPTH_2 = 1

CHUNK = 64
Q_BLOCK = 128
NORM_EPS = 1e-6

GDN_HEADS = 4
GDN_HEAD_DIM = 128
GDN_WIDTH = GDN_HEADS * GDN_HEAD_DIM
CONV_WIDTH_2 = 4

MLA_HEADS = 8
MLA_NOPE_DIM = 64
MLA_ROPE_DIM = 32
MLA_V_DIM = 64
MLA_Q_RANK = 256
MLA_KV_RANK = 128
MLA_WIDTH = MLA_HEADS * MLA_V_DIM
ROPE_THETA = 10000.0

MIX_WIDTH = GDN_WIDTH + MLA_WIDTH
D_FF = 4 * D_MODEL

IN_SIZES = (GDN_WIDTH, GDN_WIDTH, GDN_WIDTH, GDN_WIDTH, GDN_HEADS, GDN_HEADS,
            MLA_Q_RANK, MLA_KV_RANK, MLA_ROPE_DIM)
IN_WIDTH = 4 * GDN_WIDTH + 2 * GDN_HEADS + MLA_Q_RANK + MLA_KV_RANK + MLA_ROPE_DIM


def rms_norm_2(x, gain):
    xf = x.astype(jnp.float32)
    y = xf * lax.rsqrt(jnp.mean(xf * xf, axis=-1, keepdims=True) + NORM_EPS)
    return (y * gain.astype(jnp.float32)).astype(x.dtype)

def l2_norm(x):
    xf = x.astype(jnp.float32)
    return xf * lax.rsqrt(jnp.sum(xf * xf, axis=-1, keepdims=True) + NORM_EPS)

def causal_depthwise_conv(x, w):
    k = w.shape[0]
    return lax.conv_general_dilated(
        x, w[:, None, :].astype(x.dtype), window_strides=(1,), padding=[(k - 1, 0)],
        dimension_numbers=("NWC", "WIO", "NWC"), feature_group_count=x.shape[-1])

def rope_angles(positions):
    inv_freq = ROPE_THETA ** (-jnp.arange(0, MLA_ROPE_DIM, 2, dtype=jnp.float32) / MLA_ROPE_DIM)
    ang = positions.astype(jnp.float32)[..., None] * inv_freq
    return jnp.cos(ang), jnp.sin(ang)

def apply_rope(x, cos, sin):
    xf = x.astype(jnp.float32)
    x1, x2 = jnp.split(xf, 2, axis=-1)
    return jnp.concatenate([x1 * cos - x2 * sin, x2 * cos + x1 * sin], axis=-1).astype(x.dtype)

def gated_delta_rule(q, k, v, beta, log_a):
    b, s, h, dk = q.shape
    dv = v.shape[-1]
    n = s // CHUNK

    def chunks(t):
        t = t.reshape((b, n, CHUNK, h) + t.shape[3:])
        return jnp.moveaxis(t, 3, 1)

    q, k, v = chunks(q), chunks(k), chunks(v)
    beta, log_a = chunks(beta), chunks(log_a)
    g = jnp.cumsum(log_a, axis=-1)
    idx = jnp.arange(CHUNK)
    strict = idx[:, None] > idx[None, :]
    causal = idx[:, None] >= idx[None, :]
    gdiff = g[..., :, None] - g[..., None, :]
    decay_strict = jnp.exp(jnp.where(strict, gdiff, -jnp.inf))
    decay_causal = jnp.exp(jnp.where(causal, gdiff, -jnp.inf))

    k_beta = k * beta[..., None]
    a_mat = jnp.einsum("bhnid,bhnjd->bhnij", k_beta, k) * decay_strict
    eye = jnp.eye(CHUNK, dtype=jnp.float32)
    t_inv = lax.linalg.triangular_solve(eye + a_mat, jnp.broadcast_to(eye, a_mat.shape),
                                        left_side=True, lower=True)
    u = t_inv @ (v * beta[..., None])
    w = t_inv @ (k_beta * jnp.exp(g)[..., None])
    p = jnp.einsum("bhnid,bhnjd->bhnij", q, k) * decay_causal
    q_dec = q * jnp.exp(g)[..., None]
    g_last = g[..., -1]
    k_dec = k * jnp.exp(g_last[..., None] - g)[..., None]

    def step(state, xs):
        q_c, k_c, u_c, w_c, p_c, gl = xs
        v_new = u_c - jnp.einsum("bhcd,bhde->bhce", w_c, state)
        o = (jnp.einsum("bhcd,bhde->bhce", q_c, state)
             + jnp.einsum("bhij,bhje->bhie", p_c, v_new))
        state = state * jnp.exp(gl)[..., None, None] + jnp.einsum("bhcd,bhce->bhde", k_c, v_new)
        return state, o

    xs = tuple(jnp.moveaxis(t, 2, 0) for t in (q_dec, k_dec, u, w, p, g_last))
    state0 = jnp.zeros((b, h, dk, dv), jnp.float32)
    _, o = lax.scan(step, state0, xs)
    return jnp.transpose(o, (1, 0, 3, 2, 4)).reshape(b, s, h, dv)

def gated_deltanet_group(q, k, v, gate, a_logit, b_logit, conv_w, a_log, dt_bias, out_norm):
    bsz, s, _ = q.shape
    qkv = jax.nn.silu(causal_depthwise_conv(jnp.concatenate([q, k, v], axis=-1), conv_w))
    q, k, v = jnp.split(qkv, 3, axis=-1)
    q = l2_norm(q.reshape(bsz, s, GDN_HEADS, GDN_HEAD_DIM)) * (GDN_HEAD_DIM ** -0.5)
    k = l2_norm(k.reshape(bsz, s, GDN_HEADS, GDN_HEAD_DIM))
    v = v.reshape(bsz, s, GDN_HEADS, GDN_HEAD_DIM).astype(jnp.float32)
    beta = jax.nn.sigmoid(b_logit.astype(jnp.float32))
    log_a = -jnp.exp(a_log.astype(jnp.float32)) * jax.nn.softplus(
        a_logit.astype(jnp.float32) + dt_bias.astype(jnp.float32))
    o = gated_delta_rule(q, k, v, beta, log_a)
    g = jax.nn.silu(gate.astype(jnp.float32)).reshape(bsz, s, GDN_HEADS, GDN_HEAD_DIM)
    o = rms_norm_2(o, out_norm) * g
    return o.reshape(bsz, s, GDN_WIDTH).astype(gate.dtype)

def mla_group(c_q, c_kv, k_rope, cos, sin, q_norm, w_q_up, kv_norm, w_kv_up):
    b, s, _ = c_q.shape
    dqk = MLA_NOPE_DIM + MLA_ROPE_DIM
    q = (rms_norm_2(c_q, q_norm) @ w_q_up).reshape(b, s, MLA_HEADS, dqk)
    q_nope, q_rope = q[..., :MLA_NOPE_DIM], q[..., MLA_NOPE_DIM:]
    kv = (rms_norm_2(c_kv, kv_norm) @ w_kv_up).reshape(b, s, MLA_HEADS, MLA_NOPE_DIM + MLA_V_DIM)
    k_nope, v = kv[..., :MLA_NOPE_DIM], kv[..., MLA_NOPE_DIM:]
    q_rope = apply_rope(q_rope, cos[:, :, None, :], sin[:, :, None, :])
    k_rope = apply_rope(k_rope, cos, sin)
    q = jnp.concatenate([q_nope, q_rope], axis=-1)
    k = jnp.concatenate(
        [k_nope, jnp.broadcast_to(k_rope[:, :, None, :], (b, s, MLA_HEADS, MLA_ROPE_DIM))], axis=-1)
    scale = dqk ** -0.5
    n_blk = s // Q_BLOCK
    q_blocks = jnp.moveaxis(q.reshape(b, n_blk, Q_BLOCK, MLA_HEADS, dqk), 1, 0)
    key_chunk = jnp.arange(s) // CHUNK

    def attend(xs):
        q_b, blk = xs
        q_chunk = (blk * Q_BLOCK + jnp.arange(Q_BLOCK)) // CHUNK
        scores = jnp.einsum("bqhd,bkhd->bhqk", q_b, k,
                            preferred_element_type=jnp.float32) * scale
        mask = key_chunk[None, :] <= q_chunk[:, None]
        probs = jax.nn.softmax(jnp.where(mask, scores, -jnp.inf), axis=-1).astype(v.dtype)
        return jnp.einsum("bhqk,bkhd->bqhd", probs, v)

    o = lax.map(attend, (q_blocks, jnp.arange(n_blk)))
    return jnp.moveaxis(o, 0, 1).reshape(b, s, MLA_WIDTH)

def second_inputs(seed: int = 0) -> dict:
    key = jax.random.key(seed)
    ks = jax.random.split(key, 20)
    f32 = jnp.float32

    def normal(k, shape, fan_in):
        return jax.random.normal(k, shape, f32) * (fan_in ** -0.5)

    def gain(k, shape):
        return 1.0 + 0.1 * jax.random.normal(k, shape, f32)

    x = jax.random.normal(ks[0], (BATCH, SEQ, D_MODEL), f32)
    offsets = jax.random.randint(ks[1], (BATCH, 1), 0, 4096)
    positions = (offsets + jnp.arange(SEQ)[None, :]).astype(jnp.int32)
    a_log = jnp.log(jax.random.uniform(ks[2], (DEPTH_2, GDN_HEADS), f32, 1.0, 16.0))
    dt = jnp.exp(jax.random.uniform(ks[3], (DEPTH_2, GDN_HEADS), f32,
                                    float(np.log(1e-3)), float(np.log(1e-1))))
    dt_bias = dt + jnp.log(-jnp.expm1(-dt))
    return {
        "x": x,
        "positions": positions,
        "mix_pre_norm": gain(ks[4], (DEPTH_2, D_MODEL)),
        "w_in": normal(ks[5], (DEPTH_2, D_MODEL, IN_WIDTH), D_MODEL),
        "conv_w": normal(ks[6], (DEPTH_2, CONV_WIDTH_2, 3 * GDN_WIDTH), CONV_WIDTH_2),
        "a_log": a_log,
        "dt_bias": dt_bias,
        "gdn_out_norm": gain(ks[7], (DEPTH_2, GDN_HEAD_DIM)),
        "q_norm": gain(ks[8], (DEPTH_2, MLA_Q_RANK)),
        "w_q_up": normal(ks[9], (DEPTH_2, MLA_Q_RANK, MLA_HEADS * (MLA_NOPE_DIM + MLA_ROPE_DIM)), MLA_Q_RANK),
        "kv_norm": gain(ks[10], (DEPTH_2, MLA_KV_RANK)),
        "w_kv_up": normal(ks[11], (DEPTH_2, MLA_KV_RANK, MLA_HEADS * (MLA_NOPE_DIM + MLA_V_DIM)), MLA_KV_RANK),
        "w_out": normal(ks[12], (DEPTH_2, MIX_WIDTH, D_MODEL), MIX_WIDTH),
        "mix_post_norm": gain(ks[13], (DEPTH_2, D_MODEL)),
        "ffn_pre_norm": gain(ks[14], (DEPTH_2, D_MODEL)),
        "w_up": normal(ks[15], (DEPTH_2, D_MODEL, D_FF), D_MODEL),
        "w_down": normal(ks[16], (DEPTH_2, D_FF, D_MODEL), D_FF),
        "ffn_post_norm": gain(ks[17], (DEPTH_2, D_MODEL)),
    }

def second_block(x, positions, mix_pre_norm, w_in, conv_w, a_log, dt_bias, gdn_out_norm,
              q_norm, w_q_up, kv_norm, w_kv_up, w_out, mix_post_norm,
              ffn_pre_norm, w_up, w_down, ffn_post_norm):
    cos, sin = rope_angles(positions)
    offsets = [int(o) for o in np.cumsum(IN_SIZES)[:-1]]
    for l in range(DEPTH_2):
        h = rms_norm_2(x, mix_pre_norm[l])
        proj = h @ w_in[l]
        gq, gk, gv, gg, ga, gb, cq, ckv, kr = jnp.split(proj, offsets, axis=-1)
        o_gdn = gated_deltanet_group(gq, gk, gv, gg, ga, gb, conv_w[l], a_log[l],
                                     dt_bias[l], gdn_out_norm[l])
        o_mla = mla_group(cq, ckv, kr, cos, sin, q_norm[l], w_q_up[l], kv_norm[l], w_kv_up[l])
        mixed = jnp.concatenate([o_gdn.astype(x.dtype), o_mla.astype(x.dtype)], axis=-1) @ w_out[l]
        x = x + rms_norm_2(mixed, mix_post_norm[l])
        h = rms_norm_2(x, ffn_pre_norm[l])
        f = jnp.square(jax.nn.relu(h @ w_up[l])) @ w_down[l]
        x = x + rms_norm_2(f, ffn_post_norm[l])
    return x


def setup_inputs(seed=0):
    out = dict(first_inputs(seed))
    for name, value in second_inputs(seed + 1).items():
        if name != "x":
            out[name + "_2"] = value
    return out


def reference(
    x, c, ctx, c_ctx, ada_w, ada_b, norm_mix, norm_ffn, ret_w_qkvg, ret_w_o, conv_w_in, conv_w,
    conv_w_out, ffn_w1, ffn_w3, ffn_w2, final_norm, positions_2, mix_pre_norm_2, w_in_2,
    conv_w_2, a_log_2, dt_bias_2, gdn_out_norm_2, q_norm_2, w_q_up_2, kv_norm_2, w_kv_up_2,
    w_out_2, mix_post_norm_2, ffn_pre_norm_2, w_up_2, w_down_2, ffn_post_norm_2,
):
    x = first_block(
        x, c, ctx, c_ctx, ada_w, ada_b, norm_mix, norm_ffn, ret_w_qkvg, ret_w_o, conv_w_in,
        conv_w, conv_w_out, ffn_w1, ffn_w3, ffn_w2, final_norm,
    )
    return second_block(
        x, positions_2, mix_pre_norm_2, w_in_2, conv_w_2, a_log_2, dt_bias_2, gdn_out_norm_2,
        q_norm_2, w_q_up_2, kv_norm_2, w_kv_up_2, w_out_2, mix_post_norm_2, ffn_pre_norm_2,
        w_up_2, w_down_2, ffn_post_norm_2,
    )


_drawn_inputs = setup_inputs


def setup_inputs(seed=0):
    import zlib

    import numpy as np

    out = dict(_drawn_inputs(seed))
    spreads = {}
    factors = {'norm_mix': 2.668, 'norm_ffn': 4.438, 'q_norm_2': 3.432}
    for name, (base, spread) in spreads.items():
        noise = np.random.default_rng([zlib.crc32(name.encode()), seed]).standard_normal(out[name].shape)
        drawn = base * np.exp(spread * noise) if base else spread * noise
        out[name] = __import__('jax').numpy.asarray(drawn.astype(out[name].dtype))
    for name, factor in factors.items():
        out[name] = (out[name] * factor).astype(out[name].dtype)
    return out
```

```python
from contextlib import ExitStack

import numpy as np

import concourse.bass as bass
from concourse import mybir

P = 128
D = 1024
KT = D // P
T = 512
TT = T // P
C = 256
CT = C // P
EPS = 1e-6
SLAB = 2048

RH = 4
RD = D // RH
RV = 2 * D // RH
RDT, RVT = RD // P, RV // P
KEYT = TT + CT
TOEP_X = T + (TT - 1) * P
TOEP_C = T + (CT - 1) * P
GRID_W = 64

FT = 22
FCH = (12, 10)
F2T = 32
F2CH = (16, 16)

GH = 4
MH = 8
NOPE, ROPE, MV = 64, 32, 64
QK = NOPE + ROPE
NCONV = 12
LEVELS = 7
NEG = -1.0e30

CON = {}
_at = 0
for _name, _n in (("ident", P), ("upper", P), ("causal", P), ("mask_q", P), ("mask_k", P), ("levels", LEVELS * P),
                  ("freq", 1), ("turn", 1), ("phase", 1), ("sign", 1)):
    CON[_name] = _at
    _at += _n
N_CON = _at

RET = 0
FFN0 = RET + 8 * RH
CONV = FFN0 + FT + FT // 2
FFN1 = CONV + 16
MIX = FFN1 + FT + FT // 2
FFN2 = MIX + 16
N_SLABS = FFN2 + F2T // 2 + F2T // 2
STAGES = ("ret", "ffn0", "conv", "ffn1", "mix", "all")
UPTO = "all"
ENDS = {"ret": FFN0 + 2, "ffn0": CONV, "conv": FFN1 + 2, "ffn1": MIX, "mix": FFN2 + 2, "all": N_SLABS}

N_ADA = 48

VEC = {}
_at = 0
for _name, _n in (("ada_b", 96), ("c", 8), ("c_ctx", 8), ("norm_mix", 16), ("norm_ffn", 16), ("final_norm", 8),
                  ("mix_pre", 8), ("mix_post", 8), ("ffn_pre", 8), ("ffn_post", 8), ("conv_w", 24),
                  ("conv_w_2", 48), ("gdn_out", 1), ("q_norm", 2), ("kv_norm", 1)):
    VEC[_name] = _at
    _at += _n
N_VEC = _at

F32 = mybir.dt.float32
F32R = mybir.dt.float32r
I32 = mybir.dt.int32
ALU = mybir.AluOpType
ACT = mybir.ActivationFunctionType
AX = mybir.AxisListType


def build(nc, slabs, ada, x_in, ctx_in, vecs, decay, rope1, consts, positions, per_head, out):
    done_at = STAGES.index(UPTO)
    n_slabs = ENDS[UPTO]

    def has(stage):
        return STAGES.index(stage) <= done_at

    with ExitStack() as ctx:
        def sem(name):
            return ctx.enter_context(nc.semaphore(name))

        def sb(name, shape, dt=F32, scope=ctx):
            return scope.enter_context(nc.sbuf_tensor(name, shape, dt))

        PS = ctx.enter_context(nc.psum_tensor("PS", [P, 8, 512], F32))
        raw = sb("raw", [P, 2, SLAB])
        w_hi = sb("w_hi", [P, 2, SLAB], F32R)
        w_lo = sb("w_lo", [P, 2, SLAB], F32R)
        x = sb("x", [P, KT, T])
        vec = sb("vec", [P, N_VEC])
        silu_c = sb("silu_c", [P, KT, 2])
        mod = sb("mod", [P, 2 * 6 * KT])
        mod_ctx = sb("mod_ctx", [P, 2 * KT])
        gain = sb("gain", [P, 5, KT])
        ones = sb("ones", [P, P])
        eps = sb("eps", [P, 1])
        std = sb("std", [P, T])
        rstd = sb("rstd", [P, T])
        normed = sb("normed", [P, 2, T])
        acc = sb("acc", [P, D])
        sq = acc[:, :].rearrange("p (two t) -> p two t", two=2)

        with ExitStack() as own:
            act_hi = sb("act_hi", [P, KT, T], F32R, own)
            act_lo = sb("act_lo", [P, KT, T], F32R, own)
            early = own.enter_context(ExitStack())
            ada_raw = sb("ada_raw", [P, 2, SLAB], F32, early)
            with ExitStack() as ret:
                ctx_hi = sb("ctx_hi", [P, KT, C], F32R, ret)
                ctx_lo = sb("ctx_lo", [P, KT, C], F32R, ret)
                rq = sb("rq", [P, RDT, T], F32, ret)
                rk = sb("rk", [P, RDT, T + C], F32, ret)
                rv = sb("rv", [P, KEYT, RV], F32, ret)
                rs = sb("rs", [P, KEYT, T], F32, ret)
                rg = sb("rg", [P, RVT, T], F32, ret)
                ry_hi = sb("ry_hi", [P, RVT, T], F32R, ret)
                ry_lo = sb("ry_lo", [P, RVT, T], F32R, ret)
                toep = sb("toep", [P, TOEP_X + TOEP_C], F32, ret)
                rope = sb("rope", [P, 2 * (T // GRID_W + GRID_W)], F32, ret)
                xc = rs[:, 0:4, :].rearrange("p a b -> p (a b)").rearrange("p (k t) -> p k t", k=KT)
            with ExitStack() as ffn:
                hid_hi = sb("hid_hi", [P, FCH[0], T], F32R, ffn)
                hid_lo = sb("hid_lo", [P, FCH[0], T], F32R, ffn)
                sg = sb("sg", [P, 2, T], F32, ffn)
                hraw = sb("hraw", [P, 2, T], F32, ffn)
                u = sb("u", [P, KT, T + 2], F32, ffn)
            early.close()
            with ExitStack() as mix:
                qkv = sb("qkv", [P, NCONV, T], F32, mix)
                gate = sb("gate", [P, GH, T], F32, mix)
                con = sb("con", [P, N_CON], F32, mix)
                heads_c = sb("heads_c", [P, 2 * GH], F32, mix)
                ab = sb("ab", [P, TT, 2 * GH], F32, mix)
                rowsrc = sb("rowsrc", [P, TT, 3 * GH], F32, mix)
                cols = sb("cols", [P, 12, TT, GH], F32, mix)
                ssqk = sb("ssqk", [P, TT, 2 * GH], F32, mix)
                csn = sb("csn", [P, T], F32, mix)
                small = sb("small", [P, 3, 4], F32, mix)
                with ExitStack() as mla:
                    cvin = sb("cvin", [P, 4, T + 3], F32, mla)
                    cv = sb("cv", [P, 4, T], F32, mla)
                    cqr = sb("cqr", [P, 3, T], F32, mla)
                    krope = sb("krope", [P, T], F32, mla)
                    mc_hi = sb("mc_hi", [P, 3, T], F32R, mla)
                    mc_lo = sb("mc_lo", [P, 3, T], F32R, mla)
                    mstd = sb("mstd", [P, 2, T], F32, mla)
                    qh = cv[:, 2:4, :]
                    kh = sb("kh", [P, 2, T], F32, mla)
                    mv = sb("mv", [P, TT, MH * MV], F32, mla)
                    pr = cv[:, 0:2, :]
                    prt = cvin[:, :, 0:T]
                    pos_i = cv[:, 0, :].bitcast(I32)
                with ExitStack() as gdn:
                    mt = sb("mt", [P, TT, T], F32, gdn)
                    gx = sb("gx", [P, TT, T], F32, gdn)
                    gy = sb("gy", [P, TT, T], F32, gdn)
                    gp = sb("gp", [P, TT, T], F32, gdn)
                    ptm = sb("ptm", [P, TT, T], F32, gdn)
                    kbg = sb("kbg", [P, TT, T], F32, gdn)
                    lv = sb("lv", [P, 2, T], F32, gdn)
                    ex = sb("ex", [P, T], F32, gdn)
                    egrow = sb("egrow", [P, T], F32, gdn)
                    bcs = gx[:, 0:3, :].rearrange("p a (b i) -> p (a b) i", i=P)
                    state = lv[:, 0, :].rearrange("p (h i) -> p h i", h=GH)
            with ExitStack() as ffn2:
                facc = sb("facc", [P, KT, T], F32, ffn2)
                hid2_hi = sb("hid2_hi", [P, 16, T], F32R, ffn2)
                hid2_lo = sb("hid2_lo", [P, 16, T], F32R, ffn2)
                sg2 = sb("sg2", [P, 2, T], F32, ffn2)
                hraw2 = sb("hraw2", [P, 2, T], F32, ffn2)

        slab_landed = [sem(f"slab_landed{j}") for j in range(2)]
        w_hi_done = sem("w_hi_done")
        w_lo_done = sem("w_lo_done")
        slab_done = sem("slab_done")
        vec_landed = sem("vec_landed")
        x_landed = sem("x_landed")
        xc_landed = sem("xc_landed")
        rope_landed = sem("rope_landed")
        toep_landed = sem("toep_landed")
        ada_landed = [sem(f"ada_landed{j}") for j in range(2)]
        ada_used = sem("ada_used")
        consts_set = sem("consts_set")
        silu_c_done = sem("silu_c_done")
        mod0_summed = sem("mod0_summed")
        gain_done = sem("gain_done")
        sq_ready = sem("sq_ready")
        sq_used = sem("sq_used")
        std_ready = sem("std_ready")
        y_ready = sem("y_ready")
        hi_ready = sem("hi_ready")
        lo_ready = sem("lo_ready")
        banks_free = sem("banks_free")
        rope_read = sem("rope_read")
        roped = sem("roped")
        kctx_done = sem("kctx_done")
        v_done = sem("v_done")
        s_ready = sem("s_ready")
        s_decayed = sem("s_decayed")
        g_done = sem("g_done")
        pv_ready = sem("pv_ready")
        osq_ready = sem("osq_ready")
        osum_ready = sem("osum_ready")
        ostd_ready = sem("ostd_ready")
        ry_ready = sem("ry_ready")
        ry_hi_done = sem("ry_hi_done")
        ry_lo_done = sem("ry_lo_done")
        acc_ready = sem("acc_ready")
        unit_summed = sem("unit_summed")
        unit_done = sem("unit_done")
        act_silu = sem("act_silu")
        hraw_ready = sem("hraw_ready")
        hid_hi_done = sem("hid_hi_done")
        hid_lo_done = sem("hid_lo_done")
        pads_zero = sem("pads_zero")
        conv_step = sem("conv_step")
        conv_y = sem("conv_y")
        wout_added = sem("wout_added")
        down_added = sem("down_added")
        x_final = sem("x_final")
        out_stored = sem("out_stored")
        vchain = sem("vchain")
        unit_step = sem("unit_step")
        final_done = sem("final_done")
        con_landed = sem("con_landed")
        pos_landed = sem("pos_landed")
        heads_landed = sem("heads_landed")
        cvin_done = sem("cvin_done")
        conv2_step = sem("conv2_step")
        conv2_done = sem("conv2_done")
        silu2_done = sem("silu2_done")
        gate2_done = sem("gate2_done")
        cqr_done = sem("cqr_done")
        ab_done = sem("ab_done")
        msq_ready = sem("msq_ready")
        msum_ready = sem("msum_ready")
        mstd_done = sem("mstd_done")
        mc_ready = sem("mc_ready")
        mc_hi_done = sem("mc_hi_done")
        mc_lo_done = sem("mc_lo_done")
        mv_ready = sem("mv_ready")
        mv_done = sem("mv_done")
        krope_done = sem("krope_done")
        kr_copied = sem("kr_copied")
        q_ready = sem("q_ready")
        k_ready = sem("k_ready")
        qn_done = sem("qn_done")
        qr_done = sem("qr_done")
        kn_done = sem("kn_done")
        ms_ready = sem("ms_ready")
        nmx_done = sem("nmx_done")
        exp_done = sem("exp_done")
        p_ready = sem("p_ready")
        t_ready = sem("t_ready")
        prt_done = sem("prt_done")
        o2_ready = sem("o2_ready")
        mo_hi_done = sem("mo_hi_done")
        mo_lo_done = sem("mo_lo_done")
        trig_step = sem("trig_step")
        trig_ready = sem("trig_ready")
        trig_done = sem("trig_done")
        qsq_ready = sem("qsq_ready")
        qsq_used = sem("qsq_used")
        ss_ready = sem("ss_ready")
        ssd_done = sem("ssd_done")
        gcum_ready = sem("gcum_ready")
        soft1 = sem("soft1")
        soft2 = sem("soft2")
        beta1 = sem("beta1")
        cols_done = sem("cols_done")
        rows_ready = sem("rows_ready")
        bcs_done = sem("bcs_done")
        eraw_done = sem("eraw_done")
        e_done = sem("e_done")
        kd_raw = sem("kd_raw")
        kd_exp = sem("kd_exp")
        kd_done = sem("kd_done")
        kq_ready = sem("kq_ready")
        mt_done = sem("mt_done")
        ptm_done = sem("ptm_done")
        qdec_done = sem("qdec_done")
        kvt_done = sem("kvt_done")
        y0_done = sem("y0_done")
        x0_ready = sem("x0_ready")
        x0_done = sem("x0_done")
        lv_done = sem("lv_done")
        lp_ready = sem("lp_ready")
        lp_done = sem("lp_done")
        xx_ready = sem("xx_ready")
        xy_done = sem("xy_done")
        uw_ready = sem("uw_ready")
        u_done = sem("u_done")
        wt_done = sem("wt_done")
        ws_ready = sem("ws_ready")
        vn_done = sem("vn_done")
        o3_ready = sem("o3_ready")
        o3_done = sem("o3_done")
        sup_ready = sem("sup_ready")
        state_done = sem("state_done")
        gsq_ready = sem("gsq_ready")
        gss_ready = sem("gss_ready")
        gstd_done = sem("gstd_done")
        go_ready = sem("go_ready")
        go_hi_done = sem("go_hi_done")
        go_lo_done = sem("go_lo_done")
        f_free = sem("f_free")
        f_done = sem("f_done")
        post_step = sem("post_step")
        post_done = sem("post_done")
        relu_done = sem("relu_done")
        sqr_done = sem("sqr_done")
        h2_hi_done = sem("h2_hi_done")
        h2_lo_done = sem("h2_lo_done")
        f2_copied = sem("f2_copied")
        rope_step = sem("rope_step")
        orstd_done = sem("orstd_done")
        o_scaled = sem("o_scaled")

        norms = ["ctx", "mix0", "ffn0", "mix1", "ffn1", "final", "pre2", "post2", "ffn2", "last"]
        split = [q for q in norms if q not in ("final", "post2", "last")]

        def nth(name):
            return norms.index(name)

        def nth_split(name):
            return split.index(name)

        slot = lambda n: n % 2
        bank = lambda b: PS[:, b, :]
        BANK_V = (5, 6, 7, 0, 1, 2)
        BANK_S = (3, 4, 5, 6, 7, 0)
        BANK_G = (1, 2, 3, 4)
        BANK_O = (5, 6, 7, 0)

        mod_at = lambda layer, part: (layer * 6 + part) * KT

        cc = lambda name, n=P: con[:, CON[name]:CON[name] + n]
        ccol = lambda name, lo=0, hi=P: con[lo:hi, CON[name]:CON[name] + 1]
        GCOL, BETA, BK, RK, RQ, EG, KBS, GL, KD, KDS, EGL, TMP = range(12)
        col = lambda i, c, h: cols[:, i, c, h:h + 1]
        hb = lambda ap: ap.rearrange("p (h i) -> p h i", h=GH)
        q_at = lambda h, c: qkv[:, h, c * P:(c + 1) * P]
        k_at = lambda h, c: qkv[:, GH + h, c * P:(c + 1) * P]
        v_at = lambda h, c: qkv[:, 2 * GH + h, c * P:(c + 1) * P]
        hs = lambda h: slice(h * P, (h + 1) * P)
        oT = mt
        gstd = kbg

        block = ctx.enter_context(nc.Block())

        @block.sync
        def _(sp):
            def load(n, j):
                sp.dma_start(raw[:, j, :], slabs[bass.ds(n, 1)].rearrange("o p n -> p (o n)")).then_inc(slab_landed[j], 16)

            for j in range(2):
                load(j, j)
            with sp.Fori(0, n_slabs // 2 - 1) as i:
                for j in range(2):
                    sp.wait_ge(w_lo_done, i * 2 + (j + 1))
                    load(i * 2 + (2 + j), j)
            if n_slabs % 2:
                sp.wait_ge(w_lo_done, n_slabs - 2)
                load(n_slabs - 1, (n_slabs - 1) % 2)
            sp.wait_ge(x_final, KT)
            sp.dma_start(out, x[:, :, :]).then_inc(out_stored, 16)
            sp.wait_ge(out_stored, 16)

        @block.gpsimd
        def _(pool):
            def load(n, j):
                pool.dma_start(ada_raw[:, j, :], ada[bass.ds(n, 1)].rearrange("o p n -> p (o n)")).then_inc(ada_landed[j], 16)

            for j in range(2):
                load(j, j)
            n_ada = 24 if UPTO == "ret" else N_ADA
            with pool.Fori(0, n_ada // 2 - 1) as i:
                for j in range(2):
                    pool.wait_ge(ada_used, i * 2 + (j + 1))
                    load(i * 2 + (2 + j), j)

        @block.tensor
        def _(pe):
            def product(o, w, a, first, last):
                pe.matmul(o, w[0], a[0], start=first, stop=False)
                pe.matmul(o, w[0], a[1], start=False, stop=False)
                return pe.matmul(o, w[1], a[0], start=False, stop=last)

            def wcols(n, a, b):
                return w_hi[:, slot(n), a:b], w_lo[:, slot(n), a:b]

            def out_tile(n, m, o, moving, kts=KT):
                for k in range(kts):
                    mm = product(o, wcols(n, k * 256 + m * P, k * 256 + (m + 1) * P), moving(k), k == 0, k == kts - 1)
                return mm

            def norm_sum(q, tiles, width, b=7):
                for k in range(tiles):
                    pe.wait_ge(sq_ready, 8 * q + k + 1)
                    pe.matmul(PS[:, b, 0:width], ones[:, :], sq[:, k % 2, 0:width], start=(k == 0),
                              stop=(k == tiles - 1)).then_inc(sq_used, 1)

            def unit_sum(count):
                pe.wait_ge(acc_ready, count)
                for m in range(KT):
                    mm = pe.matmul(PS[:, 2, m:m + 1], acc[:, m * P:(m + 1) * P], ones[:, 0:1], start=True, stop=True)
                mm.then_inc(unit_summed, 1)

            act = lambda k: (act_hi[:, k, :], act_lo[:, k, :])
            acx = lambda k: (ctx_hi[:, k, :], ctx_lo[:, k, :])

            pe.wait_ge(silu_c_done, 2)
            pe.wait_ge(consts_set, 2)
            for a in range(8):
                pe.wait_ge(ada_landed[a % 2], 16 * (a // 2 + 1))
                for kk in range(2):
                    k = 2 * (a % 4) + kk
                    for m in range(KT):
                        col = 2 * (a // 4 * KT + m)
                        mm = pe.matmul(PS[:, 0, col:col + 2], ada_raw[:, a % 2, kk * D + m * P:kk * D + (m + 1) * P],
                                       silu_c[:, k, :], start=(a == 0 and kk == 0 and m == 0), stop=(k == KT - 1),
                                       skip_group_check=True)
                mm.then_inc(ada_used, 1)
            norm_sum(nth("ctx"), KT, C)
            pe.wait_ge(std_ready, 1)
            norm_sum(nth("mix0"), KT, T)

            pe.wait_ge(lo_ready, 8 * 2)
            with pe.Fori(0, RH) as h:
                n0 = h * 8
                pe.wait_ge(w_lo_done, n0 + 1)
                for m in range(RDT):
                    pe.wait_ge(banks_free, n0 + (m + 1))
                    mm = out_tile(0, m, bank(m), act)
                mm.then_inc(slab_done, 1)
                pe.wait_ge(w_lo_done, n0 + 2)
                for m in range(RDT):
                    pe.wait_ge(banks_free, n0 + (m + 3))
                    out_tile(1, m, bank(2 + m), act)
                pe.wait_ge(banks_free, n0 + 5)
                for m in range(RDT):
                    mm = out_tile(1, m, PS[:, 4, m * C:(m + 1) * C], acx)
                mm.then_inc(slab_done, 1)
                for j in range(2):
                    pe.wait_ge(w_lo_done, n0 + (3 + j))
                    for t in range(KEYT):
                        if j == 0 and t < 3:
                            pe.wait_ge(banks_free, n0 + (t + 6))
                        elif j == 0:
                            pe.wait_ge(rope_read, h * 4 + (t - 2))
                        for kk in range(4):
                            k = 4 * j + kk
                            if t < TT:
                                st = act_hi[:, k, t * P:(t + 1) * P], act_lo[:, k, t * P:(t + 1) * P]
                            else:
                                st = ctx_hi[:, k, (t - TT) * P:(t - TT + 1) * P], ctx_lo[:, k, (t - TT) * P:(t - TT + 1) * P]
                            mm = product(bank(BANK_V[t]), st, wcols(j, kk * RV, (kk + 1) * RV), k == 0, k == KT - 1)
                    mm.then_inc(slab_done, 1)
                pe.wait_ge(roped, h * 4 + 5)
                pe.wait_ge(kctx_done, h + 1)
                for t in range(KEYT):
                    if t >= 2:
                        pe.wait_ge(v_done, h * 6 + (t - 1))
                    for d in range(RDT):
                        mm = pe.matmul(bank(BANK_S[t]), rk[:, d, t * P:(t + 1) * P], rq[:, d, :],
                                       start=(d == 0), stop=(d == RDT - 1))
                    mm.then_inc(s_ready, 1)
                for j in range(2):
                    pe.wait_ge(w_lo_done, n0 + (5 + j))
                    for m in range(2):
                        if j == 0:
                            pe.wait_ge(v_done, h * 6 + (5 + m))
                        else:
                            pe.wait_ge(s_decayed, h * 6 + (1 + m))
                        mm = out_tile(j, m, bank(BANK_G[2 * j + m]), act)
                    mm.then_inc(slab_done, 1)
                pe.wait_ge(s_decayed, h * 6 + 6)
                for e in range(RVT):
                    for t in range(KEYT):
                        mm = pe.matmul(bank(BANK_O[e]), rv[:, t, e * P:(e + 1) * P], rs[:, t, :],
                                       start=(t == 0), stop=(t == KEYT - 1))
                    mm.then_inc(pv_ready, 1)
                pe.wait_ge(g_done, h * 4 + 4)
                unit_sum(h + 1)
                for e in range(RVT):
                    pe.wait_ge(osq_ready, h * 4 + (e + 1))
                    mm = pe.matmul(bank(1), ones[:, :], rs[:, e, :], start=(e == 0), stop=(e == RVT - 1))
                mm.then_inc(osum_ready, 1)
                pe.wait_ge(ry_lo_done, h * 4 + 4)
                pe.wait_ge(unit_done, h + 1)
                for j in range(2):
                    pe.wait_ge(w_lo_done, n0 + (7 + j))
                    for kk in range(2):
                        e = 2 * j + kk
                        for m in range(KT):
                            mm = product(bank(m), wcols(j, kk * D + m * P, kk * D + (m + 1) * P),
                                         (ry_hi[:, e, :], ry_lo[:, e, :]), e == 0, e == RVT - 1)
                    mm.then_inc(slab_done, 1)

            def up(n, tiles, seen, units=0):
                with pe.Fori(0, tiles // 2) as i:
                    for j in range(2):
                        pe.wait_ge(w_lo_done, i * 2 + (n + j + 1))
                        for m in range(2):
                            if j == 0:
                                pe.wait_ge(act_silu, i * 2 + (seen + m + 1))
                            else:
                                pe.wait_ge(hraw_ready, i * 2 + (seen + m + 1))
                            mm = out_tile(n + j, m, bank(2 * j + m), act)
                        mm.then_inc(slab_done, 1)
                    if units:
                        pe.wait_ge(acc_ready, i + (units + 1))
                        for m in range(KT):
                            mm = pe.matmul(PS[:, 4, m:m + 1], acc[:, m * P:(m + 1) * P], ones[:, 0:1],
                                           start=True, stop=True)
                        mm.then_inc(unit_summed, 1)

            def down(n, tiles, h_hi, h_lo):
                def turn(i, first, last, slabs_here=2):
                    for j in range(slabs_here):
                        pe.wait_ge(w_lo_done, i * 2 + (n + j + 1))
                        for kk in range(2):
                            t = i * 4 + (2 * j + kk)
                            hi = h_hi[:, bass.ds(t, 1), :].rearrange("p o t -> p (o t)")
                            lo = h_lo[:, bass.ds(t, 1), :].rearrange("p o t -> p (o t)")
                            for b in (4, 5, 6, 7, 0, 1, 2, 3):
                                mm = product(bank(b), wcols(n + j, kk * D + b * P, kk * D + (b + 1) * P), (hi, lo),
                                             first and j == 0 and kk == 0,
                                             last and j == slabs_here - 1 and kk == 1)
                        mm.then_inc(slab_done, 1)

                full, rest = divmod(tiles // 2, 2)
                turn(0, True, False)
                if full > 2 or (full > 1 and rest):
                    with pe.Fori(1, full if rest else full - 1) as i:
                        turn(i, False, False)
                turn(full if rest else full - 1, False, True, 1 if rest else 2)

            def swiglu(n, seen, added, units):
                for c, tiles in enumerate(FCH):
                    if c:
                        pe.wait_ge(down_added, added + 8)
                    up(n, tiles, seen, units if c == 0 else 0)
                    n += tiles
                    seen += tiles
                    if c == 0 and units:
                        pe.wait_ge(unit_done, 10)
                    pe.wait_ge(hid_lo_done, seen + 2)
                    down(n, tiles, hid_hi, hid_lo)
                    n += tiles // 2

            def norm(name):
                norm_sum(nth(name), KT, T)
                if name in split:
                    pe.wait_ge(lo_ready, 8 * (nth_split(name) + 1))
                else:
                    pe.wait_ge(std_ready, nth(name) + 1)

            hid = lambda t: (hid_hi[:, t, :], hid_lo[:, t, :])

            def two_turns(n, moving, free):
                with pe.Fori(0, 2) as i:
                    for j in range(2):
                        pe.wait_ge(w_lo_done, i * 2 + (n + j + 1))
                        for m in range(2):
                            pe.wait_ge(free, i * 4 + (2 * j + m + 1))
                            mm = out_tile(n + j, m, bank(2 * j + m), moving)
                        mm.then_inc(slab_done, 1)

            if has("ffn0"):
                pe.wait_ge(banks_free, 8 * (RH + 1))
                norm("ffn0")
                swiglu(FFN0, 0, 0, RH)
            if has("conv"):
                norm("mix1")
                up(CONV, KT, FT)
                pe.wait_ge(hraw_ready, 2 + FT + KT)
                two_turns(CONV + 8, act, conv_y)
                pe.wait_ge(hid_lo_done, FT + KT + 2)
                two_turns(CONV + 12, hid, wout_added)
            if has("ffn1"):
                norm("ffn1")
                swiglu(FFN1, FT + KT, 16, 0)

            if has("mix"):
                norm("final")
                norm("pre2")
                n = MIX
                with pe.Fori(0, 3) as i:
                    for j in range(2):
                        pe.wait_ge(w_lo_done, i * 2 + (n + j + 1))
                        for m in range(2):
                            pe.wait_ge(cvin_done, i * 4 + (2 * j + m + 1))
                            mm = out_tile(n + j, m, bank(2 * j + m), act)
                        mm.then_inc(slab_done, 1)
                for j in range(2):
                    pe.wait_ge(w_lo_done, n + 7 + j)
                    for m in range(2):
                        pe.wait_ge(cvin_done, 12 + 2 * j + m + 1)
                        mm = out_tile(n + 6 + j, m, bank(2 * j + m), act)
                    mm.then_inc(slab_done, 1)
                pe.wait_ge(w_lo_done, n + 9)
                for m in range(2):
                    mm = out_tile(n + 8, m, bank(4 + m), act)
                mm.then_inc(slab_done, 1)
                pe.wait_ge(w_lo_done, n + 10)
                for m in range(2):
                    out_tile(n + 9, m, bank(6 + m), act)
                pe.wait_ge(gate2_done, 1)
                for t in range(TT):
                    for k in range(KT):
                        mm = product(PS[:, 0, t * 8:t * 8 + 8], (act_hi[:, k, t * P:(t + 1) * P], act_lo[:, k, t * P:(t + 1) * P]),
                                     wcols(n + 9, k * 256 + P, k * 256 + P + 8), k == 0, k == KT - 1)
                mm.then_inc(slab_done, 1)
                pe.wait_ge(gate2_done, 2)
                for t in range(2 * GH):
                    pe.wait_ge(qsq_ready, t + 1)
                    for c in range(TT):
                        at = c * 2 * GH + t
                        mm = pe.matmul(PS[:, 1, at:at + 1], sq[:, t % 2, c * P:(c + 1) * P], ones[:, 0:1], start=True, stop=True)
                    mm.then_inc(qsq_used, 1)
                pe.wait_ge(cols_done, 1)
                pe.wait_ge(ssd_done, 1)
                for c in range(TT):
                    mm = pe.matmul(PS[:, 1, 64 + c * GH:64 + (c + 1) * GH], cc("upper"), rowsrc[:, c, 0:GH], start=True, stop=True)
                mm.then_inc(gcum_ready, 1)
                for k in range(3):
                    pe.wait_ge(msq_ready, k + 1)
                    if k == 0:
                        pe.wait_ge(gate2_done, 4)
                    mm = pe.matmul(bank(2 if k < 2 else 3), ones[:, :], sq[:, k, :] if k < 2 else rstd[:, :],
                                   start=(k != 1), stop=(k != 0))
                    if k:
                        mm.then_inc(msum_ready, 1)
                pe.wait_ge(mc_lo_done, 3)
                mc = lambda k: (mc_hi[:, k, :], mc_lo[:, k, :])
                pe.wait_ge(w_lo_done, n + 12)
                pe.wait_ge(cols_done, 2)
                BANK_MV = (3, 4, 5, 6)
                for t in range(TT):
                    mm = product(bank(BANK_MV[t]), (mc_hi[:, 2, t * P:(t + 1) * P], mc_lo[:, 2, t * P:(t + 1) * P]),
                                 wcols(n + 11, MH * NOPE, MH * (NOPE + MV)), True, True)
                    mm.then_inc(mv_ready, 1)

                def project(h):
                    if h == 0:
                        pe.wait_ge(ab_done, 1)
                    else:
                        pe.wait_ge(qn_done, h)
                        pe.wait_ge(qr_done, h)
                    if h % 2 == 0:
                        if h:
                            pe.wait_ge(kn_done, h)
                        product(bank(1), wcols(n + 11, h * NOPE, (h + 2) * NOPE), mc(2), True, True)
                    for k in range(2):
                        mm = product(bank(0), wcols(n + 10, k * D + h * P, k * D + (h + 1) * P), mc(k), k == 0, k == 1)
                    mm.then_inc(q_ready, 1)

                def attend(h):
                    pe.wait_ge(qn_done, h + 1)
                    pe.wait_ge(qr_done, h + 1)
                    pe.wait_ge(kn_done, h + 1)
                    if h == 0:
                        pe.wait_ge(kr_copied, 2)
                        pe.wait_ge(mstd_done, 2)
                        pe.wait_ge(mv_done, 4)
                    for t in range(TT):
                        if h:
                            pe.wait_ge(exp_done, 4 * (h - 1) + t + 1)
                        w = (t + 1) * P
                        pe.matmul(PS[:, 2 + t, 0:w], qh[0:QK, h % 2, t * P:w], kh[0:QK, h % 2, 0:w], start=True, stop=False,
                                  skip_group_check=True)
                        pe.matmul(PS[:, 2 + t, t * P:w], cc("mask_q"), cc("mask_k"), start=False, stop=True,
                                  skip_group_check=True).then_inc(ms_ready, 1)

                project(0)
                attend(0)
                for h in range(MH):
                    if h + 1 < MH:
                        project(h + 1)
                    for t in range(TT):
                        pe.wait_ge(p_ready, 4 * h + t + 1)
                        if h or t:
                            pe.wait_ge(prt_done, 4 * h + t)
                        for kt in range(t + 1):
                            mm = pe.transpose(PS[:, 6, kt * P:(kt + 1) * P], pr[:, t % 2, kt * P:(kt + 1) * P], cc("ident"))
                        mm.then_inc(t_ready, 1)
                    if h + 1 < MH:
                        attend(h + 1)
                    pe.wait_ge(prt_done, 4 * h + 4)
                    if h == 0:
                        pe.wait_ge(krope_done, 1)
                    elif h % 2 == 0:
                        pe.wait_ge(mo_lo_done, h // 2)
                    r0 = MV * (h % 2)
                    for kt in range(TT):
                        mm = pe.matmul(PS[r0:r0 + MV, 7, kt * P:T], mv[:, kt, h * MV:(h + 1) * MV], prt[:, kt, kt * P:T],
                                       start=(kt == 0), stop=(kt == TT - 1), skip_group_check=True)
                    mm.then_inc(o2_ready, 1)
                pe.sem_inc(slab_done, 2)

                for c in range(TT):
                    pe.wait_ge(bcs_done, c + 1)
                    if c == 0:
                        pe.wait_ge(mo_lo_done, 4)
                        pe.wait_ge(prt_done, 4 * MH)
                        pe.wait_ge(exp_done, 4 * MH)
                    else:
                        pe.wait_ge(qdec_done, c)
                        pe.wait_ge(e_done, c)
                        pe.wait_ge(kvt_done, 3 * GH * c)
                    for h in range(GH):
                        pe.matmul(PS[:, 0, hs(h)], bcs[:, h, :], cc("upper"), start=True, stop=True)
                        pe.matmul(PS[:, 1, hs(h)], bcs[:, GH + h, :], cc("ident"), start=True, stop=True)
                        mm = pe.matmul(PS[:, 2, hs(h)], bcs[:, 2 * GH + h, :], cc("ident"), start=True, stop=True)
                    mm.then_inc(rows_ready, 1)
                    for h in range(GH):
                        pe.matmul(PS[:, 3, hs(h)], k_at(h, c), k_at(h, c), start=True, stop=True)
                        pe.matmul(PS[:, 4, hs(h)], k_at(h, c), q_at(h, c), start=True, stop=True)
                        pe.transpose(PS[:, 5, hs(h)], k_at(h, c), cc("ident"))
                        mm = pe.transpose(PS[:, 6, hs(h)], v_at(h, c), cc("ident"))
                    mm.then_inc(kq_ready, 1)
                for c in range(TT):
                    pe.wait_ge(y0_done, c + 1)
                    if c == 0:
                        pe.wait_ge(kvt_done, 3 * GH * TT)
                    if c >= 2:
                        pe.wait_ge(x0_done, c - 1)
                    for h in range(GH):
                        mm = pe.transpose(PS[:, 6 + c % 2, hs(h)], gy[:, c, hs(h)], cc("ident"))
                    mm.then_inc(x0_ready, 1)

                def level_first(g):
                    c = g % TT
                    pe.wait_ge(lv_done, g + 1)
                    if g < TT:
                        pe.wait_ge(x0_done, c + 1)
                    else:
                        pe.wait_ge(xy_done, 2 * (g - TT + 1))
                    if g >= 2:
                        pe.wait_ge(lp_done, g - 1)
                    for h in range(GH):
                        mm = pe.matmul(PS[:, g % 2, hs(h)], lv[:, g % 2, hs(h)], gx[:, c, hs(h)], start=True, stop=True)
                    mm.then_inc(lp_ready, 1)

                def level_second(g):
                    c = g % TT
                    pe.wait_ge(lp_done, g + 1)
                    if g >= 2:
                        pe.wait_ge(xy_done, 2 * (g - 1))
                    for h in range(GH):
                        pe.matmul(PS[:, 2 + g % 2, hs(h)], gy[:, c, hs(h)], gp[:, c, hs(h)], start=True, stop=True)
                        mm = pe.matmul(PS[:, 4 + g % 2, hs(h)], gp[:, c, hs(h)], gy[:, c, hs(h)], start=True, stop=True)
                    mm.then_inc(xx_ready, 1)

                G = (LEVELS - 1) * TT
                for g in range(G + 1):
                    if g < G:
                        level_first(g)
                    if g:
                        level_second(g - 1)
                for c in range(TT):
                    pe.wait_ge(xy_done, 2 * (G - TT + c + 1))
                    if c == 0:
                        pe.wait_ge(x0_done, TT)
                    else:
                        pe.wait_ge(u_done, c)
                        pe.wait_ge(wt_done, c)
                    for h in range(GH):
                        pe.matmul(PS[:, 6, hs(h)], gy[:, c, hs(h)], v_at(h, c), start=True, stop=True)
                        mm = pe.matmul(PS[:, 7, hs(h)], kbg[:, c, hs(h)], gy[:, c, hs(h)], start=True, stop=True)
                    mm.then_inc(uw_ready, 1)
                for c in range(TT):
                    if c == 0:
                        pe.wait_ge(xy_done, 2 * G)
                    if c:
                        pe.wait_ge(state_done, GH * c)
                        pe.wait_ge(vn_done, c)
                        for h in range(GH):
                            mm = pe.matmul(PS[:, 0, hs(h)], gp[:, c, hs(h)], state[:, h, :], start=True, stop=True)
                        mm.then_inc(ws_ready, 1)
                        pe.wait_ge(o3_done, c)
                    pe.wait_ge(vn_done, c + 1)
                    if c + 1 < TT:
                        for h in range(GH):
                            mm = pe.matmul(PS[:, 2, hs(h)], k_at(h, c), gx[:, c, hs(h)], start=True, stop=True)
                        mm.then_inc(sup_ready, 1)
                    for h in range(GH):
                        if c:
                            pe.matmul(PS[:, 1, hs(h)], state[:, h, :], q_at(h, c), start=True, stop=False)
                        mm = pe.matmul(PS[:, 1, hs(h)], gx[:, c, hs(h)], ptm[:, c, hs(h)], start=(c == 0), stop=True)
                    mm.then_inc(o3_ready, 1)
                for h in range(GH):
                    pe.wait_ge(gsq_ready, h + 1)
                    pe.matmul(bank(3 + h), ones[:, :], sq[:, h % 2, :], start=True, stop=True).then_inc(gss_ready, 1)
                pe.wait_ge(go_lo_done, GH)
                pe.wait_ge(mo_lo_done, 4)
                two_turns(n + 12, act, f_free)
                norm("post2")

            if has("all"):
                norm("ffn2")
                n = FFN2
                seen = 0
                for c, tiles in enumerate(F2CH):
                    if c:
                        pe.wait_ge(f2_copied, KT)
                    with pe.Fori(0, tiles // 4) as i:
                        for j in range(2):
                            pe.wait_ge(w_lo_done, i * 2 + (n + j + 1))
                            for m in range(2):
                                pe.wait_ge(relu_done, i * 4 + (seen + 2 * j + m + 1))
                                mm = out_tile(n + j, m, bank(2 * j + m), act)
                            mm.then_inc(slab_done, 1)
                    n += tiles // 2
                    seen += tiles
                    pe.wait_ge(h2_lo_done, seen + 2)
                    down(n, tiles, hid2_hi, hid2_lo)
                    n += tiles // 2
                norm("last")

        @block.scalar
        def _(act):
            act.dma_start(vec[:, :], vecs).then_inc(vec_landed, 16)
            act.dma_start(xc, ctx_in).then_inc(xc_landed, 16)
            act.dma_start(x[:, :, :], x_in).then_inc(x_landed, 16)
            act.dma_start(rope[:, :], rope1).then_inc(rope_landed, 16)
            act.dma_start(toep[:, :], decay[0]).then_inc(toep_landed, 16)

            def round_slab(n, i=0, step=2):
                act.wait_ge(slab_landed[n % 2], i * (step * 8) + 16 * (n // 2 + 1))
                act.activation(w_hi[:, n % 2, :], raw[:, n % 2, :], ACT.Copy).then_inc(w_hi_done, 1)

            def after(n, i=0, step=2):
                act.wait_ge(slab_done, i * step + (n + 1))
                round_slab(n + 2, i, step)

            def squares(q, src, tiles, width):
                for k in range(tiles):
                    if 8 * q + k >= 2:
                        act.wait_ge(sq_used, 8 * q + k - 1)
                    act.activation(sq[:, k % 2, 0:width], src(k), ACT.Square).then_inc(sq_ready, 1)

            def root(q, width, features):
                act.wait_ge(sq_used, 8 * q + 8)
                act.activation(std[:, 0:width], PS[:, 7, 0:width], ACT.Sqrt, bias=eps[:, 0:1],
                               scale=1.0 / features).then_inc(std_ready, 1)

            def shifted(q, shift, dst, width):
                for k in range(KT):
                    act.wait_ge(y_ready, 8 * q + k + 1)
                    act.activation(dst(k), normed[:, k % 2, 0:width], ACT.Identity, bias=shift(k)).then_inc(hi_ready, 1)

            act.sem_inc(act_silu, 2)
            act.sem_inc(hid_hi_done, 2)
            act.wait_ge(vec_landed, 16)
            for j, name in enumerate(("c", "c_ctx")):
                act.activation(silu_c[:, :, j], vec[:, VEC[name]:VEC[name] + KT], ACT.Silu).then_inc(silu_c_done, 1)
            round_slab(0)
            round_slab(1)
            act.wait_ge(xc_landed, 16)
            act.wait_ge(consts_set, 2)
            squares(0, lambda k: xc[:, k, :], KT, C)
            root(0, C, D)
            act.wait_ge(x_landed, 16)
            squares(1, lambda k: x[:, k, :], KT, T)
            act.wait_ge(gain_done, 3)
            shifted(0, lambda k: mod_ctx[:, k:k + 1], lambda k: ctx_hi[:, k, :], C)
            root(1, T, D)
            shifted(1, lambda k: mod[:, k:k + 1], lambda k: act_hi[:, k, :], T)

            with act.Fori(0, RH) as h:
                after(0, h, 8)
                after(1, h, 8)
                act.activation(rk[:, :, T:T + C], PS[:, 4, :].rearrange("p (m t) -> p m t", m=RDT),
                               ACT.Copy).then_inc(kctx_done, 1)
                after(2, h, 8)
                after(3, h, 8)
                for t in range(KEYT):
                    act.activation(rv[:, t, :], bank(BANK_V[t]), ACT.Copy).then_inc(v_done, 1)
                for j in range(2):
                    after(4 + j, h, 8)
                    for m in range(2):
                        act.activation(rg[:, 2 * j + m, :], bank(BANK_G[2 * j + m]), ACT.Silu).then_inc(g_done, 1)
                act.wait_ge(s_decayed, h * 6 + 6)
                act.dma_start(toep[:, :], decay[bass.ds(h + 1, 1)].rearrange("o p n -> p (o n)")).then_inc(toep_landed, 16)
                act.wait_ge(pv_ready, h * 4 + 4)
                for e in range(RVT):
                    act.activation(rs[:, e, :], bank(BANK_O[e]), ACT.Square).then_inc(osq_ready, 1)
                act.wait_ge(osum_ready, h + 1)
                act.activation(std[:, :], bank(1), ACT.Sqrt, bias=eps[:, 0:1], scale=1.0 / RV).then_inc(ostd_ready, 1)
                for e in range(RVT):
                    act.wait_ge(ry_ready, h * 4 + (e + 1))
                    act.activation(ry_hi[:, e, :], rs[:, e, :], ACT.Copy).then_inc(ry_hi_done, 1)
                after(6, h, 8)
                after(7, h, 8)

            act.wait_ge(toep_landed, 16 * (RH + 1))

            def after_static(n):
                act.wait_ge(slab_done, n + 1)
                if n + 2 < n_slabs:
                    round_slab(n + 2)

            def up(n, tiles, seen, func=ACT.Silu):
                with act.Fori(0, tiles // 2) as i:
                    after(n, i)
                    for m in range(2):
                        act.wait_ge(hraw_ready, i * 2 + (seen + m + 1))
                        act.activation(sg[:, m, :], bank(m), func).then_inc(act_silu, 1)
                    after(n + 1, i)
                    for m in range(0 if func == ACT.Copy else 2):
                        act.wait_ge(hraw_ready, i * 2 + (seen + m + 3))
                        act.activation(hid_hi[:, bass.ds(i * 2 + m, 1), :].rearrange("p o t -> p (o t)"),
                                       hraw[:, m, :], ACT.Copy).then_inc(hid_hi_done, 1)

            def down(n, tiles):
                full, rest = divmod(tiles // 2, 2)
                if full > 1:
                    with act.Fori(0, full - 1) as i:
                        after(n, i)
                        after(n + 1, i)
                for j in range(2 + rest):
                    after_static(n + 2 * full - 2 + j)

            def swiglu(n, seen):
                for tiles in FCH:
                    up(n, tiles, seen)
                    n += tiles
                    seen += tiles
                    down(n, tiles)
                    n += tiles // 2

            def norm(name, shift):
                q = nth(name)
                squares(q, lambda k: x[:, k, :], KT, T)
                root(q, T, D)
                if shift is not None:
                    shifted(nth_split(name), lambda k: mod[:, shift + k:shift + k + 1], lambda k: act_hi[:, k, :], T)

            if has("ffn0"):
                act.wait_ge(banks_free, 8 * (RH + 1))
                norm("ffn0", mod_at(0, 3))
                swiglu(FFN0, 0)
            if has("conv"):
                act.wait_ge(down_added, 16)
                norm("mix1", mod_at(1, 0))
                up(CONV, KT, FT, ACT.Copy)
                with act.Fori(0, 2) as i:
                    for j in range(2):
                        after(CONV + 8 + j, i)
                        for m in range(2):
                            act.wait_ge(conv_y, i * 4 + (2 * j + m + 5))
                            act.activation(hid_hi[:, bass.ds(i * 4 + (2 * j + m), 1), :].rearrange("p o t -> p (o t)"),
                                           hraw[:, m, :], ACT.Copy).then_inc(hid_hi_done, 1)
                for n in range(CONV + 12, CONV + 16):
                    after_static(n)
            if has("ffn1"):
                act.wait_ge(wout_added, 12)
                norm("ffn1", mod_at(1, 3))
                swiglu(FFN1, FT + KT)

            def norm2(name, src, dst):
                squares(nth(name), src, KT, T)
                root(nth(name), T, D)
                if dst is not None:
                    q = nth_split(name)
                    for k in range(KT):
                        act.wait_ge(y_ready, 8 * q + k + 1)
                        act.activation(dst(k), normed[:, k % 2, :], ACT.Copy).then_inc(hi_ready, 1)

            x_tile = lambda k: x[:, k, :]
            if has("mix"):
                act.wait_ge(down_added, 32)
                act.dma_start(con[:, :], consts).then_inc(con_landed, 16)
                act.dma_start(heads_c[:, :], per_head).then_inc(heads_landed, 16)
                act.dma_start(pos_i, positions).then_inc(pos_landed, 16)
                norm2("final", x_tile, None)
                act.wait_ge(final_done, KT)
                norm2("pre2", x_tile, lambda k: act_hi[:, k, :])
                act.wait_ge(trig_ready, 1)
                act.activation(csn[64:128, :], cv[64:128, 3, :], ACT.Sin).then_inc(trig_done, 1)
                n = MIX
                with act.Fori(0, 3) as i:
                    for j in range(2):
                        after(n + j, i)
                        for m in range(2):
                            c = 2 * j + m
                            act.wait_ge(conv2_done, i * 4 + (c + 1))
                            act.activation(cvin[:, c, 3:T + 3], bank(c), ACT.Copy).then_inc(cvin_done, 1)
                    for c in range(4):
                        act.wait_ge(conv2_done, i * 4 + (c + 5))
                        act.activation(qkv[:, bass.ds(i * 4 + c, 1), :].rearrange("p o t -> p (o t)"), cv[:, c, :],
                                       ACT.Silu).then_inc(silu2_done, 1)
                for j in range(2):
                    after_static(n + 6 + j)
                    for m in range(2):
                        act.activation(gate[:, 2 * j + m, :], bank(2 * j + m), ACT.Silu).then_inc(gate2_done, 1)
                after_static(n + 8)
                for m in range(2):
                    act.activation(cqr[:, m, :], bank(4 + m), ACT.Copy).then_inc(cqr_done, 1)
                after_static(n + 9)
                act.activation(cqr[:, 2, :], bank(6), ACT.Copy).then_inc(cqr_done, 1)
                act.wait_ge(silu2_done, NCONV + 4)
                for t in range(2 * GH):
                    if t >= 2:
                        act.wait_ge(qsq_used, t - 1)
                    act.activation(sq[:, t % 2, :], qkv[:, t, :], ACT.Square).then_inc(qsq_ready, 1)
                act.wait_ge(soft1, 1)
                act.activation(cols[:, TMP, :, :], cols[:, TMP, :, :], ACT.Exp).then_inc(soft2, 1)
                act.wait_ge(soft2, 1)
                act.activation(cols[:, EG, :, :], cols[:, TMP, :, :], ACT.Ln, bias=1.0).then_inc(soft2, 1)
                act.wait_ge(heads_landed, 16)
                act.activation(small[:, 0, :], heads_c[:, 0:GH], ACT.Exp).then_inc(soft2, 1)
                act.activation(cols[:, BETA, :, :], ab[:, :, GH:2 * GH], ACT.Exp, scale=-1.0).then_inc(beta1, 1)
                act.wait_ge(qsq_used, 2 * GH)
                act.activation(ssqk[:, :, :], PS[:, 1, 0:TT * 2 * GH].rearrange("p (c t) -> p c t", c=TT), ACT.Sqrt,
                               bias=eps[:, 0:1]).then_inc(ssd_done, 1)
                act.wait_ge(cqr_done, 3)
                for k in range(3):
                    act.activation(sq[:, k, :] if k < 2 else rstd[:, :], cqr[:, k, :], ACT.Square).then_inc(msq_ready, 1)
                for k in range(2):
                    act.wait_ge(msum_ready, k + 1)
                    act.activation(mstd[:, k, :], bank(2 + k), ACT.Sqrt, bias=eps[:, 0:1],
                                   scale=1.0 / (2 * P if k == 0 else P)).then_inc(mstd_done, 1)
                for k in range(3):
                    act.wait_ge(mc_ready, k + 1)
                    act.activation(mc_hi[:, k, :], cqr[:, k, :], ACT.Copy).then_inc(mc_hi_done, 1)
                act.wait_ge(cols_done, 2)
                act.activation(cols[:, EG, :, :], cols[:, GCOL, :, :], ACT.Exp).then_inc(soft2, 1)
                for t in range(TT):
                    act.wait_ge(mv_ready, t + 1)
                    act.activation(mv[:, t, :], bank((3, 4, 5, 6)[t]), ACT.Copy).then_inc(mv_done, 1)
                act.wait_ge(krope_done, 1)
                for b in range(2):
                    act.activation(kh[64:96, b, :], krope[64:96, :], ACT.Copy).then_inc(kr_copied, 1)

                def head_parts(h):
                    act.wait_ge(q_ready, h + 1)
                    if h >= 2:
                        act.wait_ge(ms_ready, 4 * (h - 1))
                    act.activation(qh[0:NOPE, h % 2, :], PS[0:NOPE, 0, :], ACT.Copy).then_inc(qn_done, 1)
                    if h % 2 == 0:
                        if h:
                            act.wait_ge(ms_ready, 4 * h)
                        for b in range(2):
                            act.activation(kh[0:NOPE, b, :], PS[b * NOPE:(b + 1) * NOPE, 1, :], ACT.Copy).then_inc(kn_done, 1)

                def exps(h, t):
                    g = 4 * h + t
                    act.wait_ge(nmx_done, g + 1)
                    if g >= 2:
                        act.wait_ge(t_ready, g - 1)
                    act.activation(pr[:, t % 2, 0:(t + 1) * P], PS[:, 2 + t, 0:(t + 1) * P], ACT.Exp, bias=small[:, 1, t:t + 1],
                                   scale=QK ** -0.5, accum_out=small[:, 2, t:t + 1]).then_inc(exp_done, 1)

                def turned(h, t):
                    act.wait_ge(t_ready, 4 * h + t + 1)
                    if h and t == 0:
                        act.wait_ge(o2_ready, h)
                    act.activation(prt[:, 0:t + 1, t * P:(t + 1) * P],
                                   PS[:, 6, 0:(t + 1) * P].rearrange("p (k q) -> p k q", q=P), ACT.Copy).then_inc(prt_done, 1)

                head_parts(0)
                for h in range(MH):
                    exps(h, 0)
                    if h + 1 < MH:
                        head_parts(h + 1)
                    exps(h, 1)
                    turned(h, 0)
                    exps(h, 2)
                    turned(h, 1)
                    exps(h, 3)
                    turned(h, 2)
                    turned(h, 3)
                    if h % 2:
                        act.wait_ge(o2_ready, h + 1)
                        act.activation(act_hi[:, 4 + h // 2, :], bank(7), ACT.Copy).then_inc(mo_hi_done, 1)
                after_static(n + 10)
                after_static(n + 11)

                for c in range(TT):
                    act.wait_ge(eraw_done, c + 1)
                    act.activation(ex[:, :], ex[:, :], ACT.Exp).then_inc(e_done, 1)
                    if c:
                        act.wait_ge(qdec_done, c)
                    act.activation(egrow[:, :], bank(0), ACT.Exp).then_inc(kd_exp, 1)
                    act.activation(cols[:, KDS, c, :], cols[:, KD, c, :], ACT.Exp).then_inc(kd_exp, 1)
                    act.activation(cols[:, EGL, c, :], cols[:, GL, c, :], ACT.Exp).then_inc(kd_exp, 1)
                    act.wait_ge(kq_ready, c + 1)
                    act.wait_ge(kd_done, c + 1)
                    for h in range(GH):
                        act.activation(kbg[:, c, hs(h)], PS[:, 5, hs(h)], ACT.Copy, scale=col(KBS, c, h)).then_inc(kvt_done, 1)
                        act.activation(k_at(h, c), PS[:, 5, hs(h)], ACT.Copy, scale=col(KDS, c, h)).then_inc(kvt_done, 1)
                        act.activation(v_at(h, c), PS[:, 6, hs(h)], ACT.Copy, scale=col(BETA, c, h)).then_inc(kvt_done, 1)
                for c in range(TT):
                    act.wait_ge(x0_ready, c + 1)
                    act.activation(gx[:, c, :], bank(6 + c % 2), ACT.Copy).then_inc(x0_done, 1)
                for g in range((LEVELS - 1) * TT):
                    act.wait_ge(lp_ready, g + 1)
                    if g >= TT:
                        act.wait_ge(xx_ready, g - TT + 1)
                    act.activation(gp[:, g % TT, :], bank(g % 2), ACT.Copy).then_inc(lp_done, 1)
                for c in range(TT):
                    act.wait_ge(uw_ready, c + 1)
                    act.activation(gx[:, c, :], bank(6), ACT.Copy).then_inc(u_done, 1)
                for c in range(TT):
                    act.wait_ge(o3_ready, c + 1)
                    act.activation(oT[:, :, c * P:(c + 1) * P], hb(bank(1)), ACT.Copy).then_inc(o3_done, 1)
                act.wait_ge(o3_done, TT)
                for h in range(GH):
                    if h >= 2:
                        act.wait_ge(gss_ready, h - 1)
                    act.activation(sq[:, h % 2, :], oT[:, h, :], ACT.Square).then_inc(gsq_ready, 1)
                for h in range(GH):
                    act.wait_ge(gss_ready, h + 1)
                    act.activation(gstd[:, h, :], bank(3 + h), ACT.Sqrt, bias=eps[:, 0:1], scale=1.0 / P).then_inc(gstd_done, 1)
                for h in range(GH):
                    act.wait_ge(go_ready, h + 1)
                    act.activation(act_hi[:, h, :], oT[:, h, :], ACT.Copy).then_inc(go_hi_done, 1)
                act.wait_ge(go_lo_done, GH)
                for j in range(4):
                    after_static(n + 12 + j)
                    for m in range(2):
                        act.activation(facc[:, 2 * j + m, :], bank(2 * (j % 2) + m), ACT.Copy).then_inc(f_free, 1)
                act.wait_ge(f_free, 4 + KT)
                norm2("post2", lambda k: facc[:, k, :], None)

            if has("all"):
                act.wait_ge(post_done, KT)
                norm2("ffn2", x_tile, lambda k: act_hi[:, k, :])
                n, seen = FFN2, 0
                for c, tiles in enumerate(F2CH):
                    with act.Fori(0, tiles // 4) as i:
                        for j in range(2):
                            after(n + j, i)
                            for m in range(2):
                                t = 2 * j + m
                                act.wait_ge(sqr_done, i * 4 + (seen + t + 1))
                                act.activation(sg2[:, m, :], bank(t), ACT.Relu).then_inc(relu_done, 1)
                            for m in range(2):
                                t = 2 * j + m
                                act.wait_ge(sqr_done, i * 4 + (seen + t + 3))
                                act.activation(hid2_hi[:, bass.ds(i * 4 + t, 1), :].rearrange("p o t -> p (o t)"),
                                               hraw2[:, m, :], ACT.Copy).then_inc(h2_hi_done, 1)
                    n += tiles // 2
                    seen += tiles
                    down(n, tiles)
                    n += tiles // 2
                    if c == 0:
                        for b in range(KT):
                            act.activation(facc[:, b, :], bank(b), ACT.Copy).then_inc(f2_copied, 1)
                act.wait_ge(f_done, KT)
                norm2("last", lambda k: facc[:, k, :], None)

        @block.vector
        def _(dve):
            links = [0]

            def link(ins):
                links[0] += 1
                ins.then_inc(vchain, 1)
                dve.wait_ge(vchain, links[0])

            dve.memset(ones[:, :], 1.0).then_inc(consts_set, 1)
            dve.memset(eps[:, :], EPS).then_inc(consts_set, 1)

            def rest_slab(n, k):
                dve.wait_ge(w_hi_done, n + 1)
                dve.tensor_tensor(w_lo[:, k % 2, :], raw[:, k % 2, :], w_hi[:, k % 2, :].bitcast(F32),
                                  ALU.subtract).then_inc(w_lo_done, 1)

            def norm_tail(name, src, g, shift, hi, lo, width):
                dve.wait_ge(std_ready, nth(name) + 1)
                q = nth_split(name)
                link(dve.reciprocal(rstd[:, 0:width], std[:, 0:width]))

                def rest(k):
                    dve.wait_ge(hi_ready, 8 * q + k + 1)
                    dve.scalar_tensor_tensor(out=lo(k), in0=normed[:, k % 2, 0:width], scalar=shift(k),
                                             in1=hi(k).bitcast(F32), op0=ALU.add, op1=ALU.subtract).then_inc(lo_ready, 1)

                for k in range(KT):
                    if 8 * q + k >= 2:
                        dve.wait_ge(lo_ready, 8 * q + k - 1)
                    dve.scalar_tensor_tensor(out=normed[:, k % 2, 0:width], in0=src(k), scalar=g(k),
                                             in1=rstd[:, 0:width], op0=ALU.mult, op1=ALU.mult).then_inc(y_ready, 1)
                    if k:
                        rest(k - 1)
                rest(KT - 1)

            def make_gain(i, norm_col, scale):
                dve.scalar_tensor_tensor(out=gain[:, i, :], in0=scale, scalar=1.0, in1=vec[:, norm_col:norm_col + KT],
                                         op0=ALU.add, op1=ALU.mult).then_inc(gain_done, 1)

            def unit(i, parts=range(4)):
                for a in parts:
                    dve.wait_ge(ada_landed[a % 2], i * 32 + 16 * (4 + a // 2 + 1))
                    for kk in range(2):
                        k = 2 * a + kk
                        w = ada_raw[:, a % 2, kk * D:(kk + 1) * D]
                        if k == 0:
                            ins = dve.tensor_scalar(acc[:, :], w, silu_c[:, 0, 0:1], None, ALU.mult)
                        else:
                            dve.wait_ge(unit_step, i * 9 + k)
                            ins = dve.scalar_tensor_tensor(out=acc[:, :], in0=w, scalar=silu_c[:, k, 0:1],
                                                           in1=acc[:, :], op0=ALU.mult, op1=ALU.add)
                        ins.then_inc(unit_step, 1)
                    dve.wait_ge(unit_step, i * 9 + (2 * a + 2))
                    dve.sem_inc(ada_used, 1)
                if 3 in parts:
                    dve.sem_inc(unit_step, 1)
                    dve.sem_inc(acc_ready, 1)

            def unit_store(i, b, col):
                dve.wait_ge(unit_summed, i + 1)
                dve.tensor_tensor(mod[:, bass.ds(i * KT + col, KT)], PS[:, b, 0:KT], vec[:, bass.ds(i * KT + col, KT)],
                                  ALU.add).then_inc(unit_done, 1)

            dve.sem_inc(hraw_ready, 2)
            dve.sem_inc(hid_lo_done, 2)
            dve.sem_inc(roped, 1)
            rest_slab(0, 0)
            rest_slab(1, 1)
            dve.wait_ge(vec_landed, 16)
            dve.wait_ge(ada_used, 8)
            sums = PS[:, 0, 0:4 * KT].rearrange("p (u two) -> p u two", two=2)
            dve.tensor_tensor(mod[:, 0:2 * KT], sums[:, :, 0], vec[:, 0:2 * KT], ALU.add).then_inc(mod0_summed, 1)
            dve.tensor_tensor(mod_ctx[:, :], sums[:, :, 1], vec[:, 0:2 * KT], ALU.add).then_inc(mod0_summed, 1)
            dve.wait_ge(mod0_summed, 2)
            make_gain(0, VEC["norm_mix"], mod_ctx[:, KT:2 * KT])
            make_gain(1, VEC["norm_mix"], mod[:, KT:2 * KT])
            dve.sem_inc(gain_done, 1)
            dve.wait_ge(gain_done, 3)
            g = lambda i: (lambda k: gain[:, i, k:k + 1])
            norm_tail("ctx", lambda k: xc[:, k, :], g(0), lambda k: mod_ctx[:, k:k + 1],
                      lambda k: ctx_hi[:, k, :], lambda k: ctx_lo[:, k, :], C)
            norm_tail("mix0", lambda k: x[:, k, :], g(1), lambda k: mod[:, k:k + 1],
                      lambda k: act_hi[:, k, :], lambda k: act_lo[:, k, :], T)
            dve.sem_inc(banks_free, 8)

            dve.wait_ge(rope_landed, 16)
            RW = T // GRID_W
            row_cos, row_sin = rope[:, 0:RW], rope[:, RW:2 * RW]
            col_cos, col_sin = rope[:, 2 * RW:2 * RW + GRID_W], rope[:, 2 * RW + GRID_W:2 * RW + 2 * GRID_W]

            def table(tab, m, lo=0, hi=P):
                if m == 0:
                    return tab[lo:hi, :].unsqueeze(2).to_broadcast([hi - lo, RW, GRID_W])
                return tab[lo:hi, :].unsqueeze(1).to_broadcast([hi - lo, RW, GRID_W])

            def rotate(b, m, dst, count):
                grid = lambda ap: ap.rearrange("p (r c) -> p r c", c=GRID_W)
                cos, sin = ((row_cos, row_sin), (col_cos, col_sin))[m]
                dve.wait_ge(roped, count + 1)
                dve.tensor_tensor(grid(normed[:, 0, :]), grid(bank(b)), table(cos, m), ALU.mult).then_inc(rope_step, 1)
                dve.tensor_tensor(grid(normed[0:64, 1, :]), grid(PS[64:128, b, :]), table(sin, m, 64, 128),
                                  ALU.mult).then_inc(rope_step, 1)
                dve.tensor_tensor(grid(normed[64:128, 1, :]), grid(PS[0:64, b, :]), table(sin, m, 0, 64),
                                  ALU.mult).then_inc(rope_read, 1)
                dve.wait_ge(rope_step, count * 2 + 2)
                dve.wait_ge(rope_read, count + 1)
                dve.tensor_tensor(dst, normed[:, 0, :], normed[:, 1, :], ALU.add).then_inc(roped, 1)

            with dve.Fori(0, RH) as h:
                n0 = h * 8
                rest_slab(n0 + 2, 0)
                dve.wait_ge(slab_done, n0 + 1)
                for m in range(RDT):
                    rotate(m, m, rq[:, m, :], h * 4 + m)
                rest_slab(n0 + 3, 1)
                dve.wait_ge(slab_done, n0 + 2)
                for m in range(RDT):
                    rotate(2 + m, m, rk[:, m, 0:T], h * 4 + (2 + m))
                rest_slab(n0 + 4, 0)
                rest_slab(n0 + 5, 1)
                dve.wait_ge(toep_landed, h * 16 + 16)
                for t in range(KEYT):
                    off = (TT - 1 - t) * P if t < TT else TOEP_X + (KEYT - 1 - t) * P
                    dve.wait_ge(s_ready, h * 6 + (t + 1))
                    dve.tensor_tensor(rs[:, t, :], bank(BANK_S[t]), toep[:, off:off + T], ALU.mult).then_inc(s_decayed, 1)
                rest_slab(n0 + 6, 0)
                unit(h)
                rest_slab(n0 + 7, 1)
                unit_store(h, 2, 2 * KT)
                dve.wait_ge(ostd_ready, h + 1)
                dve.reciprocal(rstd[:, :], std[:, :]).then_inc(orstd_done, 1)
                dve.wait_ge(orstd_done, h + 1)
                for e in range(RVT):
                    dve.tensor_tensor(rs[:, e, :], bank(BANK_O[e]), rstd[:, :], ALU.mult).then_inc(o_scaled, 1)
                for e in range(RVT):
                    dve.wait_ge(o_scaled, h * 4 + (e + 1))
                    dve.tensor_tensor(rs[:, e, :], rs[:, e, :], rg[:, e, :], ALU.mult).then_inc(ry_ready, 1)
                for e in range(RVT):
                    dve.wait_ge(ry_hi_done, h * 4 + (e + 1))
                    dve.tensor_tensor(ry_lo[:, e, :], rs[:, e, :], ry_hi[:, e, :].bitcast(F32),
                                      ALU.subtract).then_inc(ry_lo_done, 1)
                rest_slab(n0 + 8, 0)
                rest_slab(n0 + 9, 1)
                dve.wait_ge(slab_done, n0 + 8)
                for m in range(KT):
                    dve.scalar_tensor_tensor(out=x[:, m, :], in0=bank(m), scalar=mod[:, mod_at(0, 2) + m:mod_at(0, 2) + m + 1],
                                             in1=x[:, m, :], op0=ALU.mult, op1=ALU.add).then_inc(banks_free, 1)

            def static_rest(n):
                if n < n_slabs:
                    rest_slab(n, n)

            def up(n, tiles, seen, unit0=None, conv=False):
                with dve.Fori(0, tiles // 2) as i:
                    if unit0 is not None:
                        unit(i + unit0, (0, 1))
                    rest_slab(i * 2 + (n + 2), n)
                    if unit0 is not None:
                        unit(i + unit0, (2, 3))
                    rest_slab(i * 2 + (n + 3), n + 1)
                    dve.wait_ge(slab_done, i * 2 + (n + 2))
                    if conv:
                        for m in range(2):
                            dve.wait_ge(act_silu, i * 2 + (seen + m + 3))
                            dve.tensor_tensor(u[:, bass.ds(i * 2 + m, 1), 1:T + 1].rearrange("p o t -> p (o t)"),
                                              sg[:, m, :], bank(2 + m), ALU.mult).then_inc(hraw_ready, 1)
                    for m in range(0 if conv else 2):
                        dve.wait_ge(act_silu, i * 2 + (seen + m + 3))
                        dve.wait_ge(hid_lo_done, i * 2 + (seen + m + 1))
                        dve.tensor_tensor(hraw[:, m, :], sg[:, m, :], bank(2 + m), ALU.mult).then_inc(hraw_ready, 1)
                    for m in range(0 if conv else 2):
                        dve.wait_ge(hid_hi_done, i * 2 + (seen + m + 3))
                        t = bass.ds(i * 2 + m, 1)
                        dve.tensor_tensor(hid_lo[:, t, :].rearrange("p o t -> p (o t)"), hraw[:, m, :],
                                          hid_hi[:, t, :].rearrange("p o t -> p (o t)").bitcast(F32),
                                          ALU.subtract).then_inc(hid_lo_done, 1)
                    if unit0 is not None:
                            unit_store(i + unit0, 4, 2 * KT)

            def down(n, tiles, layer, last):
                full, rest = divmod(tiles // 2, 2)
                if full > 1:
                    with dve.Fori(0, full - 1) as i:
                        rest_slab(i * 2 + (n + 2), n)
                        rest_slab(i * 2 + (n + 3), n + 1)
                for j in range(2 + rest):
                    static_rest(n + 2 * full + j)
                dve.wait_ge(slab_done, n + tiles // 2)
                for m in range(KT):
                    at = mod_at(layer, 5) + m
                    ins = dve.scalar_tensor_tensor(out=x[:, m, :], in0=bank(m), scalar=mod[:, at:at + 1],
                                                   in1=x[:, m, :], op0=ALU.mult, op1=ALU.add)
                    ins.then_inc(x_final if last else down_added, 1)

            def swiglu(n, seen, layer, last, unit0=None):
                for c, tiles in enumerate(FCH):
                    up(n, tiles, seen, unit0 if c == 0 else None)
                    n += tiles
                    seen += tiles
                    down(n, tiles, layer, last and c == len(FCH) - 1)
                    n += tiles // 2

            def norm(name, gi, norm_col, layer, scale, shift):
                make_gain(gi, norm_col, mod[:, mod_at(layer, scale):mod_at(layer, scale) + KT])
                dve.wait_ge(gain_done, gi + 2)
                at = mod_at(layer, shift)
                norm_tail(name, lambda k: x[:, k, :], g(gi), lambda k: mod[:, at + k:at + k + 1],
                          lambda k: act_hi[:, k, :], lambda k: act_lo[:, k, :], T)

            if has("ffn0"):
                norm("ffn0", 2, VEC["norm_ffn"], 0, 4, 3)
                swiglu(FFN0, 0, 0, UPTO == "ffn0", RH)
            if has("conv"):
                dve.memset(u[:, :, 0], 0.0).then_inc(pads_zero, 1)
                dve.memset(u[:, :, T + 1], 0.0).then_inc(pads_zero, 1)
                norm("mix1", 3, VEC["norm_mix"] + KT, 1, 1, 0)
                up(CONV, KT, FT, None, True)
                dve.wait_ge(hraw_ready, 2 + FT + KT)
                dve.wait_ge(pads_zero, 2)
                dve.sem_inc(conv_y, 4)
                dve.sem_inc(wout_added, 4)
                tap = lambda k, t: vec[:, bass.ds(t + (VEC["conv_w"] + k * KT), 1)]
                with dve.Fori(0, 2) as i:
                    for j in range(2):
                        n = CONV + 8 + j
                        for m in range(2):
                            c = 2 * j + m
                            t = i * 4 + c
                            ut = lambda k: u[:, bass.ds(t, 1), k:k + T].rearrange("p o t -> p (o t)")
                            dve.wait_ge(hid_lo_done, i * 4 + (FT + c + 1))
                            dve.tensor_scalar(hraw[:, m, :], ut(0), tap(0, t), None, ALU.mult).then_inc(conv_step, 1)
                            dve.wait_ge(conv_step, i * 12 + (3 * c + 1))
                            dve.scalar_tensor_tensor(out=hraw[:, m, :], in0=ut(1), scalar=tap(1, t), in1=hraw[:, m, :],
                                                     op0=ALU.mult, op1=ALU.add).then_inc(conv_step, 1)
                            dve.wait_ge(conv_step, i * 12 + (3 * c + 2))
                            dve.scalar_tensor_tensor(out=hraw[:, m, :], in0=ut(2), scalar=tap(2, t), in1=hraw[:, m, :],
                                                     op0=ALU.mult, op1=ALU.add).then_inc(conv_step, 1)
                        rest_slab(i * 2 + (n + 2), n)
                        dve.wait_ge(slab_done, i * 2 + (n + 1))
                        for m in range(2):
                            c = 2 * j + m
                            dve.wait_ge(conv_step, i * 12 + (3 * c + 3))
                            dve.tensor_tensor(hraw[:, m, :], hraw[:, m, :], bank(c), ALU.mult).then_inc(conv_y, 1)
                        for m in range(2):
                            c = 2 * j + m
                            t = bass.ds(i * 4 + c, 1)
                            dve.wait_ge(hid_hi_done, i * 4 + (FT + c + 3))
                            dve.tensor_tensor(hid_lo[:, t, :].rearrange("p o t -> p (o t)"), hraw[:, m, :],
                                              hid_hi[:, t, :].rearrange("p o t -> p (o t)").bitcast(F32),
                                              ALU.subtract).then_inc(hid_lo_done, 1)
                with dve.Fori(0, 2) as i:
                    for j in range(2):
                        n = CONV + 12 + j
                        rest_slab(i * 2 + (n + 2), n)
                        dve.wait_ge(slab_done, i * 2 + (n + 1))
                        for m in range(2):
                            c = 2 * j + m
                            xt = x[:, bass.ds(i * 4 + c, 1), :].rearrange("p o t -> p (o t)")
                            dve.scalar_tensor_tensor(out=xt, in0=bank(c), scalar=mod[:, bass.ds(i * 4 + (mod_at(1, 2) + c), 1)],
                                                     in1=xt, op0=ALU.mult, op1=ALU.add).then_inc(wout_added, 1)
            if has("ffn1"):
                norm("ffn1", 4, VEC["norm_ffn"] + KT, 1, 4, 3)
                swiglu(FFN1, FT + KT, 1, UPTO == "ffn1")
            if UPTO == "conv":
                dve.wait_ge(wout_added, 12)
                dve.sem_inc(x_final, KT)
            def norm_in(name, src, g, dst):
                dve.wait_ge(std_ready, nth(name) + 1)
                link(dve.reciprocal(rstd[:, :], std[:, :]))
                if dst is not None:
                    for k in range(KT):
                        dst(k)
                    return
                q = nth_split(name)

                def rest(k):
                    dve.wait_ge(hi_ready, 8 * q + k + 1)
                    dve.tensor_tensor(act_lo[:, k, :], normed[:, k % 2, :], act_hi[:, k, :].bitcast(F32),
                                      ALU.subtract).then_inc(lo_ready, 1)

                for k in range(KT):
                    dve.wait_ge(lo_ready, 8 * q + k - 1)
                    dve.scalar_tensor_tensor(out=normed[:, k % 2, :], in0=src(k), scalar=g(k), in1=rstd[:, :],
                                             op0=ALU.mult, op1=ALU.mult).then_inc(y_ready, 1)
                    if k:
                        rest(k - 1)
                rest(KT - 1)

            vcol = lambda name: (lambda k: vec[:, VEC[name] + k:VEC[name] + k + 1])
            x_tile = lambda k: x[:, k, :]

            def post(name, gain_name, done):
                g = vcol(gain_name)

                def step(k):
                    if k >= 2:
                        dve.wait_ge(done, k - 1)
                    link(dve.scalar_tensor_tensor(out=normed[:, k % 2, :], in0=facc[:, k, :], scalar=g(k), in1=rstd[:, :],
                                                  op0=ALU.mult, op1=ALU.mult))
                    dve.tensor_tensor(x[:, k, :], x[:, k, :], normed[:, k % 2, :], ALU.add).then_inc(done, 1)

                norm_in(name, None, None, step)

            if has("mix"):
                def final(k):
                    dve.scalar_tensor_tensor(out=x[:, k, :], in0=x[:, k, :], scalar=vcol("final_norm")(k), in1=rstd[:, :],
                                             op0=ALU.mult, op1=ALU.mult).then_inc(final_done, 1)

                norm_in("final", None, None, final)
                dve.wait_ge(final_done, KT)
                norm_in("pre2", x_tile, vcol("mix_pre"), None)
                dve.wait_ge(pos_landed, 16)
                dve.wait_ge(con_landed, 16)
                R = slice(64, 128)
                a0, a1, a2, a3 = (cv[R, k, :] for k in range(4))
                TURN = 2.0 * np.pi
                C1 = 6.28125
                C2 = float(np.float32(np.round((TURN - C1) * 2 ** 20) / 2 ** 20))
                C3 = float(TURN - C1 - C2)
                MAGIC = 1.5 * 2 ** 23
                link(dve.tensor_copy(a1, pos_i[R, :]))
                link(dve.tensor_scalar(a1, a1, ccol("freq", 64, 128), None, ALU.mult))
                link(dve.tensor_scalar(a2, a1, 1.0 / TURN, ccol("turn", 64, 128), ALU.mult, ALU.add))
                link(dve.tensor_scalar(a2, a2, MAGIC, None, ALU.add))
                link(dve.tensor_scalar(a2, a2, -MAGIC, None, ALU.add))
                for step in (C1, C2, C3):
                    link(dve.scalar_tensor_tensor(out=a1, in0=a2, scalar=-step, in1=a1, op0=ALU.mult, op1=ALU.add))
                link(dve.tensor_scalar(a1, a1, ccol("phase", 64, 128), float(np.float32(3.1415925)), ALU.add, ALU.min))
                dve.tensor_scalar(a3, a1, float(np.float32(-3.1415925)), None, ALU.max).then_inc(trig_ready, 1)
                dve.wait_ge(trig_done, 1)
                link(dve.tensor_scalar(csn[R, :], csn[R, :], ccol("sign", 64, 128), None, ALU.mult))
                n = MIX
                link(dve.memset(cvin[:, :, 0:3], 0.0))
                dve.sem_inc(conv2_done, 4)
                dve.sem_inc(cvin_done, 4)
                dve.sem_inc(silu2_done, 4)
                dve.sem_inc(f_free, 4)
                taps = lambda k, t: vec[:, bass.ds(t + (VEC["conv_w_2"] + k * NCONV), 1)]
                with dve.Fori(0, 3) as i:
                    for j in range(2):
                        rest_slab(i * 2 + (n + j + 2), n + j)
                        for m in range(2):
                            c = 2 * j + m
                            t = i * 4 + c
                            dve.wait_ge(cvin_done, i * 4 + (c + 5))
                            dve.wait_ge(silu2_done, i * 4 + (c + 1))
                            dve.tensor_scalar(cv[:, c, :], cvin[:, c, 0:T], taps(0, t), None, ALU.mult).then_inc(conv2_step, 1)
                            for k in range(1, 4):
                                dve.wait_ge(conv2_step, i * 12 + (3 * c + k))
                                dve.scalar_tensor_tensor(out=cv[:, c, :], in0=cvin[:, c, k:k + T], scalar=taps(k, t), in1=cv[:, c, :],
                                                         op0=ALU.mult, op1=ALU.add).then_inc(conv2_step if k < 3 else conv2_done, 1)
                for j in range(4):
                    static_rest(n + 8 + j)
                dve.wait_ge(slab_done, n + 10)
                dve.tensor_tensor(normed[64:96, 0, :], PS[64:96, 7, :], csn[64:96, :], ALU.mult).then_inc(trig_step, 1)
                dve.tensor_tensor(normed[64:96, 1, :], PS[96:128, 7, :], csn[96:128, :], ALU.mult).then_inc(trig_step, 1)
                dve.wait_ge(trig_step, 2)
                dve.tensor_tensor(krope[64:96, :], normed[64:96, 0, :], normed[64:96, 1, :], ALU.add).then_inc(krope_done, 1)
                link(dve.tensor_copy(ab[:, :, :], PS[:, 0, 0:TT * 8].rearrange("p (t e) -> p t e", t=TT)))
                dve.sem_inc(ab_done, 1)
                dve.wait_ge(heads_landed, 16)
                per = lambda ap: ap.unsqueeze(1).to_broadcast([P, TT, GH])
                link(dve.tensor_tensor(cols[:, GL, :, :], ab[:, :, 0:GH], per(heads_c[:, GH:2 * GH]), ALU.add))
                link(dve.tensor_scalar(cols[:, KD, :, :], cols[:, GL, :, :], 0.0, None, ALU.max))
                dve.scalar_tensor_tensor(out=cols[:, TMP, :, :], in0=cols[:, KD, :, :], scalar=-2.0, in1=cols[:, GL, :, :],
                                         op0=ALU.mult, op1=ALU.add).then_inc(soft1, 1)
                dve.wait_ge(soft2, 3)
                link(dve.tensor_tensor(cols[:, EG, :, :], cols[:, KD, :, :], cols[:, EG, :, :], ALU.add))
                dve.scalar_tensor_tensor(out=rowsrc[:, :, 0:GH], in0=cols[:, EG, :, :], scalar=-1.0, in1=per(small[:, 0, :]),
                                         op0=ALU.mult, op1=ALU.mult).then_inc(cols_done, 1)
                dve.wait_ge(beta1, 1)
                link(dve.tensor_scalar(cols[:, BETA, :, :], cols[:, BETA, :, :], 1.0, None, ALU.add))
                link(dve.reciprocal(cols[:, BETA, :, :], cols[:, BETA, :, :]))
                dve.wait_ge(ssd_done, 1)
                link(dve.reciprocal(ssqk[:, :, :], ssqk[:, :, :]))
                link(dve.tensor_scalar(rowsrc[:, :, 2 * GH:3 * GH], ssqk[:, :, 0:GH], float(P) ** -0.5, None, ALU.mult))
                link(dve.tensor_copy(cols[:, RK, :, :], ssqk[:, :, GH:2 * GH]))
                link(dve.tensor_tensor(rowsrc[:, :, GH:2 * GH], cols[:, BETA, :, :], cols[:, RK, :, :], ALU.mult))
                dve.wait_ge(gcum_ready, 1)
                dve.tensor_copy(cols[:, GCOL, :, :], PS[:, 1, 64:64 + TT * GH].rearrange("p (c h) -> p c h", c=TT)).then_inc(cols_done, 1)
                dve.wait_ge(mstd_done, 2)
                link(dve.reciprocal(mstd[:, :, :], mstd[:, :, :]))
                for k in range(3):
                    g = vcol("q_norm")(k) if k < 2 else vcol("kv_norm")(0)
                    dve.scalar_tensor_tensor(out=cqr[:, k, :], in0=cqr[:, k, :], scalar=g, in1=mstd[:, k // 2, :],
                                             op0=ALU.mult, op1=ALU.mult).then_inc(mc_ready, 1)
                for k in range(3):
                    dve.wait_ge(mc_hi_done, k + 1)
                    dve.tensor_tensor(mc_lo[:, k, :], cqr[:, k, :], mc_hi[:, k, :].bitcast(F32), ALU.subtract).then_inc(mc_lo_done, 1)
                dve.wait_ge(soft2, 4)
                link(dve.tensor_tensor(cols[:, KBS, :, :], rowsrc[:, :, GH:2 * GH], cols[:, EG, :, :], ALU.mult))

                def head_rope(h):
                    dve.wait_ge(q_ready, h + 1)
                    if h:
                        dve.wait_ge(qr_done, h)
                    if h >= 2:
                        dve.wait_ge(ms_ready, 4 * (h - 1))
                    dve.tensor_tensor(normed[64:96, 0, :], PS[64:96, 0, :], csn[64:96, :], ALU.mult).then_inc(trig_step, 1)
                    dve.tensor_tensor(normed[64:96, 1, :], PS[96:128, 0, :], csn[96:128, :], ALU.mult).then_inc(trig_step, 1)
                    dve.wait_ge(trig_step, 2 * h + 4)
                    dve.tensor_tensor(qh[64:96, h % 2, :], normed[64:96, 0, :], normed[64:96, 1, :], ALU.add).then_inc(qr_done, 1)

                def row_max(h, t):
                    g = 4 * h + t
                    dve.wait_ge(ms_ready, g + 1)
                    if h:
                        dve.wait_ge(exp_done, g - 3)
                    link(dve.tensor_reduce(small[:, 0, t:t + 1], PS[:, 2 + t, 0:(t + 1) * P], AX.X, ALU.max))
                    dve.tensor_scalar(small[:, 1, t:t + 1], small[:, 0, t:t + 1], -(QK ** -0.5), None, ALU.mult).then_inc(nmx_done, 1)

                def weigh(h, t):
                    dve.wait_ge(exp_done, 4 * h + t + 1)
                    link(dve.reciprocal(small[:, 2, t:t + 1], small[:, 2, t:t + 1]))
                    p = pr[:, t % 2, 0:(t + 1) * P]
                    dve.tensor_scalar(p, p, small[:, 2, t:t + 1], None, ALU.mult).then_inc(p_ready, 1)

                dve.wait_ge(krope_done, 1)
                head_rope(0)
                for t in range(TT):
                    row_max(0, t)
                for h in range(MH):
                    weigh(h, 0)
                    if h + 1 < MH:
                        head_rope(h + 1)
                    for t in range(1, TT):
                        weigh(h, t)
                    if h + 1 < MH:
                        for t in range(TT):
                            row_max(h + 1, t)
                    if h % 2:
                        dve.wait_ge(mo_hi_done, h // 2 + 1)
                        dve.tensor_tensor(act_lo[:, 4 + h // 2, :], bank(7), act_hi[:, 4 + h // 2, :].bitcast(F32),
                                          ALU.subtract).then_inc(mo_lo_done, 1)
                static_rest(n + 12)
                static_rest(n + 13)

                dve.wait_ge(o2_ready, MH)
                for c in range(TT):
                    if c:
                        dve.wait_ge(rows_ready, c)
                    dve.tensor_copy(bcs[:, :, :], rowsrc[:, c, :].unsqueeze(2).to_broadcast([P, 3 * GH, P])).then_inc(bcs_done, 1)
                    dve.wait_ge(rows_ready, c + 1)
                    if c:
                        dve.wait_ge(ptm_done, GH * c)
                    for h in range(GH):
                        ins = dve.scalar_tensor_tensor(out=ex[:, hs(h)], in0=PS[:, 0, hs(h)], scalar=col(GCOL, c, h), in1=cc("causal"),
                                                       op0=ALU.subtract, op1=ALU.add)
                        if h < GH - 1:
                            link(ins)
                    link(ins)
                    link(dve.tensor_copy(cols[:, GL, c, :], hb(bank(0))[:, :, P - 1]))
                    link(dve.tensor_tensor(cols[:, KD, c, :], cols[:, GL, c, :], cols[:, GCOL, c, :], ALU.subtract))
                    dve.sem_inc(eraw_done, 1)
                    dve.wait_ge(kd_exp, 3 * c + 3)
                    link(dve.tensor_tensor(cols[:, KDS, c, :], cols[:, KDS, c, :], cols[:, RK, c, :], ALU.mult))
                    dve.sem_inc(kd_done, 1)
                    dve.wait_ge(kq_ready, c + 1)
                    dve.wait_ge(e_done, c + 1)
                    for h in range(GH):
                        dve.scalar_tensor_tensor(out=mt[:, c, hs(h)], in0=PS[:, 3, hs(h)], scalar=col(RK, c, h), in1=ex[:, hs(h)],
                                                 op0=ALU.mult, op1=ALU.mult).then_inc(mt_done, 1)
                    for h in range(GH):
                        dve.scalar_tensor_tensor(out=ptm[:, c, hs(h)], in0=PS[:, 4, hs(h)], scalar=col(RK, c, h), in1=ex[:, hs(h)],
                                                 op0=ALU.mult, op1=ALU.mult).then_inc(ptm_done, 1)
                    dve.wait_ge(mt_done, GH * (c + 1))
                    link(dve.tensor_tensor(mt[:, c, :], mt[:, c, :], bank(1), ALU.mult))
                    dve.wait_ge(ptm_done, GH * (c + 1))
                    link(dve.tensor_tensor(ptm[:, c, :], ptm[:, c, :], bank(2), ALU.mult))
                    link(dve.tensor_tensor(egrow[:, :], egrow[:, :], bank(2), ALU.mult))
                    dve.tensor_tensor(qkv[:, 0:GH, c * P:(c + 1) * P], qkv[:, 0:GH, c * P:(c + 1) * P], hb(egrow[:, :]),
                                      ALU.mult).then_inc(qdec_done, 1)
                wide = lambda ap: ap.unsqueeze(1).to_broadcast([P, GH, P])
                level = lambda s: wide(con[:, CON["levels"] + s * P:CON["levels"] + (s + 1) * P])
                for c in range(TT):
                    link(dve.tensor_tensor(hb(gy[:, c, :]), hb(mt[:, c, :]), level(0), ALU.mult))
                    dve.tensor_tensor(hb(gy[:, c, :]), wide(cc("ident")), hb(gy[:, c, :]), ALU.subtract).then_inc(y0_done, 1)

                def mask_level(g):
                    if g >= 2:
                        dve.wait_ge(lp_ready, g - 1)
                    dve.tensor_tensor(hb(lv[:, g % 2, :]), hb(mt[:, g % TT, :]), level(g // TT + 1), ALU.mult).then_inc(lv_done, 1)

                G = (LEVELS - 1) * TT
                mask_level(0)
                mask_level(1)
                dve.wait_ge(y0_done, TT)
                dve.wait_ge(x0_done, TT)
                for g in range(G):
                    if g + 2 < G:
                        mask_level(g + 2)
                    c = g % TT
                    dve.wait_ge(xx_ready, g + 1)
                    if g >= TT:
                        dve.wait_ge(xy_done, 2 * (g - TT + 1))
                    dve.tensor_tensor(gx[:, c, :], gx[:, c, :], bank(2 + g % 2), ALU.subtract).then_inc(xy_done, 1)
                    dve.tensor_tensor(gy[:, c, :], gy[:, c, :], bank(4 + g % 2), ALU.subtract).then_inc(xy_done, 1)
                for c in range(TT):
                    dve.wait_ge(uw_ready, c + 1)
                    dve.tensor_copy(gp[:, c, :], bank(7)).then_inc(wt_done, 1)
                dve.wait_ge(u_done, TT)
                for c in range(TT):
                    if c == 0:
                        dve.sem_inc(vn_done, 1)
                    else:
                        dve.wait_ge(ws_ready, c)
                        dve.tensor_tensor(gx[:, c, :], gx[:, c, :], bank(0), ALU.subtract).then_inc(vn_done, 1)
                    if c + 1 < TT:
                        dve.wait_ge(sup_ready, c + 1)
                        if c:
                            dve.wait_ge(o3_ready, c + 1)
                        for h in range(GH):
                            if c == 0:
                                ins = dve.tensor_copy(state[:, h, :], PS[:, 2, hs(h)])
                            else:
                                ins = dve.scalar_tensor_tensor(out=state[:, h, :], in0=state[:, h, :], scalar=col(EGL, c, h),
                                                               in1=PS[:, 2, hs(h)], op0=ALU.mult, op1=ALU.add)
                            ins.then_inc(state_done, 1)
                        dve.wait_ge(state_done, GH * (c + 1))
                for h in range(GH):
                    dve.wait_ge(gstd_done, h + 1)
                    link(dve.reciprocal(gstd[:, h, :], gstd[:, h, :]))
                    link(dve.scalar_tensor_tensor(out=oT[:, h, :], in0=oT[:, h, :], scalar=vcol("gdn_out")(0), in1=gstd[:, h, :],
                                                  op0=ALU.mult, op1=ALU.mult))
                    dve.tensor_tensor(oT[:, h, :], oT[:, h, :], gate[:, h, :], ALU.mult).then_inc(go_ready, 1)
                for h in range(GH):
                    dve.wait_ge(go_hi_done, h + 1)
                    dve.tensor_tensor(act_lo[:, h, :], oT[:, h, :], act_hi[:, h, :].bitcast(F32), ALU.subtract).then_inc(go_lo_done, 1)
                for j in range(4):
                    static_rest(n + 14 + j)
                post("post2", "mix_post", post_done)
                dve.wait_ge(post_done, KT)

            if has("all"):
                dve.sem_inc(relu_done, 4)
                dve.sem_inc(sqr_done, 2)
                dve.sem_inc(h2_lo_done, 2)
                norm_in("ffn2", x_tile, vcol("ffn_pre"), None)
                n, seen = FFN2, 0
                for c, tiles in enumerate(F2CH):
                    with dve.Fori(0, tiles // 4) as i:
                        for j in range(2):
                            rest_slab(i * 2 + (n + j + 2), n + j)
                            for m in range(2):
                                t = 2 * j + m
                                dve.wait_ge(relu_done, i * 4 + (seen + t + 5))
                                dve.wait_ge(h2_lo_done, i * 4 + (seen + t + 1))
                                dve.tensor_tensor(hraw2[:, m, :], sg2[:, m, :], sg2[:, m, :], ALU.mult).then_inc(sqr_done, 1)
                            for m in range(2):
                                t = 2 * j + m
                                dve.wait_ge(h2_hi_done, i * 4 + (seen + t + 1))
                                at = bass.ds(i * 4 + t, 1)
                                dve.tensor_tensor(hid2_lo[:, at, :].rearrange("p o t -> p (o t)"), hraw2[:, m, :],
                                                  hid2_hi[:, at, :].rearrange("p o t -> p (o t)").bitcast(F32),
                                                  ALU.subtract).then_inc(h2_lo_done, 1)
                    n += tiles // 2
                    seen += tiles
                    with dve.Fori(0, tiles // 4 - 1) as i:
                        rest_slab(i * 2 + (n + 2), n)
                        rest_slab(i * 2 + (n + 3), n + 1)
                    n += tiles // 2
                    static_rest(n)
                    static_rest(n + 1)
                dve.wait_ge(f2_copied, KT)
                dve.wait_ge(slab_done, N_SLABS)
                for b in range(KT):
                    dve.tensor_tensor(facc[:, b, :], facc[:, b, :], bank(b), ALU.add).then_inc(f_done, 1)
                dve.wait_ge(f_done, KT)
                post("last", "ffn_post", x_final)
            if UPTO == "mix":
                dve.sem_inc(x_final, KT)
            if UPTO == "ret":
                dve.wait_ge(banks_free, 8 * (RH + 1))
                dve.sem_inc(x_final, KT)


def decay_tables():
    h = np.arange(RH, dtype=np.float64)
    lf = np.log1p(-np.exp2(-5.0 - h))[:, None, None]
    lb = np.log1p(-np.exp2(-5.5 - h))[:, None, None]
    dx = (np.arange(TOEP_X)[None, :] - (TT - 1) * P - np.arange(P)[:, None])[None]
    fwd = np.where(dx >= 0, np.exp(np.maximum(dx, 0) * lf), 0.0)
    bwd = np.where(dx <= 0, np.exp(np.maximum(-dx, 0) * lb), 0.0)
    dc = (np.arange(TOEP_C)[None, :] - (CT - 1) * P - np.arange(P)[:, None])[None]
    both = np.exp((dc + C) * lf) + np.exp((T - dc) * lb)
    tab = np.concatenate([fwd + bwd, both], axis=2) / np.sqrt(RD)
    return np.concatenate([tab, tab[-1:]], axis=0).astype(np.float32)


def rope1_table():
    n = RD // 4
    freq = 10000.0 ** (-np.arange(n, dtype=np.float32) / n)
    both = np.concatenate([freq, freq]).astype(np.float32)[:, None]
    sign = np.concatenate([np.ones(n), -np.ones(n)])[:, None]
    row = both * np.arange(T // GRID_W, dtype=np.float32)[None]
    col = both * np.arange(GRID_W, dtype=np.float32)[None]
    return np.concatenate([np.cos(row), sign * np.sin(row), np.cos(col), sign * np.sin(col)], axis=1).astype(np.float32)


def constant_table():
    i = np.arange(P)
    key, query = i[:, None], i[None, :]
    tab = np.zeros((P, N_CON), np.float64)

    def put(name, v):
        v = np.asarray(v, np.float64).reshape(P, -1)
        tab[:, CON[name]:CON[name] + v.shape[1]] = v

    put("ident", np.eye(P))
    put("upper", key <= query)
    put("causal", np.where(query >= key, 0.0, NEG))
    put("mask_q", (key == 0) & (query < 64))
    put("mask_k", np.where((key == 0) & (query >= 64), NEG, 0.0))
    levels = []
    for s in range(LEVELS):
        b = 2 ** s
        levels.append((query // b % 2 == 1) & (key // b == query // b - 1))
    put("levels", np.concatenate(levels, axis=1))
    inv = 10000.0 ** (-np.arange(0, ROPE, 2, dtype=np.float32) / ROPE)
    r = i - 64
    freq = np.where(r >= 0, inv[r % (ROPE // 2)], 0.0)
    cosine = (r >= 0) & (r < ROPE)
    put("freq", freq)
    put("turn", np.where(cosine, 0.25, 0.0))
    put("phase", np.where(cosine, np.pi / 2, 0.0))
    put("sign", np.where((r >= ROPE) & (r < ROPE + ROPE // 2), -1.0, 1.0))
    return tab.astype(np.float32)


def by_columns(w, c0):
    return w[:, c0:c0 + 256].reshape(KT, P, 256).transpose(1, 0, 2).reshape(P, SLAB)


def by_rows(w, r0):
    return w[r0:r0 + 256].reshape(2, P, D).transpose(1, 0, 2).reshape(P, SLAB)


def value_slab(w, r0, c0):
    return w[r0:r0 + 512, c0:c0 + 512].reshape(4, P, 512).transpose(1, 0, 2).reshape(P, SLAB)


def swiglu_slabs(w1, w3, w2):
    out, t0 = [], 0
    for tiles in FCH:
        for t in range(t0, t0 + tiles, 2):
            out += [by_columns(w1, t * P), by_columns(w3, t * P)]
        out += [by_rows(w2, t * P) for t in range(t0, t0 + tiles, 2)]
        t0 += tiles
    return out


def slab_stream(a):
    out = []
    w, wo = a["ret_w_qkvg"][0], a["ret_w_o"][0]
    for h in range(RH):
        out += [by_columns(w, h * RD), by_columns(w, D + h * RD)]
        out += [value_slab(w, r, 2 * D + h * RV) for r in (0, 512)]
        out += [by_columns(w, 4 * D + h * RV + c) for c in (0, 256)]
        out += [by_rows(wo, h * RV + r) for r in (0, 256)]
    out += swiglu_slabs(a["ffn_w1"][0], a["ffn_w3"][0], a["ffn_w2"][0])
    w, wo = a["conv_w_in"][0], a["conv_w_out"][0]
    for t in range(0, KT, 2):
        out += [by_columns(w, D + t * P), by_columns(w, 2 * D + t * P)]
    out += [by_columns(w, c) for c in range(0, D, 256)]
    out += [by_columns(wo, c) for c in range(0, D, 256)]
    out += swiglu_slabs(a["ffn_w1"][1], a["ffn_w3"][1], a["ffn_w2"][1])
    w = a["w_in_2"][0]
    g, swap = GH * P, np.r_[ROPE // 2:ROPE, 0:ROPE // 2]
    out += [by_columns(w, c) for c in range(0, 4 * g, 256)]
    ab, cq = w[:, 4 * g:4 * g + 2 * GH], w[:, 4 * g + 2 * GH:4 * g + 2 * GH + 256]
    ckv, kr = w[:, -(P + ROPE):-ROPE], w[:, -ROPE:]
    out.append(by_columns(cq, 0))
    blank = np.zeros((D, 64 - 2 * GH), np.float32)
    out.append(by_columns(np.concatenate([ckv, ab, blank, kr, kr[:, swap]], axis=1), 0))
    qu = a["w_q_up_2"][0].reshape(2 * P, MH, QK)
    out.append(by_rows(np.concatenate([qu, qu[:, :, NOPE:][:, :, swap]], axis=2).reshape(2 * P, D), 0))
    kv = a["w_kv_up_2"][0].reshape(P, MH, NOPE + MV)
    out.append(np.concatenate([kv[:, :, :NOPE].reshape(P, -1), kv[:, :, NOPE:].reshape(P, -1),
                               np.zeros((P, SLAB - D), np.float32)], axis=1))
    out += [by_columns(a["w_out_2"][0], c) for c in range(0, D, 256)]
    t0 = 0
    for tiles in F2CH:
        out += [by_columns(a["w_up_2"][0], t * P) for t in range(t0, t0 + tiles, 2)]
        out += [by_rows(a["w_down_2"][0], t * P) for t in range(t0, t0 + tiles, 2)]
        t0 += tiles
    return np.stack(out)


def feature_major(t):
    return np.ascontiguousarray(t.T.reshape(-1, P, t.shape[0]).transpose(1, 0, 2))


def vector_table(a):
    rows = [a["ada_b"].reshape(-1), a["c"].reshape(-1), a["c_ctx"], a["norm_mix"].reshape(-1),
            a["norm_ffn"].reshape(-1), a["final_norm"], a["mix_pre_norm_2"][0], a["mix_post_norm_2"][0],
            a["ffn_pre_norm_2"][0], a["ffn_post_norm_2"][0], a["conv_w"][0].reshape(-1), a["conv_w_2"][0].reshape(-1),
            a["gdn_out_norm_2"][0], a["q_norm_2"][0], a["kv_norm_2"][0]]
    return np.ascontiguousarray(np.concatenate(rows).reshape(-1, P).T)


def kernel(**inputs):
    import concourse.bacc as _bacc
    from concourse.bass_utils import run_bass_kernel_spmd as _run

    a = {k: np.asarray(v) for k, v in inputs.items()}
    arrays = {
        "slabs": slab_stream(a),
        "ada": np.stack([by_rows(a["ada_w"][l][:, u * D:(u + 1) * D], r * 256)
                         for l in range(2) for u in range(6) for r in range(4)]),
        "x_t": feature_major(a["x"][0]),
        "ctx_t": feature_major(a["ctx"][0]),
        "vecs": vector_table(a),
        "decay": decay_tables(),
        "rope1": rope1_table(),
        "consts": constant_table(),
        "positions": np.ascontiguousarray(np.broadcast_to(a["positions_2"], (P, T))),
        "per_head": np.ascontiguousarray(np.broadcast_to(
            np.concatenate([a["a_log_2"][0], a["dt_bias_2"][0]])[None], (P, 2 * GH))),
    }
    nc = _bacc.Bacc("TRN2", target_bir_lowering=False, num_devices=1)
    args = [nc.dram_tensor(name, v.shape, mybir.dt.from_np(v.dtype), kind="ExternalInput").ap()
            for name, v in arrays.items()]
    args.append(nc.dram_tensor("out_t", (P, KT, T), F32, kind="ExternalOutput").ap())
    build(nc, *args)
    r = _run(nc, [arrays], core_ids=[0])
    got = r.results[0]["out_t"]
    return np.ascontiguousarray(got.transpose(1, 0, 2).reshape(D, T).T)[None]
```

```python
from contextlib import ExitStack

import numpy as np

import concourse.bass as bass
from concourse import mybir

P = 128
D = 1024
KT = D // P
T = 512
TT = T // P
C = 256
CT = C // P
EPS = 1e-6
SLAB = 2048

RH = 4
RD = D // RH
RV = 2 * D // RH
RDT, RVT = RD // P, RV // P
KEYT = TT + CT
TOEP_X = T + (TT - 1) * P
TOEP_C = T + (CT - 1) * P
GRID_W = 64

FT = 22
FCH = (12, 10)
F2T = 32
F2CH = (16, 16)

GH = 4
MH = 8
NOPE, ROPE, MV = 64, 32, 64
QK = NOPE + ROPE
NCONV = 12
LEVELS = 7
NEG = -1.0e30

CON = {}
_at = 0
for _name, _n in (("ident", P), ("upper", P), ("causal", P), ("mask_q", P), ("mask_k", P), ("levels", LEVELS * P),
                  ("freq", 1), ("turn", 1), ("phase", 1), ("sign", 1)):
    CON[_name] = _at
    _at += _n
N_CON = _at

RET = 0
FFN0 = RET + 8 * RH
CONV = FFN0 + FT + FT // 2
FFN1 = CONV + 16
MIX = FFN1 + FT + FT // 2
FFN2 = MIX + 16
N_SLABS = FFN2 + F2T // 2 + F2T // 2

N_ADA = 48

VEC = {}
_at = 0
for _name, _n in (("ada_b", 96), ("c", 8), ("c_ctx", 8), ("norm_mix", 16), ("norm_ffn", 16), ("final_norm", 8),
                  ("mix_pre", 8), ("mix_post", 8), ("ffn_pre", 8), ("ffn_post", 8), ("conv_w", 24),
                  ("conv_w_2", 48), ("gdn_out", 1), ("q_norm", 2), ("kv_norm", 1)):
    VEC[_name] = _at
    _at += _n
N_VEC = _at

F32 = mybir.dt.float32
F32R = mybir.dt.float32r
I32 = mybir.dt.int32
ALU = mybir.AluOpType
ACT = mybir.ActivationFunctionType
AX = mybir.AxisListType


def build(nc, slabs, ada, x_in, ctx_in, vecs, decay, rope1, consts, positions, per_head, out):
    with ExitStack() as ctx:
        def sem(name):
            return ctx.enter_context(nc.semaphore(name))

        def sb(name, shape, dt=F32, scope=ctx):
            return scope.enter_context(nc.sbuf_tensor(name, shape, dt))

        PS = ctx.enter_context(nc.psum_tensor("PS", [P, 8, 512], F32))
        raw = sb("raw", [P, 2, SLAB])
        w_hi = sb("w_hi", [P, 2, SLAB], F32R)
        w_lo = sb("w_lo", [P, 2, SLAB], F32R)
        x = sb("x", [P, KT, T])
        vec = sb("vec", [P, N_VEC])
        silu_c = sb("silu_c", [P, KT, 2])
        mod = sb("mod", [P, 2 * 6 * KT])
        mod_ctx = sb("mod_ctx", [P, 2 * KT])
        gain = sb("gain", [P, 5, KT])
        ones = sb("ones", [P, P])
        eps = sb("eps", [P, 1])
        std = sb("std", [P, T])
        rstd = sb("rstd", [P, T])
        normed = sb("normed", [P, 2, T])
        acc = sb("acc", [P, D])
        sq = acc[:, :].rearrange("p (two t) -> p two t", two=2)

        with ExitStack() as own:
            with ExitStack() as start:
                early_raw = sb("early_raw", [P, 4, SLAB], F32, start)
            act_hi = sb("act_hi", [P, KT, T], F32R, own)
            act_lo = sb("act_lo", [P, KT, T], F32R, own)
            early = own.enter_context(ExitStack())
            ada_raw = sb("ada_raw", [P, 2, SLAB], F32, early)
            early_slab = [ada_raw[:, 0, :], ada_raw[:, 1, :]] + [early_raw[:, a, :] for a in range(4)]
            early_slab += early_slab[0:2]
            with ExitStack() as ret:
                ctx_hi = sb("ctx_hi", [P, KT, C], F32R, ret)
                ctx_lo = sb("ctx_lo", [P, KT, C], F32R, ret)
                rq = sb("rq", [P, RDT, T], F32, ret)
                rk = sb("rk", [P, RDT, T + C], F32, ret)
                rv = sb("rv", [P, KEYT, RV], F32, ret)
                rs = sb("rs", [P, KEYT, T], F32, ret)
                rg = sb("rg", [P, RVT, T], F32, ret)
                ry_hi = sb("ry_hi", [P, RVT, T], F32R, ret)
                ry_lo = sb("ry_lo", [P, RVT, T], F32R, ret)
                toep = sb("toep", [P, TOEP_X + TOEP_C], F32, ret)
                rope = sb("rope", [P, 2 * (T // GRID_W + GRID_W)], F32, ret)
                pre = [rv[:, 2 * a:2 * a + 2, :].rearrange("p a b -> p (a b)") for a in range(3)]
                pre.append(rg[:, 0:2, :].rearrange("p a b -> p (a b)"))
                std_c, rstd_c = rs[:, 4, 0:C], rs[:, 5, 0:C]
                xc = rs[:, 0:4, :].rearrange("p a b -> p (a b)").rearrange("p (k t) -> p k t", k=KT)
            with ExitStack() as ffn:
                hid_hi = sb("hid_hi", [P, FCH[0], T], F32R, ffn)
                hid_lo = sb("hid_lo", [P, FCH[0], T], F32R, ffn)
                sg = sb("sg", [P, 2, T], F32, ffn)
                hraw = sb("hraw", [P, 2, T], F32, ffn)
                u = sb("u", [P, KT, T + 2], F32, ffn)
            early.close()
            with ExitStack() as mix:
                qkv = sb("qkv", [P, NCONV, T], F32, mix)
                gate = sb("gate", [P, GH, T], F32, mix)
                con = sb("con", [P, N_CON], F32, mix)
                heads_c = sb("heads_c", [P, 2 * GH], F32, mix)
                ab = sb("ab", [P, TT, 2 * GH], F32, mix)
                rowsrc = sb("rowsrc", [P, TT, 3 * GH], F32, mix)
                cols = sb("cols", [P, 10, TT, GH], F32, mix)
                ssqk = sb("ssqk", [P, TT, 2 * GH], F32, mix)
                csn = sb("csn", [P, T], F32, mix)
                small = sb("small", [P, 3, 4], F32, mix)
                with ExitStack() as mla:
                    cvin = sb("cvin", [P, 4, T + 3], F32, mla)
                    cv = sb("cv", [P, 4, T], F32, mla)
                    cqr = sb("cqr", [P, 3, T], F32, mla)
                    krope = sb("krope", [P, T], F32, mla)
                    mc_hi = sb("mc_hi", [P, 3, T], F32R, mla)
                    mc_lo = sb("mc_lo", [P, 3, T], F32R, mla)
                    mstd = sb("mstd", [P, 2, T], F32, mla)
                    qh = cv[:, 2:4, :]
                    kh = sb("kh", [P, 2, T], F32, mla)
                    mv = sb("mv", [P, TT, MH * MV], F32, mla)
                    pr2 = sb("pr2", [P, 2, T], F32, mla)
                    pr = [cv[:, 0, :], cv[:, 1, :], pr2[:, 0, :], pr2[:, 1, :]]
                    prt = cvin[:, :, 0:T]
                    pos_i = cv[:, 0, :].bitcast(I32)
                with ExitStack() as gdn:
                    mt = sb("mt", [P, TT, T], F32, gdn)
                    gx = sb("gx", [P, TT, T], F32, gdn)
                    gy = sb("gy", [P, TT, T], F32, gdn)
                    gp = sb("gp", [P, TT, T], F32, gdn)
                    ptm = sb("ptm", [P, TT, T], F32, gdn)
                    kbg = sb("kbg", [P, TT, T], F32, gdn)
                    lv = sb("lv", [P, 2, T], F32, gdn)
                    ex = sb("ex", [P, T], F32, gdn)
                    egrow = sb("egrow", [P, T], F32, gdn)
                    bcs = gx[:, 0:3, :].rearrange("p a (b i) -> p (a b) i", i=P)
                    state = lv[:, 0, :].rearrange("p (h i) -> p h i", h=GH)
            with ExitStack() as ffn2:
                facc = sb("facc", [P, KT, T], F32, ffn2)
                hid2_hi = sb("hid2_hi", [P, 16, T], F32R, ffn2)
                hid2_lo = sb("hid2_lo", [P, 16, T], F32R, ffn2)
                sg2 = sb("sg2", [P, 2, T], F32, ffn2)
                hraw2 = sb("hraw2", [P, 2, T], F32, ffn2)

        slab_landed = [sem(f"slab_landed{j}") for j in range(2)]
        w_hi_done = sem("w_hi_done")
        w_lo_done = sem("w_lo_done")
        slab_done = sem("slab_done")
        vec_landed = sem("vec_landed")
        x_landed = sem("x_landed")
        xc_landed = sem("xc_landed")
        rope_landed = sem("rope_landed")
        toep_landed = sem("toep_landed")
        ada_landed = [sem(f"ada_landed{j}") for j in range(2)]
        early_landed = ada_landed + [sem(f"early_landed{a}") for a in range(2, 6)]
        ada_used = sem("ada_used")
        consts_set = sem("consts_set")
        silu_c_done = sem("silu_c_done")
        mod0_summed = sem("mod0_summed")
        pre_step = sem("pre_step")
        pre_ready = sem("pre_ready")
        pre_summed = sem("pre_summed")
        gain_done = sem("gain_done")
        sq_ready = sem("sq_ready")
        sq_used = sem("sq_used")
        std_ready = sem("std_ready")
        y_ready = sem("y_ready")
        hi_ready = sem("hi_ready")
        lo_ready = sem("lo_ready")
        banks_free = sem("banks_free")
        rope_read = sem("rope_read")
        roped = sem("roped")
        kctx_done = sem("kctx_done")
        v_done = sem("v_done")
        s_ready = sem("s_ready")
        s_decayed = sem("s_decayed")
        g_done = sem("g_done")
        pv_ready = sem("pv_ready")
        osq_ready = sem("osq_ready")
        osum_ready = sem("osum_ready")
        ostd_ready = sem("ostd_ready")
        ry_ready = sem("ry_ready")
        ry_hi_done = sem("ry_hi_done")
        ry_lo_done = sem("ry_lo_done")
        acc_ready = sem("acc_ready")
        unit_summed = sem("unit_summed")
        unit_done = sem("unit_done")
        act_silu = sem("act_silu")
        hraw_ready = sem("hraw_ready")
        hid_hi_done = sem("hid_hi_done")
        hid_lo_done = sem("hid_lo_done")
        pads_zero = sem("pads_zero")
        conv_step = sem("conv_step")
        conv_y = sem("conv_y")
        wout_added = sem("wout_added")
        tile_summed = sem("tile_summed")
        head_summed = sem("head_summed")
        down_added = sem("down_added")
        x_final = sem("x_final")
        out_stored = sem("out_stored")
        vchain = sem("vchain")
        unit_step = sem("unit_step")
        final_done = sem("final_done")
        con_landed = sem("con_landed")
        pos_landed = sem("pos_landed")
        heads_landed = sem("heads_landed")
        cvin_done = sem("cvin_done")
        conv2_step = sem("conv2_step")
        conv2_done = sem("conv2_done")
        silu2_done = sem("silu2_done")
        gate2_done = sem("gate2_done")
        cqr_done = sem("cqr_done")
        ab_done = sem("ab_done")
        msq_ready = sem("msq_ready")
        msum_ready = sem("msum_ready")
        mstd_done = sem("mstd_done")
        mc_ready = sem("mc_ready")
        mc_hi_done = sem("mc_hi_done")
        mc_lo_done = sem("mc_lo_done")
        mv_ready = sem("mv_ready")
        mv_done = sem("mv_done")
        krope_done = sem("krope_done")
        kr_copied = sem("kr_copied")
        q_ready = sem("q_ready")
        qn_done = sem("qn_done")
        qr_done = sem("qr_done")
        kn_done = sem("kn_done")
        ms_ready = sem("ms_ready")
        nmx_done = sem("nmx_done")
        exp_done = sem("exp_done")
        p_ready = sem("p_ready")
        t_ready = sem("t_ready")
        prt_done = sem("prt_done")
        o2_ready = sem("o2_ready")
        mo_hi_done = sem("mo_hi_done")
        mo_lo_done = sem("mo_lo_done")
        trig_step = sem("trig_step")
        trig_ready = sem("trig_ready")
        trig_done = sem("trig_done")
        qsq_ready = sem("qsq_ready")
        qsq_used = sem("qsq_used")
        ssd_done = sem("ssd_done")
        gcum_ready = sem("gcum_ready")
        soft1 = sem("soft1")
        soft2 = sem("soft2")
        beta1 = sem("beta1")
        cols_done = sem("cols_done")
        rows_ready = sem("rows_ready")
        rows_used = sem("rows_used")
        bcs_done = sem("bcs_done")
        eraw_done = sem("eraw_done")
        e_done = sem("e_done")
        kd_raw = sem("kd_raw")
        kd_exp = sem("kd_exp")
        kd_done = sem("kd_done")
        kq_ready = sem("kq_ready")
        mt_done = sem("mt_done")
        ptm_done = sem("ptm_done")
        qdec_done = sem("qdec_done")
        kvt_done = sem("kvt_done")
        y0_done = sem("y0_done")
        x0_ready = sem("x0_ready")
        x0_done = sem("x0_done")
        lv_done = sem("lv_done")
        lp_ready = sem("lp_ready")
        lp_done = sem("lp_done")
        xx_ready = sem("xx_ready")
        xy_done = sem("xy_done")
        uw_ready = sem("uw_ready")
        u_done = sem("u_done")
        wt_done = sem("wt_done")
        ws_ready = sem("ws_ready")
        vn_done = sem("vn_done")
        o3_ready = sem("o3_ready")
        o3_done = sem("o3_done")
        sup_ready = sem("sup_ready")
        state_done = sem("state_done")
        gsq_ready = sem("gsq_ready")
        gss_ready = sem("gss_ready")
        gstd_done = sem("gstd_done")
        go_ready = sem("go_ready")
        go_hi_done = sem("go_hi_done")
        go_lo_done = sem("go_lo_done")
        f_free = sem("f_free")
        f_done = sem("f_done")
        post_step = sem("post_step")
        post_done = sem("post_done")
        relu_done = sem("relu_done")
        sqr_done = sem("sqr_done")
        h2_hi_done = sem("h2_hi_done")
        h2_lo_done = sem("h2_lo_done")
        f2_copied = sem("f2_copied")
        rope_step = sem("rope_step")
        orstd_done = sem("orstd_done")
        o_scaled = sem("o_scaled")

        norms = ["mix0", "ctx", "ffn0", "mix1", "ffn1", "final", "pre2", "post2", "ffn2", "last"]
        gathered = ("mix1", "ffn1", "final", "post2", "last")
        split = [q for q in norms if q not in ("final", "post2", "last")]

        def nth(name):
            return norms.index(name)

        def nth_split(name):
            return split.index(name)

        slot = lambda n: n % 2
        bank = lambda b: PS[:, b, :]
        BANK_V = (5, 6, 7, 0, 1, 2)
        BANK_S = (3, 4, 5, 6, 7, 0)
        BANK_O = (1, 2, 3, 4)
        BANK_G = (5, 6, 0, 7)
        FIN = (7, 0, 1, 2, 3, 4, 5, 6)
        BANK_T = (0, 6, 0, 6)
        MSQ = (mstd[:, 0, :], std[:, :], rstd[:, :])
        BANK_F = (4, 5, 6, 7, 0, 1, 4, 5)

        mod_at = lambda layer, part: (layer * 6 + part) * KT

        cc = lambda name, n=P: con[:, CON[name]:CON[name] + n]
        ccol = lambda name, lo=0, hi=P: con[lo:hi, CON[name]:CON[name] + 1]
        GCOL, BETA, RK, EG, KBS, GL, KD, KDS, EGL, TMP = range(10)
        col = lambda i, c, h: cols[:, i, c, h:h + 1]
        hb = lambda ap: ap.rearrange("p (h i) -> p h i", h=GH)
        q_at = lambda h, c: qkv[:, h, c * P:(c + 1) * P]
        k_at = lambda h, c: qkv[:, GH + h, c * P:(c + 1) * P]
        v_at = lambda h, c: qkv[:, 2 * GH + h, c * P:(c + 1) * P]
        hs = lambda h: slice(h * P, (h + 1) * P)
        oT = mt
        gstd = kbg

        block = ctx.enter_context(nc.Block())

        @block.sync
        def _(sp):
            def load(n, j):
                sp.dma_start(raw[:, j, :], slabs[bass.ds(n, 1)].rearrange("o p n -> p (o n)")).then_inc(slab_landed[j], 16)

            sp.wait_ge(early_landed[4], 16)
            for j in range(2):
                load(j, j)
            with sp.Fori(0, N_SLABS // 2 - 1) as i:
                for j in range(2):
                    sp.wait_ge(w_lo_done, i * 2 + (j + 1))
                    load(i * 2 + (2 + j), j)
            for k in range(2, KT + 1, 2):
                sp.wait_ge(x_final, k)
                sp.dma_start(out[:, k - 2:k, :], x[:, k - 2:k, :]).then_inc(out_stored, 16)
            sp.wait_ge(out_stored, 16 * (KT // 2))

        @block.gpsimd
        def _(pool):
            def load(n, j):
                pool.dma_start(ada_raw[:, j, :], ada[bass.ds(n, 1)].rearrange("o p n -> p (o n)")).then_inc(ada_landed[j], 16)

            for a in range(6):
                pool.dma_start(early_slab[a], ada[a]).then_inc(early_landed[a], 16)
            with pool.Fori(0, N_ADA // 2 - 3) as i:
                for j in range(2):
                    pool.wait_ge(ada_used, i * 2 + (j + 1))
                    load(i * 2 + (6 + j), j)

        @block.tensor
        def _(pe):
            def product(o, w, a, first, last):
                pe.matmul(o, w[0], a[0], start=first, stop=False)
                pe.matmul(o, w[0], a[1], start=False, stop=False)
                return pe.matmul(o, w[1], a[0], start=False, stop=last)

            def wcols(n, a, b):
                return w_hi[:, slot(n), a:b], w_lo[:, slot(n), a:b]

            def out_tile(n, m, o, moving, kts=KT):
                for k in range(kts):
                    mm = product(o, wcols(n, k * 256 + m * P, k * 256 + (m + 1) * P), moving(k), k == 0, k == kts - 1)
                return mm

            def tile_pair(n, b, moving, ready, before):
                for k in range(KT):
                    pe.wait_ge(ready, before + k + 1)
                    for m in range(2):
                        mm = product(bank(b + m), wcols(n, k * 256 + m * P, k * 256 + (m + 1) * P), moving(k),
                                     k == 0, k == KT - 1)
                return mm

            def norm_step(q, k, width=T, b=7):
                pe.wait_ge(sq_ready, 8 * q + k + 1)
                pe.matmul(PS[:, b, 0:width], ones[:, :], sq[:, k % 2, 0:width], start=(k == 0),
                          stop=(k == KT - 1)).then_inc(sq_used, 1)

            def gathered_sum(q, b=7):
                for k, part in ((5, std[:, :]), (6, sq[:, 0, :]), (7, sq[:, 1, :])):
                    pe.wait_ge(sq_ready, 8 * q + k + 1)
                    pe.wait_ge(sq_used, 8 * q + k)
                    pe.matmul(PS[:, b, :], ones[:, :], part, start=(k == 5), stop=(k == 7)).then_inc(sq_used, 1)

            def norm_sum(q, width=T, b=7):
                for k in range(KT):
                    norm_step(q, k, width, b)

            act = lambda k: (act_hi[:, k, :], act_lo[:, k, :])
            acx = lambda k: (ctx_hi[:, k, :], ctx_lo[:, k, :])

            pe.wait_ge(consts_set, 2)
            norm_sum(nth("mix0"))
            norm_sum(nth("ctx"), C, 6)
            pe.wait_ge(pre_ready, 1)
            for j in range(2):
                for m in range(KT):
                    at = 2 * m + j
                    pe.matmul(PS[:, 0, at:at + 1], pre[j][:, m * P:(m + 1) * P], ones[:, 0:1], start=True, stop=True)
            pe.wait_ge(silu_c_done, 2)
            pe.wait_ge(ada_landed[1], 32)
            for kk in range(2):
                for m in range(KT):
                    if kk == 1 and m == KT - 1:
                        pe.wait_ge(ada_used, 3)
                    mm = pe.matmul(PS[:, 1, 2 * m:2 * m + 2], early_slab[7][:, kk * D + m * P:kk * D + (m + 1) * P],
                              silu_c[:, 6 + kk, :], start=(kk == 0 and m == 0), stop=False, skip_group_check=True)
            mm.then_inc(ada_used, 1)
            pe.wait_ge(pre_ready, 2)
            for j in range(2):
                for m in range(KT):
                    at = 2 * m + j
                    mm = pe.matmul(PS[:, 1, at:at + 1], pre[2 + j][:, m * P:(m + 1) * P], ones[:, 0:1], start=False,
                                   stop=True, skip_group_check=True)
            mm.then_inc(pre_summed, 1)

            with pe.Fori(0, RH) as h:
                n0 = h * 8
                pe.wait_ge(w_lo_done, n0 + 1)
                pe.wait_ge(banks_free, n0 + 3)
                tile_pair(0, 0, act, lo_ready, 0).then_inc(slab_done, 1)
                pe.wait_ge(w_lo_done, n0 + 2)
                for m in range(RDT):
                    pe.wait_ge(banks_free, n0 + (m + 4))
                    out_tile(1, m, bank(2 + m), act)
                pe.wait_ge(banks_free, n0 + 6)
                pe.wait_ge(lo_ready, 2 * KT)
                for m in range(RDT):
                    mm = out_tile(1, m, PS[:, 4, m * C:(m + 1) * C], acx)
                mm.then_inc(slab_done, 1)
                for j in range(2):
                    pe.wait_ge(w_lo_done, n0 + (3 + j))
                    for t in range(KEYT):
                        if j == 0 and t < 2:
                            pe.wait_ge(banks_free, n0 + (t + 7))
                        elif j == 0 and t > 2:
                            pe.wait_ge(rope_read, h * 4 + (t - 2))
                        for kk in range(4):
                            k = 4 * j + kk
                            if t < TT:
                                st = act_hi[:, k, t * P:(t + 1) * P], act_lo[:, k, t * P:(t + 1) * P]
                            else:
                                st = ctx_hi[:, k, (t - TT) * P:(t - TT + 1) * P], ctx_lo[:, k, (t - TT) * P:(t - TT + 1) * P]
                            mm = product(bank(BANK_V[t]), st, wcols(j, kk * RV, (kk + 1) * RV), k == 0, k == KT - 1)
                    mm.then_inc(slab_done, 1)
                pe.wait_ge(roped, h * 4 + 5)
                pe.wait_ge(kctx_done, h + 1)
                for t in range(KEYT):
                    if t >= 2:
                        pe.wait_ge(v_done, h * 6 + (t - 1))
                    for d in range(RDT):
                        mm = pe.matmul(bank(BANK_S[t]), rk[:, d, t * P:(t + 1) * P], rq[:, d, :],
                                       start=(d == 0), stop=(d == RDT - 1))
                    mm.then_inc(s_ready, 1)
                pe.wait_ge(v_done, h * 6 + 6)
                for e in range(RVT):
                    for t in range(KEYT):
                        if e == 0:
                            pe.wait_ge(s_decayed, h * 6 + (t + 1))
                        mm = pe.matmul(bank(BANK_O[e]), rv[:, t, e * P:(e + 1) * P], rs[:, t, :],
                                       start=(t == 0), stop=(t == KEYT - 1))
                    mm.then_inc(pv_ready, 1)
                for j in range(2):
                    pe.wait_ge(w_lo_done, n0 + (5 + j))
                    for m in range(2):
                        if j and m:
                            pe.wait_ge(ostd_ready, h + 1)
                        mm = out_tile(j, m, bank(BANK_G[2 * j + m]), act)
                    mm.then_inc(slab_done, 1)
                    for e in range(0 if j else RVT):
                        pe.wait_ge(osq_ready, h * 4 + (e + 1))
                        mm = pe.matmul(bank(7), ones[:, :], rs[:, e, :], start=(e == 0), stop=(e == RVT - 1))
                    if j == 0:
                        mm.then_inc(osum_ready, 1)
                pe.wait_ge(g_done, h * 4 + 2)
                pe.wait_ge(acc_ready, h + 1)
                for m in range(KT):
                    mm = pe.matmul(PS[:, 5, m:m + 1], acc[:, m * P:(m + 1) * P], ones[:, 0:1], start=True, stop=True)
                mm.then_inc(unit_summed, 1)
                pe.wait_ge(w_lo_done, n0 + 7)
                for kk in range(2):
                    pe.wait_ge(ry_lo_done, h * 4 + (kk + 1))
                    for m in (1, 2, 3, 4, 6, 0, 7, 5):
                        if kk == 0 and m == 1:
                            pe.wait_ge(o_scaled, h * 4 + 4)
                        if kk == 0 and m == 0:
                            pe.wait_ge(g_done, h * 4 + 4)
                        if kk == 0 and m == 5:
                            pe.wait_ge(unit_done, h + 1)
                        mm = product(bank(m), wcols(0, kk * D + m * P, kk * D + (m + 1) * P),
                                     (ry_hi[:, kk, :], ry_lo[:, kk, :]), kk == 0, False)
                mm.then_inc(slab_done, 1)
                pe.wait_ge(w_lo_done, n0 + 8)
                pe.wait_ge(ry_lo_done, h * 4 + 4)
                for s, m in enumerate(FIN):
                    for kk in range(2):
                        mm = product(bank(m), wcols(1, kk * D + m * P, kk * D + (m + 1) * P),
                                     (ry_hi[:, 2 + kk, :], ry_lo[:, 2 + kk, :]), False, kk == 1)
                    mm.then_inc(head_summed if s < KT - 1 else slab_done, 1)

            def up(n, tiles, seen, parts, units=0):
                with pe.Fori(0, tiles // 2) as i:
                    for j in range(2):
                        pe.wait_ge(w_lo_done, i * 2 + (n + j + 1))
                        if j == 0:
                            pe.wait_ge(act_silu, i * 2 + (seen + 2))
                            mm = tile_pair(n, 0, act, lo_ready, parts)
                        for m in range(2 if j else 0):
                            pe.wait_ge(hraw_ready, i * 2 + (seen + m + 1))
                            mm = out_tile(n + j, m, bank(2 * j + m), act)
                        mm.then_inc(slab_done, 1)
                    if units:
                        pe.wait_ge(acc_ready, i + (units + 1))
                        for m in range(KT):
                            mm = pe.matmul(PS[:, 4, m:m + 1], acc[:, m * P:(m + 1) * P], ones[:, 0:1],
                                           start=True, stop=True)
                        mm.then_inc(unit_summed, 1)

            def down(n, tiles, h_hi, h_lo, lo_done, seen, banks, banks_seen, norm=None, unit4=False):
                def part(t):
                    return tuple(h[:, bass.ds(t, 1), :].rearrange("p o t -> p (o t)") for h in (h_hi, h_lo))

                def slab(i, j, first=False):
                    pe.wait_ge(w_lo_done, i * 2 + (n + j + 1))
                    for kk in range(2):
                        for b in (5, 6, 7, 0, 1, 2, 3, 4):
                            if first and kk == 0 and b == 0:
                                pe.wait_ge(banks, banks_seen)
                            if first and kk == 0 and b == 4 and unit4:
                                pe.wait_ge(unit_done, 10)
                            mm = product(bank(b), wcols(n + j, kk * D + b * P, kk * D + (b + 1) * P),
                                         part(i * 4 + (2 * j + kk)), first and kk == 0, False)
                    mm.then_inc(slab_done, 1)

                pe.wait_ge(lo_done, seen)
                slab(0, 0, True)
                slab(0, 1)
                full, rest = divmod(tiles // 2, 2)
                last = full if rest else full - 1
                with pe.Fori(1, last) as i:
                    for j in range(2):
                        slab(i, j)
                if not rest:
                    slab(last, 0)
                j = 1 - rest
                pe.wait_ge(lo_done, seen + 2)
                pe.wait_ge(w_lo_done, n + tiles // 2)
                for s, b in enumerate(FIN):
                    for kk in range(2):
                        mm = product(bank(b), wcols(n + j, kk * D + b * P, kk * D + (b + 1) * P),
                                     part(tiles - 2 + kk), False, kk == 1)
                    mm.then_inc(tile_summed if s < KT - 1 else slab_done, 1)
                if norm:
                    gathered_sum(nth(norm))

            def swiglu(n, seen, added, units, parts, norm):
                for c, tiles in enumerate(FCH):
                    if c:
                        pe.wait_ge(down_added, added + 5)
                    up(n, tiles, seen, parts, units if c == 0 else 0)
                    n += tiles
                    seen += tiles
                    if c:
                        pe.wait_ge(down_added, added + 8)
                    down(n, tiles, hid_hi, hid_lo, hid_lo_done, seen, hraw_ready, seen + 2, norm if c else None,
                         c == 0 and units > 0)
                    n += tiles // 2

            hid = lambda t: (hid_hi[:, t, :], hid_lo[:, t, :])

            def two_turns(n, moving, free):
                with pe.Fori(0, 2) as i:
                    for j in range(2):
                        pe.wait_ge(w_lo_done, i * 2 + (n + j + 1))
                        for m in range(2):
                            pe.wait_ge(free, i * 4 + (2 * j + m + 1))
                            mm = out_tile(n + j, m, bank(2 * j + m), moving)
                        mm.then_inc(slab_done, 1)

            def finish_two_turns(n, moving, ready, before, free, norm):
                for j in range(4):
                    pe.wait_ge(w_lo_done, n + j + 1)
                    pe.wait_ge(free, 2 * j + 2)
                    tile_pair(n + j, 2 * (j % 2), moving, ready, before).then_inc(slab_done, 1)
                if norm:
                    gathered_sum(nth(norm))

            parts_of = lambda name: 8 * nth_split(name)
            pe.wait_ge(banks_free, 8 * (RH + 1))
            norm_sum(nth("ffn0"))
            swiglu(FFN0, 0, 0, RH, parts_of("ffn0"), "mix1")
            up(CONV, KT, FT, parts_of("mix1"))
            pe.wait_ge(act_silu, 2 + FT + KT)
            two_turns(CONV + 8, act, conv_y)
            finish_two_turns(CONV + 12, hid, hid_lo_done, FT + 2, wout_added, "ffn1")
            swiglu(FFN1, FT + KT, 16, 0, parts_of("ffn1"), "final")

            norm_sum(nth("pre2"))
            n = MIX
            with pe.Fori(0, 3) as i:
                for j in range(2):
                    pe.wait_ge(w_lo_done, i * 2 + (n + j + 1))
                    if j == 0:
                        pe.wait_ge(cvin_done, i * 4 + 2)
                        mm = tile_pair(n, 0, act, lo_ready, parts_of("pre2"))
                    for m in range(2 if j else 0):
                        pe.wait_ge(cvin_done, i * 4 + (2 * j + m + 1))
                        mm = out_tile(n + j, m, bank(2 * j + m), act)
                    mm.then_inc(slab_done, 1)
            for j in range(2):
                pe.wait_ge(w_lo_done, n + 7 + j)
                for m in range(2):
                    pe.wait_ge(cvin_done, 12 + 2 * j + m + 1)
                    mm = out_tile(n + 6 + j, m, bank(2 * j + m), act)
                mm.then_inc(slab_done, 1)
            pe.wait_ge(w_lo_done, n + 9)
            for m in range(2):
                mm = out_tile(n + 8, m, bank(4 + m), act)
            mm.then_inc(slab_done, 1)
            pe.wait_ge(w_lo_done, n + 10)
            for m in range(2):
                out_tile(n + 9, m, bank(6 + m), act)
            pe.wait_ge(gate2_done, 1)
            for t in range(TT):
                for k in range(KT):
                    mm = product(PS[:, 0, t * 8:t * 8 + 8], (act_hi[:, k, t * P:(t + 1) * P], act_lo[:, k, t * P:(t + 1) * P]),
                                 wcols(n + 9, k * 256 + P, k * 256 + P + 8), k == 0, k == KT - 1)
            mm.then_inc(slab_done, 1)
            pe.wait_ge(gate2_done, 4)
            for k in range(3):
                pe.wait_ge(msq_ready, k + 1)
                mm = pe.matmul(bank(2 if k < 2 else 3), ones[:, :], MSQ[k], start=(k != 1), stop=(k != 0))
                if k:
                    mm.then_inc(msum_ready, 1)
            pe.wait_ge(gate2_done, 2)
            for t in range(2 * GH):
                pe.wait_ge(qsq_ready, t + 1)
                for c in range(TT):
                    at = c * 2 * GH + t
                    mm = pe.matmul(PS[:, 1, at:at + 1], sq[:, t % 2, c * P:(c + 1) * P], ones[:, 0:1], start=True, stop=True)
                mm.then_inc(qsq_used, 1)
            pe.wait_ge(mc_lo_done, 3)
            mc = lambda k: (mc_hi[:, k, :], mc_lo[:, k, :])
            pe.wait_ge(w_lo_done, n + 12)
            pe.wait_ge(mstd_done, 2)
            BANK_MV = (3, 4, 5, 6)
            for t in range(TT):
                mm = product(bank(BANK_MV[t]), (mc_hi[:, 2, t * P:(t + 1) * P], mc_lo[:, 2, t * P:(t + 1) * P]),
                             wcols(n + 11, MH * NOPE, MH * (NOPE + MV)), True, True)
                mm.then_inc(mv_ready, 1)

            def project(h):
                if h == 0:
                    pe.wait_ge(ab_done, 1)
                    pe.wait_ge(ssd_done, 1)
                else:
                    pe.wait_ge(qn_done, h)
                    pe.wait_ge(qr_done, h)
                if h >= 2:
                    pe.wait_ge(prt_done, 4 * (h - 2) + 3)
                if h % 2 == 0:
                    if h:
                        pe.wait_ge(kn_done, h)
                    product(bank(1), wcols(n + 11, h * NOPE, (h + 2) * NOPE), mc(2), True, True)
                for k in range(2):
                    mm = product(bank(0), wcols(n + 10, k * D + h * P, k * D + (h + 1) * P), mc(k), k == 0, k == 1)
                mm.then_inc(q_ready, 1)

            def attend(h):
                pe.wait_ge(qn_done, h + 1)
                pe.wait_ge(qr_done, h + 1)
                pe.wait_ge(kn_done, h + 1)
                if h == 0:
                    pe.wait_ge(kr_copied, 2)
                    pe.wait_ge(mv_done, 4)
                for t in range(TT):
                    if h:
                        pe.wait_ge(exp_done, 4 * (h - 1) + t + 1)
                    w = (t + 1) * P
                    pe.matmul(PS[:, 2 + t, 0:w], qh[0:QK, h % 2, t * P:w], kh[0:QK, h % 2, 0:w], start=True, stop=False,
                              skip_group_check=True)
                    pe.matmul(PS[:, 2 + t, t * P:w], cc("mask_q"), cc("mask_k"), start=False, stop=True,
                              skip_group_check=True).then_inc(ms_ready, 1)

            project(0)
            pe.wait_ge(cols_done, 1)
            for c in range(TT):
                mm = pe.matmul(PS[:, 2, c * GH:(c + 1) * GH], cc("upper"), rowsrc[:, c, 0:GH], start=True, stop=True)
            mm.then_inc(gcum_ready, 1)
            pe.wait_ge(cols_done, 2)
            attend(0)

            def transposed(h):
                for t in range(TT):
                    pe.wait_ge(p_ready, 4 * h + t + 1)
                    if t >= 2:
                        pe.wait_ge(prt_done, 4 * h + t - 1)
                    elif t and h:
                        pe.wait_ge(prt_done, 4 * h)
                    for kt in range(t + 1):
                        mm = pe.transpose(PS[:, BANK_T[t], kt * P:(kt + 1) * P], pr[t][:, kt * P:(kt + 1) * P], cc("ident"))
                    mm.then_inc(t_ready, 1)

            def weighted(h):
                pe.wait_ge(prt_done, 4 * h + 4)
                if h == 0:
                    pe.wait_ge(krope_done, 1)
                elif h % 2 == 0:
                    pe.wait_ge(mo_lo_done, h // 2)
                r0 = MV * (h % 2)
                for kt in range(TT):
                    mm = pe.matmul(PS[r0:r0 + MV, 7, kt * P:T], mv[:, kt, h * MV:(h + 1) * MV], prt[:, kt, kt * P:T],
                                   start=(kt == 0), stop=(kt == TT - 1), skip_group_check=True)
                mm.then_inc(o2_ready, 1)

            for h in range(MH + 1):
                if h:
                    transposed(h - 1)
                if h + 1 < MH:
                    project(h + 1)
                if h:
                    weighted(h - 1)
                if h + 1 < MH:
                    attend(h + 1)
            pe.sem_inc(slab_done, 2)

            def rows(c):
                pe.wait_ge(bcs_done, c + 1)
                if c:
                    pe.wait_ge(rows_used, c)
                    pe.wait_ge(kd_exp, 3 * c)
                for h in range(GH):
                    pe.matmul(PS[:, 0, hs(h)], bcs[:, h, :], cc("upper"), start=True, stop=True)
                    pe.matmul(PS[:, 1, hs(h)], bcs[:, GH + h, :], cc("ident"), start=True, stop=True)
                    mm = pe.matmul(PS[:, 2, hs(h)], bcs[:, 2 * GH + h, :], cc("ident"), start=True, stop=True)
                mm.then_inc(rows_ready, 1)

            def key_products(c):
                if c:
                    pe.wait_ge(mt_done, GH * c)
                    pe.wait_ge(ptm_done, GH * c)
                for h in range(GH):
                    pe.matmul(PS[:, 3, hs(h)], k_at(h, c), k_at(h, c), start=True, stop=True)
                    pe.matmul(PS[:, 4, hs(h)], k_at(h, c), q_at(h, c), start=True, stop=True)
                if c:
                    pe.wait_ge(kvt_done, 3 * GH * c)
                for h in range(GH):
                    pe.transpose(PS[:, 5, hs(h)], k_at(h, c), cc("ident"))
                    mm = pe.transpose(PS[:, 6, hs(h)], v_at(h, c), cc("ident"))
                mm.then_inc(kq_ready, 1)

            pe.wait_ge(mo_lo_done, 4)
            pe.wait_ge(prt_done, 4 * MH)
            pe.wait_ge(exp_done, 4 * MH)
            key_products(0)
            rows(0)
            for c in range(1, TT):
                rows(c)
                key_products(c)
            for c in range(TT):
                pe.wait_ge(y0_done, c + 1)
                if c == 0:
                    pe.wait_ge(kvt_done, 3 * GH * TT)
                if c >= 2:
                    pe.wait_ge(x0_done, c - 1)
                for h in range(GH):
                    mm = pe.transpose(PS[:, 6 + c % 2, hs(h)], gy[:, c, hs(h)], cc("ident"))
                mm.then_inc(x0_ready, 1)

            def level_first(g):
                c = g % TT
                pe.wait_ge(lv_done, g + 1)
                if g < TT:
                    pe.wait_ge(x0_done, c + 1)
                else:
                    pe.wait_ge(xy_done, 2 * (g - TT + 1))
                if g >= 2:
                    pe.wait_ge(lp_done, g - 1)
                for h in range(GH):
                    mm = pe.matmul(PS[:, g % 2, hs(h)], lv[:, g % 2, hs(h)], gx[:, c, hs(h)], start=True, stop=True)
                mm.then_inc(lp_ready, 1)

            def level_second(g):
                c = g % TT
                pe.wait_ge(lp_done, g + 1)
                if g >= 2:
                    pe.wait_ge(xy_done, 2 * (g - 1))
                for h in range(GH):
                    pe.matmul(PS[:, 2 + g % 2, hs(h)], gy[:, c, hs(h)], gp[:, c, hs(h)], start=True, stop=True)
                    mm = pe.matmul(PS[:, 4 + g % 2, hs(h)], gp[:, c, hs(h)], gy[:, c, hs(h)], start=True, stop=True)
                mm.then_inc(xx_ready, 1)

            G = (LEVELS - 1) * TT
            for g in range(G + 1):
                if g < G:
                    level_first(g)
                if g:
                    level_second(g - 1)
            for c in range(TT):
                pe.wait_ge(xy_done, 2 * (G - TT + c + 1))
                if c == 0:
                    pe.wait_ge(x0_done, TT)
                else:
                    pe.wait_ge(u_done, c)
                    pe.wait_ge(wt_done, c)
                for h in range(GH):
                    pe.matmul(PS[:, 6, hs(h)], gy[:, c, hs(h)], v_at(h, c), start=True, stop=True)
                    mm = pe.matmul(PS[:, 7, hs(h)], kbg[:, c, hs(h)], gy[:, c, hs(h)], start=True, stop=True)
                mm.then_inc(uw_ready, 1)
            def mix_out(j, k):
                for m in range(2):
                    mm = product(bank(BANK_F[2 * j + m]), wcols(n + 12 + j, k * 256 + m * P, k * 256 + (m + 1) * P),
                                 act(k), k == 4, k == 3)
                return mm

            fill = [(j, k) for j in range(2) for k in range(4, KT)]
            pe.wait_ge(mo_lo_done, 4)
            pe.wait_ge(w_lo_done, n + 14)
            pe.wait_ge(xy_done, 2 * G)
            pe.wait_ge(u_done, TT)
            pe.wait_ge(wt_done, TT)
            for c in range(TT):
                if c:
                    pe.wait_ge(state_done, GH * c)
                    pe.wait_ge(vn_done, c)
                    for h in range(GH):
                        mm = pe.matmul(PS[:, 0, hs(h)], gp[:, c, hs(h)], state[:, h, :], start=True, stop=True)
                    mm.then_inc(ws_ready, 1)
                    pe.wait_ge(o3_done, c)
                    mix_out(*fill.pop(0))
                pe.wait_ge(vn_done, c + 1)
                if c + 1 < TT:
                    for h in range(GH):
                        mm = pe.matmul(PS[:, 2, hs(h)], k_at(h, c), gx[:, c, hs(h)], start=True, stop=True)
                    mm.then_inc(sup_ready, 1)
                for h in range(GH):
                    if c:
                        pe.matmul(PS[:, 1, hs(h)], state[:, h, :], q_at(h, c), start=True, stop=False)
                    mm = pe.matmul(PS[:, 1, hs(h)], gx[:, c, hs(h)], ptm[:, c, hs(h)], start=(c == 0), stop=True)
                mm.then_inc(o3_ready, 1)
                mix_out(*fill.pop(0))
                pe.wait_ge(gsq_ready, c + 1)
                if c:
                    pe.wait_ge(gstd_done, c)
                pe.matmul(bank(3), ones[:, :], sq[:, c % 2, :], start=True, stop=True).then_inc(gss_ready, 1)
            while fill:
                mix_out(*fill.pop(0))
            pe.wait_ge(go_lo_done, TT)
            for j in range(4):
                pe.wait_ge(w_lo_done, n + 12 + j + 1)
                if j == 3:
                    pe.wait_ge(f_free, 2)
                for k in (0, 1, 2, 3) if j < 2 else (4, 5, 6, 7, 0, 1, 2, 3):
                    mm = mix_out(j, k)
                mm.then_inc(slab_done, 1)
            gathered_sum(nth("post2"), 3)

            norm_sum(nth("ffn2"))
            n = FFN2
            seen = 0
            for c, tiles in enumerate(F2CH):
                if c:
                    pe.wait_ge(f2_copied, 5)
                with pe.Fori(0, tiles // 4) as i:
                    for j in range(2):
                        pe.wait_ge(w_lo_done, i * 2 + (n + j + 1))
                        if j == 0:
                            pe.wait_ge(relu_done, i * 4 + (seen + 2))
                            mm = tile_pair(n, 0, act, lo_ready, parts_of("ffn2"))
                        for m in range(2 if j else 0):
                            pe.wait_ge(relu_done, i * 4 + (seen + 2 * j + m + 1))
                            mm = out_tile(n + j, m, bank(2 * j + m), act)
                        mm.then_inc(slab_done, 1)
                n += tiles // 2
                seen += tiles
                if c:
                    pe.wait_ge(f2_copied, KT)
                down(n, tiles, hid2_hi, hid2_lo, h2_lo_done, seen, relu_done, seen + 4, "last" if c else None)
                n += tiles // 2

        @block.scalar
        def _(act):
            act.dma_start(vec[:, :], vecs).then_inc(vec_landed, 16)
            act.dma_start(x[:, :, :], x_in).then_inc(x_landed, 16)
            act.dma_start(xc, ctx_in).then_inc(xc_landed, 16)

            def round_slab(n, i=0, step=2):
                act.wait_ge(slab_landed[n % 2], i * (step * 8) + 16 * (n // 2 + 1))
                act.activation(w_hi[:, n % 2, :], raw[:, n % 2, :], ACT.Copy).then_inc(w_hi_done, 1)

            def after(n, i=0, step=2):
                act.wait_ge(slab_done, i * step + (n + 1))
                round_slab(n + 2, i, step)

            def square(q, k, src, width=T):
                if norms[q] in gathered:
                    act.wait_ge(sq_used, 8 * q + max(k - 2, 0))
                elif 8 * q + k >= 2:
                    act.wait_ge(sq_used, 8 * q + k - 1)
                first = norms[q] in gathered and k == 0
                act.activation(std[:, :] if first else sq[:, k % 2, 0:width], src, ACT.Square).then_inc(sq_ready, 1)

            def squares(q, src, width=T, order=range(KT), made=None, before=0):
                for k, b in enumerate(order):
                    if made is not None:
                        act.wait_ge(made, before + k + 1)
                    square(q, k, src(b), width)

            def root(q, width, features, b=7, dst=std):
                act.wait_ge(sq_used, 8 * q + 8)
                act.activation(dst[:, 0:width], PS[:, b, 0:width], ACT.Sqrt, bias=eps[:, 0:1],
                               scale=1.0 / features).then_inc(std_ready, 1)

            def shifted(q, shift, dst, width):
                for k in range(KT):
                    act.wait_ge(y_ready, 8 * q + k + 1)
                    act.activation(dst(k), normed[:, k % 2, 0:width], ACT.Identity, bias=shift(k)).then_inc(hi_ready, 1)

            act.sem_inc(act_silu, 2)
            act.sem_inc(hid_hi_done, 2)
            act.wait_ge(vec_landed, 16)
            for j, name in enumerate(("c", "c_ctx")):
                act.activation(silu_c[:, :, j], vec[:, VEC[name]:VEC[name] + KT], ACT.Silu).then_inc(silu_c_done, 1)
            act.wait_ge(consts_set, 2)
            act.wait_ge(x_landed, 16)
            squares(0, lambda k: x[:, k, :])
            root(0, T, D)
            act.wait_ge(xc_landed, 16)
            squares(1, lambda k: xc[:, k, :], C)
            root(1, C, D, 6, std_c)
            act.dma_start(rope[:, :], rope1).then_inc(rope_landed, 16)
            act.dma_start(toep[:, :], decay[0]).then_inc(toep_landed, 16)
            round_slab(0)
            round_slab(1)
            act.wait_ge(gain_done, 3)
            shifted(0, lambda k: mod[:, k:k + 1], lambda k: act_hi[:, k, :], T)
            shifted(1, lambda k: mod_ctx[:, k:k + 1], lambda k: ctx_hi[:, k, :], C)

            with act.Fori(0, RH) as h:
                after(0, h, 8)
                after(1, h, 8)
                act.activation(rk[:, :, T:T + C], PS[:, 4, :].rearrange("p (m t) -> p m t", m=RDT),
                               ACT.Copy).then_inc(kctx_done, 1)
                after(2, h, 8)
                after(3, h, 8)
                for t in range(KEYT):
                    act.activation(rv[:, t, :], bank(BANK_V[t]), ACT.Copy).then_inc(v_done, 1)
                act.wait_ge(s_decayed, h * 6 + 6)
                act.dma_start(toep[:, :], decay[bass.ds(h + 1, 1)].rearrange("o p n -> p (o n)")).then_inc(toep_landed, 16)
                act.wait_ge(pv_ready, h * 4 + 4)
                for e in range(RVT):
                    act.activation(rs[:, e, :], bank(BANK_O[e]), ACT.Square).then_inc(osq_ready, 1)
                for j in range(2):
                    after(4 + j, h, 8)
                    for m in range(2):
                        act.activation(rg[:, 2 * j + m, :], bank(BANK_G[2 * j + m]), ACT.Silu).then_inc(g_done, 1)
                    if j == 0:
                        act.wait_ge(osum_ready, h + 1)
                        act.activation(std[:, :], bank(7), ACT.Sqrt, bias=eps[:, 0:1], scale=1.0 / RV).then_inc(ostd_ready, 1)
                    for e in range(2 * j, 2 * j + 2):
                        act.wait_ge(ry_ready, h * 4 + (e + 1))
                        act.activation(ry_hi[:, e, :], rs[:, e, :], ACT.Copy).then_inc(ry_hi_done, 1)
                after(6, h, 8)
                after(7, h, 8)

            act.wait_ge(toep_landed, 16 * (RH + 1))

            def after_static(n):
                act.wait_ge(slab_done, n + 1)
                if n + 2 < N_SLABS:
                    round_slab(n + 2)

            def up(n, tiles, seen, func=ACT.Silu):
                with act.Fori(0, tiles // 2) as i:
                    after(n, i)
                    for m in range(2):
                        act.wait_ge(hraw_ready, i * 2 + (seen + m + 1))
                        act.activation(sg[:, m, :], bank(m), func).then_inc(act_silu, 1)
                    after(n + 1, i)
                    for m in range(0 if func == ACT.Copy else 2):
                        act.wait_ge(hraw_ready, i * 2 + (seen + m + 3))
                        act.activation(hid_hi[:, bass.ds(i * 2 + m, 1), :].rearrange("p o t -> p (o t)"),
                                       hraw[:, m, :], ACT.Copy).then_inc(hid_hi_done, 1)

            def down(n, tiles):
                full, rest = divmod(tiles // 2, 2)
                with act.Fori(0, full - 1) as i:
                    after(n, i)
                    after(n + 1, i)
                for j in range(1 + rest):
                    after_static(n + 2 * full - 2 + j)

            def swiglu(n, seen):
                for c, tiles in enumerate(FCH):
                    up(n, tiles, seen)
                    n += tiles
                    seen += tiles
                    down(n, tiles)
                    n += tiles // 2
                    if c == 0:
                        after_static(n - 1)

            def norm(name, shift, last_slab, order=range(KT), made=None, before=0):
                squares(nth(name), lambda k: x[:, k, :], T, order, made, before)
                root(nth(name), T, D)
                if last_slab is not None:
                    after_static(last_slab)
                shifted(nth_split(name), lambda k: mod[:, shift + k:shift + k + 1], lambda k: act_hi[:, k, :], T)

            norm("ffn0", mod_at(0, 3), None, FIN, banks_free, 8 * RH)
            swiglu(FFN0, 0)
            norm("mix1", mod_at(1, 0), CONV - 1, FIN, down_added, 8)
            up(CONV, KT, FT, ACT.Copy)
            with act.Fori(0, 2) as i:
                for j in range(2):
                    after(CONV + 8 + j, i)
                    for m in range(2):
                        act.wait_ge(conv_y, i * 4 + (2 * j + m + 5))
                        act.activation(hid_hi[:, bass.ds(i * 4 + (2 * j + m), 1), :].rearrange("p o t -> p (o t)"),
                                       hraw[:, m, :], ACT.Copy).then_inc(hid_hi_done, 1)
            for j in range(4):
                if j < 3:
                    after_static(CONV + 12 + j)
                for k in range(2 * j, 2 * j + 2):
                    act.wait_ge(wout_added, 4 + k + 1)
                    square(nth("ffn1"), k, x[:, k, :])
            root(nth("ffn1"), T, D)
            after_static(FFN1 - 1)
            shifted(nth_split("ffn1"), lambda k: mod[:, mod_at(1, 3) + k:mod_at(1, 3) + k + 1],
                    lambda k: act_hi[:, k, :], T)
            swiglu(FFN1, FT + KT)

            def norm2(name, src, dst, order=range(KT), made=None, before=0):
                squares(nth(name), src, T, order, made, before)
                root(nth(name), T, D)
                if dst is not None:
                    q = nth_split(name)
                    for k in range(KT):
                        act.wait_ge(y_ready, 8 * q + k + 1)
                        act.activation(dst(k), normed[:, k % 2, :], ACT.Copy).then_inc(hi_ready, 1)

            x_tile = lambda k: x[:, k, :]
            squares(nth("final"), x_tile, T, FIN, down_added, 24)
            root(nth("final"), T, D)
            act.wait_ge(slab_done, MIX)
            act.dma_start(con[:, :], consts).then_inc(con_landed, 16)
            act.dma_start(heads_c[:, :], per_head).then_inc(heads_landed, 16)
            act.dma_start(pos_i, positions).then_inc(pos_landed, 16)
            after_static(MIX - 1)
            norm2("pre2", x_tile, lambda k: act_hi[:, k, :], range(KT), final_done)
            act.wait_ge(trig_ready, 1)
            act.activation(csn[64:128, :], cv[64:128, 3, :], ACT.Sin).then_inc(trig_done, 1)
            n = MIX
            with act.Fori(0, 3) as i:
                for j in range(2):
                    after(n + j, i)
                    for m in range(2):
                        c = 2 * j + m
                        act.wait_ge(conv2_done, i * 4 + (c + 1))
                        act.activation(cvin[:, c, 3:T + 3], bank(c), ACT.Copy).then_inc(cvin_done, 1)
                for c in range(4):
                    act.wait_ge(conv2_done, i * 4 + (c + 5))
                    act.activation(qkv[:, bass.ds(i * 4 + c, 1), :].rearrange("p o t -> p (o t)"), cv[:, c, :],
                                   ACT.Silu).then_inc(silu2_done, 1)
            for j in range(2):
                after_static(n + 6 + j)
                for m in range(2):
                    act.activation(gate[:, 2 * j + m, :], bank(2 * j + m), ACT.Silu).then_inc(gate2_done, 1)
            after_static(n + 8)
            for m in range(2):
                act.activation(cqr[:, m, :], bank(4 + m), ACT.Copy).then_inc(cqr_done, 1)
            act.wait_ge(cqr_done, 2)
            for k in range(2):
                act.activation(MSQ[k], cqr[:, k, :], ACT.Square).then_inc(msq_ready, 1)
            after_static(n + 9)
            act.activation(cqr[:, 2, :], bank(6), ACT.Copy).then_inc(cqr_done, 1)
            act.wait_ge(cqr_done, 3)
            act.activation(MSQ[2], cqr[:, 2, :], ACT.Square).then_inc(msq_ready, 1)
            for k in range(2):
                act.wait_ge(msum_ready, k + 1)
                act.activation(mstd[:, k, :], bank(2 + k), ACT.Sqrt, bias=eps[:, 0:1],
                               scale=1.0 / (2 * P if k == 0 else P)).then_inc(mstd_done, 1)
            act.wait_ge(silu2_done, NCONV + 4)
            for t in range(2 * GH):
                if t >= 2:
                    act.wait_ge(qsq_used, t - 1)
                act.activation(sq[:, t % 2, :], qkv[:, t, :], ACT.Square).then_inc(qsq_ready, 1)
                if t in (3, 4, 5):
                    act.wait_ge(mc_ready, t - 2)
                    act.activation(mc_hi[:, t - 3, :], cqr[:, t - 3, :], ACT.Copy).then_inc(mc_hi_done, 1)
            act.wait_ge(soft1, 1)
            act.activation(cols[:, TMP, :, :], cols[:, TMP, :, :], ACT.Exp).then_inc(soft2, 1)
            act.wait_ge(soft2, 1)
            act.activation(cols[:, EG, :, :], cols[:, TMP, :, :], ACT.Ln, bias=1.0).then_inc(soft2, 1)
            act.wait_ge(heads_landed, 16)
            act.activation(small[:, 0, :], heads_c[:, 0:GH], ACT.Exp).then_inc(soft2, 1)
            act.activation(cols[:, BETA, :, :], ab[:, :, GH:2 * GH], ACT.Exp, scale=-1.0).then_inc(beta1, 1)
            act.wait_ge(qsq_used, 2 * GH)
            act.activation(ssqk[:, :, :], PS[:, 1, 0:TT * 2 * GH].rearrange("p (c t) -> p c t", c=TT), ACT.Sqrt,
                           bias=eps[:, 0:1]).then_inc(ssd_done, 1)
            for t in range(TT):
                act.wait_ge(mv_ready, t + 1)
                act.activation(mv[:, t, :], bank((3, 4, 5, 6)[t]), ACT.Copy).then_inc(mv_done, 1)
            act.wait_ge(krope_done, 1)
            for b in range(2):
                act.activation(kh[64:96, b, :], krope[64:96, :], ACT.Copy).then_inc(kr_copied, 1)

            def head_parts(h):
                act.wait_ge(q_ready, h + 1)
                if h >= 2:
                    act.wait_ge(ms_ready, 4 * (h - 1))
                act.activation(qh[0:NOPE, h % 2, :], PS[0:NOPE, 0, :], ACT.Copy).then_inc(qn_done, 1)
                if h % 2 == 0:
                    if h:
                        act.wait_ge(ms_ready, 4 * h)
                    for b in range(2):
                        act.activation(kh[0:NOPE, b, :], PS[b * NOPE:(b + 1) * NOPE, 1, :], ACT.Copy).then_inc(kn_done, 1)

            def exps(h, t):
                g = 4 * h + t
                act.wait_ge(nmx_done, g + 1)
                if h:
                    act.wait_ge(t_ready, g - 3)
                act.activation(pr[t][:, 0:(t + 1) * P], PS[:, 2 + t, 0:(t + 1) * P], ACT.Exp, bias=small[:, 1, t:t + 1],
                               scale=QK ** -0.5, accum_out=small[:, 2, t:t + 1]).then_inc(exp_done, 1)

            def turned(h, t):
                act.wait_ge(t_ready, 4 * h + t + 1)
                if h and t == 0:
                    act.wait_ge(o2_ready, h)
                act.activation(prt[:, 0:t + 1, t * P:(t + 1) * P],
                               PS[:, BANK_T[t], 0:(t + 1) * P].rearrange("p (k q) -> p k q", q=P), ACT.Copy).then_inc(prt_done, 1)

            head_parts(0)
            act.wait_ge(cols_done, 2)
            act.activation(cols[:, EG, :, :], cols[:, GCOL, :, :], ACT.Exp).then_inc(soft2, 1)
            for h in range(MH + 1):
                for t in range(TT + 1):
                    if h and t < TT:
                        turned(h - 1, t)
                    if t == TT and h + 1 < MH:
                        head_parts(h + 1)
                    if t and h < MH:
                        exps(h, t - 1)
                if h and h % 2 == 0:
                    act.wait_ge(o2_ready, h)
                    act.activation(act_hi[:, 3 + h // 2, :], bank(7), ACT.Copy).then_inc(mo_hi_done, 1)

            for c in range(TT):
                act.wait_ge(kd_raw, c + 1)
                act.activation(cols[:, KDS, c, :], cols[:, KD, c, :], ACT.Exp).then_inc(kd_exp, 1)
                act.activation(cols[:, EGL, c, :], cols[:, GL, c, :], ACT.Exp).then_inc(kd_exp, 1)
                act.wait_ge(eraw_done, GH * (c + 1))
                act.activation(ex[:, :], ex[:, :], ACT.Exp).then_inc(e_done, 1)
                if c:
                    act.wait_ge(qdec_done, c)
                act.activation(egrow[:, :], bank(0), ACT.Exp).then_inc(kd_exp, 1)
                act.wait_ge(kq_ready, c + 1)
                act.wait_ge(kd_done, c + 1)
                for h in range(GH):
                    act.activation(kbg[:, c, hs(h)], PS[:, 5, hs(h)], ACT.Copy, scale=col(KBS, c, h)).then_inc(kvt_done, 1)
                    act.activation(k_at(h, c), PS[:, 5, hs(h)], ACT.Copy, scale=col(KDS, c, h)).then_inc(kvt_done, 1)
                    act.activation(v_at(h, c), PS[:, 6, hs(h)], ACT.Copy, scale=col(BETA, c, h)).then_inc(kvt_done, 1)
            for c in range(TT):
                act.wait_ge(x0_ready, c + 1)
                act.activation(gx[:, c, :], bank(6 + c % 2), ACT.Copy).then_inc(x0_done, 1)
            for g in range((LEVELS - 1) * TT):
                if g in (2, 6):
                    after_static(n + 10 + g // 4)
                act.wait_ge(lp_ready, g + 1)
                if g >= TT:
                    act.wait_ge(xx_ready, g - TT + 1)
                act.activation(gp[:, g % TT, :], bank(g % 2), ACT.Copy).then_inc(lp_done, 1)
            for c in range(TT):
                act.wait_ge(uw_ready, c + 1)
                act.activation(gx[:, c, :], bank(6), ACT.Copy).then_inc(u_done, 1)
            def out_hi(c):
                act.wait_ge(go_ready, c + 1)
                act.activation(act_hi[:, 0:GH, c * P:(c + 1) * P], oT[:, :, c * P:(c + 1) * P], ACT.Copy).then_inc(go_hi_done, 1)

            for c in range(TT):
                act.wait_ge(o3_ready, c + 1)
                if c >= 2:
                    act.wait_ge(gss_ready, c - 1)
                act.activation(sq[:, c % 2, :], bank(1), ACT.Square).then_inc(gsq_ready, 1)
                act.activation(oT[:, :, c * P:(c + 1) * P], hb(bank(1)), ACT.Copy).then_inc(o3_done, 1)
                if c >= 2:
                    out_hi(c - 2)
                act.wait_ge(gss_ready, c + 1)
                act.activation(gstd[:, c, :], bank(3), ACT.Sqrt, bias=eps[:, 0:1], scale=1.0 / P).then_inc(gstd_done, 1)
            out_hi(TT - 2)
            out_hi(TT - 1)
            for j in range(4):
                if j < 3:
                    after_static(n + 12 + j)
                else:
                    act.wait_ge(slab_done, n + 16)
                for k in range(2 * j, 2 * j + 2):
                    act.activation(facc[:, k, :], bank(BANK_F[k]), ACT.Copy).then_inc(f_free, 1)
                for k in range(2 * j, 2 * j + 2):
                    act.wait_ge(f_free, k + 1)
                    square(nth("post2"), k, facc[:, k, :])
            root(nth("post2"), T, D, 3)
            after_static(n + 15)

            norm2("ffn2", x_tile, lambda k: act_hi[:, k, :], range(KT), post_done)
            n, seen = FFN2, 0
            for c, tiles in enumerate(F2CH):
                with act.Fori(0, tiles // 4) as i:
                    for j in range(2):
                        after(n + j, i)
                        for m in range(2):
                            t = 2 * j + m
                            act.wait_ge(sqr_done, i * 4 + (seen + t + 1))
                            act.activation(sg2[:, m, :], bank(t), ACT.Relu).then_inc(relu_done, 1)
                        for m in range(2):
                            t = 2 * j + m
                            act.wait_ge(sqr_done, i * 4 + (seen + t + 3))
                            act.activation(hid2_hi[:, bass.ds(i * 4 + t, 1), :].rearrange("p o t -> p (o t)"),
                                           hraw2[:, m, :], ACT.Copy).then_inc(h2_hi_done, 1)
                n += tiles // 2
                seen += tiles
                down(n, tiles)
                n += tiles // 2
                for s, b in enumerate(FIN if c == 0 else ()):
                    if s < KT - 1:
                        act.wait_ge(tile_summed, 7 * 4 + s + 1)
                    else:
                        after_static(n - 1)
                    act.activation(facc[:, b, :], bank(b), ACT.Copy).then_inc(f2_copied, 1)
            norm2("last", lambda k: facc[:, k, :], None, FIN, f_done)

        @block.vector
        def _(dve):
            links = [0]

            def link(ins):
                links[0] += 1
                ins.then_inc(vchain, 1)
                dve.wait_ge(vchain, links[0])

            dve.memset(ones[:, :], 1.0).then_inc(consts_set, 1)
            dve.memset(eps[:, :], EPS).then_inc(consts_set, 1)

            def rest_slab(n, k):
                dve.wait_ge(w_hi_done, n + 1)
                dve.tensor_tensor(w_lo[:, k % 2, :], raw[:, k % 2, :], w_hi[:, k % 2, :].bitcast(F32),
                                  ALU.subtract).then_inc(w_lo_done, 1)

            def norm_tail(name, src, g, shift, hi, lo, width, inverse=None):
                q = nth_split(name)
                if inverse is None:
                    inverse = rstd
                    dve.wait_ge(std_ready, nth(name) + 1)
                    link(dve.reciprocal(rstd[:, 0:width], std[:, 0:width]))

                def rest(k):
                    dve.wait_ge(hi_ready, 8 * q + k + 1)
                    dve.scalar_tensor_tensor(out=lo(k), in0=normed[:, k % 2, 0:width], scalar=shift(k),
                                             in1=hi(k).bitcast(F32), op0=ALU.add, op1=ALU.subtract).then_inc(lo_ready, 1)

                for k in range(KT):
                    if 8 * q + k >= 2:
                        dve.wait_ge(lo_ready, 8 * q + k - 1)
                    dve.scalar_tensor_tensor(out=normed[:, k % 2, 0:width], in0=src(k), scalar=g(k),
                                             in1=inverse[:, 0:width], op0=ALU.mult, op1=ALU.mult).then_inc(y_ready, 1)
                    if k:
                        rest(k - 1)
                rest(KT - 1)

            def gather(name, k):
                q = nth(name)
                dve.wait_ge(sq_ready, 8 * q + k + 1)
                dve.wait_ge(sq_used, 8 * q + k - 1)
                dve.tensor_tensor(std[:, :], std[:, :], sq[:, k % 2, :], ALU.add).then_inc(sq_used, 1)

            def make_gain(i, norm_col, scale):
                dve.scalar_tensor_tensor(out=gain[:, i, :], in0=scale, scalar=1.0, in1=vec[:, norm_col:norm_col + KT],
                                         op0=ALU.add, op1=ALU.mult).then_inc(gain_done, 1)

            def unit(i, parts=range(4)):
                for a in parts:
                    dve.wait_ge(ada_landed[a % 2], i * 32 + 16 * (2 + a // 2 + 1))
                    for kk in range(2):
                        k = 2 * a + kk
                        w = ada_raw[:, a % 2, kk * D:(kk + 1) * D]
                        if k == 0:
                            ins = dve.tensor_scalar(acc[:, :], w, silu_c[:, 0, 0:1], None, ALU.mult)
                        else:
                            dve.wait_ge(unit_step, i * 9 + k)
                            ins = dve.scalar_tensor_tensor(out=acc[:, :], in0=w, scalar=silu_c[:, k, 0:1],
                                                           in1=acc[:, :], op0=ALU.mult, op1=ALU.add)
                        ins.then_inc(unit_step, 1)
                    dve.wait_ge(unit_step, i * 9 + (2 * a + 2))
                    dve.sem_inc(ada_used, 1)
                if 3 in parts:
                    dve.sem_inc(unit_step, 1)
                    dve.sem_inc(acc_ready, 1)

            def unit_store(i, b, col):
                dve.wait_ge(unit_summed, i + 1)
                dve.tensor_tensor(mod[:, bass.ds(i * KT + col, KT)], PS[:, b, 0:KT], vec[:, bass.ds(i * KT + col, KT)],
                                  ALU.add).then_inc(unit_done, 1)

            dve.sem_inc(hraw_ready, 2)
            dve.sem_inc(hid_lo_done, 2)
            dve.sem_inc(roped, 1)
            dve.wait_ge(silu_c_done, 2)
            for a in range(7):
                if a < 6:
                    dve.wait_ge(early_landed[a], 16)
                else:
                    dve.wait_ge(ada_landed[0], 32)
                for kk in range(2):
                    k = 2 * (a % 4) + kk
                    w = early_slab[a][:, kk * D:(kk + 1) * D]
                    for j in range(2):
                        to = pre[2 * (a // 4) + j]
                        step = (2 * a + kk) * 2 + j
                        if k == 0:
                            ins = dve.tensor_scalar(to, w, silu_c[:, 0, j:j + 1], None, ALU.mult)
                        else:
                            dve.wait_ge(pre_step, step - 1)
                            ins = dve.scalar_tensor_tensor(out=to, in0=w, scalar=silu_c[:, k, j:j + 1], in1=to,
                                                           op0=ALU.mult, op1=ALU.add)
                        ins.then_inc(pre_step, 1)
                dve.wait_ge(pre_step, 4 * (a + 1))
                if a in (0, 1, 6):
                    dve.sem_inc(ada_used, 1)
                if a in (3, 6):
                    dve.sem_inc(pre_ready, 1)
            dve.wait_ge(std_ready, 2)
            link(dve.reciprocal(rstd[:, :], std[:, :]))
            rest_slab(0, 0)
            dve.wait_ge(vec_landed, 16)
            dve.wait_ge(pre_summed, 1)
            sums = PS[:, 0:2, 0:2 * KT].rearrange("p u (m two) -> p u m two", two=2)
            both = lambda t: t[:, 0:2 * KT].rearrange("p (u m) -> p u m", u=2)
            dve.tensor_tensor(both(mod), sums[:, :, :, 0], both(vec), ALU.add).then_inc(mod0_summed, 1)
            dve.tensor_tensor(both(mod_ctx), sums[:, :, :, 1], both(vec), ALU.add).then_inc(mod0_summed, 1)
            dve.wait_ge(mod0_summed, 2)
            make_gain(0, VEC["norm_mix"], mod_ctx[:, KT:2 * KT])
            make_gain(1, VEC["norm_mix"], mod[:, KT:2 * KT])
            dve.sem_inc(gain_done, 1)
            dve.wait_ge(gain_done, 3)
            dve.sem_inc(banks_free, 8)
            g = lambda i: (lambda k: gain[:, i, k:k + 1])
            norm_tail("mix0", lambda k: x[:, k, :], g(1), lambda k: mod[:, k:k + 1],
                      lambda k: act_hi[:, k, :], lambda k: act_lo[:, k, :], T, rstd)
            rest_slab(1, 1)
            link(dve.reciprocal(rstd_c, std_c))
            norm_tail("ctx", lambda k: xc[:, k, :], g(0), lambda k: mod_ctx[:, k:k + 1],
                      lambda k: ctx_hi[:, k, :], lambda k: ctx_lo[:, k, :], C, rstd_c)

            dve.wait_ge(rope_landed, 16)
            dve.wait_ge(lo_ready, 2 * KT)
            RW = T // GRID_W
            row_cos, row_sin = rope[:, 0:RW], rope[:, RW:2 * RW]
            col_cos, col_sin = rope[:, 2 * RW:2 * RW + GRID_W], rope[:, 2 * RW + GRID_W:2 * RW + 2 * GRID_W]

            def table(tab, m, lo=0, hi=P):
                if m == 0:
                    return tab[lo:hi, :].unsqueeze(2).to_broadcast([hi - lo, RW, GRID_W])
                return tab[lo:hi, :].unsqueeze(1).to_broadcast([hi - lo, RW, GRID_W])

            def rotate(b, m, dst, count):
                grid = lambda ap: ap.rearrange("p (r c) -> p r c", c=GRID_W)
                cos, sin = ((row_cos, row_sin), (col_cos, col_sin))[m]
                dve.wait_ge(roped, count + 1)
                dve.tensor_tensor(grid(normed[:, 0, :]), grid(bank(b)), table(cos, m), ALU.mult).then_inc(rope_step, 1)
                dve.tensor_tensor(grid(normed[0:64, 1, :]), grid(PS[64:128, b, :]), table(sin, m, 64, 128),
                                  ALU.mult).then_inc(rope_step, 1)
                dve.tensor_tensor(grid(normed[64:128, 1, :]), grid(PS[0:64, b, :]), table(sin, m, 0, 64),
                                  ALU.mult).then_inc(rope_read, 1)
                dve.wait_ge(rope_step, count * 2 + 2)
                dve.wait_ge(rope_read, count + 1)
                dve.tensor_tensor(dst, normed[:, 0, :], normed[:, 1, :], ALU.add).then_inc(roped, 1)

            with dve.Fori(0, RH) as h:
                n0 = h * 8
                rest_slab(n0 + 2, 0)
                dve.wait_ge(slab_done, n0 + 1)
                for m in range(RDT):
                    rotate(m, m, rq[:, m, :], h * 4 + m)
                rest_slab(n0 + 3, 1)
                dve.wait_ge(slab_done, n0 + 2)
                for m in range(RDT):
                    rotate(2 + m, m, rk[:, m, 0:T], h * 4 + (2 + m))
                rest_slab(n0 + 4, 0)
                rest_slab(n0 + 5, 1)
                dve.wait_ge(toep_landed, h * 16 + 16)
                for t in range(KEYT):
                    off = (TT - 1 - t) * P if t < TT else TOEP_X + (KEYT - 1 - t) * P
                    dve.wait_ge(s_ready, h * 6 + (t + 1))
                    dve.tensor_tensor(rs[:, t, :], bank(BANK_S[t]), toep[:, off:off + T], ALU.mult).then_inc(s_decayed, 1)
                unit(h)
                rest_slab(n0 + 6, 0)
                dve.wait_ge(ostd_ready, h + 1)
                dve.reciprocal(rstd[:, :], std[:, :]).then_inc(orstd_done, 1)
                dve.wait_ge(orstd_done, h + 1)
                for e in range(RVT):
                    dve.tensor_tensor(rs[:, e, :], bank(BANK_O[e]), rstd[:, :], ALU.mult).then_inc(o_scaled, 1)
                for j in range(2):
                    for e in range(2 * j, 2 * j + 2):
                        dve.wait_ge(o_scaled, h * 4 + (e + 1))
                        dve.wait_ge(g_done, h * 4 + (e + 1))
                        dve.tensor_tensor(rs[:, e, :], rs[:, e, :], rg[:, e, :], ALU.mult).then_inc(ry_ready, 1)
                    for e in range(2 * j, 2 * j + 2):
                        dve.wait_ge(ry_hi_done, h * 4 + (e + 1))
                        dve.tensor_tensor(ry_lo[:, e, :], rs[:, e, :], ry_hi[:, e, :].bitcast(F32),
                                          ALU.subtract).then_inc(ry_lo_done, 1)
                    if j == 0:
                        unit_store(h, 5, 2 * KT)
                rest_slab(n0 + 7, 1)
                rest_slab(n0 + 8, 0)
                for s, m in enumerate(FIN):
                    if s < KT - 1:
                        dve.wait_ge(head_summed, h * (KT - 1) + (s + 1))
                    else:
                        dve.wait_ge(slab_done, n0 + 8)
                    dve.scalar_tensor_tensor(out=x[:, m, :], in0=bank(m), scalar=mod[:, mod_at(0, 2) + m:mod_at(0, 2) + m + 1],
                                             in1=x[:, m, :], op0=ALU.mult, op1=ALU.add).then_inc(banks_free, 1)
                rest_slab(n0 + 9, 1)

            def static_rest(n):
                if n < N_SLABS:
                    rest_slab(n, n)

            def up(n, tiles, seen, unit0=None, conv=False):
                with dve.Fori(0, tiles // 2) as i:
                    if unit0 is not None:
                        unit(i + unit0, (0, 1))
                    rest_slab(i * 2 + (n + 2), n)
                    if unit0 is not None:
                        unit(i + unit0, (2, 3))
                    dve.wait_ge(slab_done, i * 2 + (n + 2))
                    if conv:
                        for m in range(2):
                            dve.wait_ge(act_silu, i * 2 + (seen + m + 3))
                            dve.tensor_tensor(u[:, bass.ds(i * 2 + m, 1), 1:T + 1].rearrange("p o t -> p (o t)"),
                                              sg[:, m, :], bank(2 + m), ALU.mult).then_inc(hraw_ready, 1)
                    for m in range(0 if conv else 2):
                        dve.wait_ge(act_silu, i * 2 + (seen + m + 3))
                        dve.wait_ge(hid_lo_done, i * 2 + (seen + m + 1))
                        dve.tensor_tensor(hraw[:, m, :], sg[:, m, :], bank(2 + m), ALU.mult).then_inc(hraw_ready, 1)
                    rest_slab(i * 2 + (n + 3), n + 1)
                    for m in range(0 if conv else 2):
                        dve.wait_ge(hid_hi_done, i * 2 + (seen + m + 3))
                        t = bass.ds(i * 2 + m, 1)
                        dve.tensor_tensor(hid_lo[:, t, :].rearrange("p o t -> p (o t)"), hraw[:, m, :],
                                          hid_hi[:, t, :].rearrange("p o t -> p (o t)").bitcast(F32),
                                          ALU.subtract).then_inc(hid_lo_done, 1)
                    if unit0 is not None:
                            unit_store(i + unit0, 4, 2 * KT)

            def down(n, tiles, layer, lot, norm):
                full, rest = divmod(tiles // 2, 2)
                with dve.Fori(0, full - 1) as i:
                    rest_slab(i * 2 + (n + 2), n)
                    rest_slab(i * 2 + (n + 3), n + 1)
                for j in range(1 + rest):
                    static_rest(n + 2 * full + j)
                for s, m in enumerate(FIN):
                    if s < KT - 1:
                        dve.wait_ge(tile_summed, (KT - 1) * lot + s + 1)
                    else:
                        dve.wait_ge(slab_done, n + tiles // 2)
                    at = mod_at(layer, 5) + m
                    ins = dve.scalar_tensor_tensor(out=x[:, m, :], in0=bank(m), scalar=mod[:, at:at + 1],
                                                   in1=x[:, m, :], op0=ALU.mult, op1=ALU.add)
                    ins.then_inc(down_added, 1)
                    if norm and 2 <= s <= 6:
                        gather(norm, s - 1)

            def swiglu(n, seen, layer, unit0=None):
                for c, tiles in enumerate(FCH):
                    up(n, tiles, seen, unit0 if c == 0 else None)
                    n += tiles
                    seen += tiles
                    down(n, tiles, layer, 2 * layer + c, ("mix1", "final")[layer] if c else None)
                    n += tiles // 2
                    if c == 0:
                        static_rest(n + 1)

            def norm(name, gi, norm_col, layer, scale, shift):
                make_gain(gi, norm_col, mod[:, mod_at(layer, scale):mod_at(layer, scale) + KT])
                dve.wait_ge(gain_done, gi + 2)
                at = mod_at(layer, shift)
                norm_tail(name, lambda k: x[:, k, :], g(gi), lambda k: mod[:, at + k:at + k + 1],
                          lambda k: act_hi[:, k, :], lambda k: act_lo[:, k, :], T)

            norm("ffn0", 2, VEC["norm_ffn"], 0, 4, 3)
            swiglu(FFN0, 0, 0, RH)
            dve.memset(u[:, :, 0], 0.0).then_inc(pads_zero, 1)
            dve.memset(u[:, :, T + 1], 0.0).then_inc(pads_zero, 1)
            norm("mix1", 3, VEC["norm_mix"] + KT, 1, 1, 0)
            static_rest(CONV + 1)
            dve.sem_inc(conv_y, 2)
            up(CONV, KT, FT, None, True)
            dve.wait_ge(hraw_ready, 2 + FT + KT)
            dve.wait_ge(pads_zero, 2)
            dve.sem_inc(conv_y, 2)
            dve.sem_inc(wout_added, 4)
            tap = lambda k, t: vec[:, bass.ds(t + (VEC["conv_w"] + k * KT), 1)]
            with dve.Fori(0, 2) as i:
                for j in range(2):
                    n = CONV + 8 + j
                    for m in range(2):
                        c = 2 * j + m
                        t = i * 4 + c
                        ut = lambda k: u[:, bass.ds(t, 1), k:k + T].rearrange("p o t -> p (o t)")
                        dve.wait_ge(hid_lo_done, i * 4 + (FT + c + 1))
                        dve.tensor_scalar(hraw[:, m, :], ut(0), tap(0, t), None, ALU.mult).then_inc(conv_step, 1)
                        dve.wait_ge(conv_step, i * 12 + (3 * c + 1))
                        dve.scalar_tensor_tensor(out=hraw[:, m, :], in0=ut(1), scalar=tap(1, t), in1=hraw[:, m, :],
                                                 op0=ALU.mult, op1=ALU.add).then_inc(conv_step, 1)
                        dve.wait_ge(conv_step, i * 12 + (3 * c + 2))
                        dve.scalar_tensor_tensor(out=hraw[:, m, :], in0=ut(2), scalar=tap(2, t), in1=hraw[:, m, :],
                                                 op0=ALU.mult, op1=ALU.add).then_inc(conv_step, 1)
                    dve.wait_ge(slab_done, i * 2 + (n + 1))
                    for m in range(2):
                        c = 2 * j + m
                        dve.wait_ge(conv_step, i * 12 + (3 * c + 3))
                        dve.tensor_tensor(hraw[:, m, :], hraw[:, m, :], bank(c), ALU.mult).then_inc(conv_y, 1)
                    for m in range(2):
                        c = 2 * j + m
                        t = bass.ds(i * 4 + c, 1)
                        dve.wait_ge(hid_hi_done, i * 4 + (FT + c + 3))
                        dve.tensor_tensor(hid_lo[:, t, :].rearrange("p o t -> p (o t)"), hraw[:, m, :],
                                          hid_hi[:, t, :].rearrange("p o t -> p (o t)").bitcast(F32),
                                          ALU.subtract).then_inc(hid_lo_done, 1)
                    rest_slab(i * 2 + (n + 2), n)
            for j in range(4):
                if j:
                    gather("ffn1", 2 * j - 1)
                dve.wait_ge(slab_done, CONV + 12 + j + 1)
                for m in range(2):
                    k = 2 * j + m
                    at = mod_at(1, 2) + k
                    dve.scalar_tensor_tensor(out=x[:, k, :], in0=bank(k % 4), scalar=mod[:, at:at + 1], in1=x[:, k, :],
                                             op0=ALU.mult, op1=ALU.add).then_inc(wout_added, 1)
                if j in (1, 2):
                    gather("ffn1", 2 * j)
                if j < 3:
                    static_rest(CONV + 14 + j)
            norm("ffn1", 4, VEC["norm_ffn"] + KT, 1, 4, 3)
            static_rest(FFN1 + 1)
            swiglu(FFN1, FT + KT, 1)
            def norm_in(name, src, g, dst):
                dve.wait_ge(std_ready, nth(name) + 1)
                link(dve.reciprocal(rstd[:, :], std[:, :]))
                if dst is not None:
                    for k in range(KT):
                        dst(k)
                    return
                q = nth_split(name)

                def rest(k):
                    dve.wait_ge(hi_ready, 8 * q + k + 1)
                    dve.tensor_tensor(act_lo[:, k, :], normed[:, k % 2, :], act_hi[:, k, :].bitcast(F32),
                                      ALU.subtract).then_inc(lo_ready, 1)

                for k in range(KT):
                    dve.wait_ge(lo_ready, 8 * q + k - 1)
                    dve.scalar_tensor_tensor(out=normed[:, k % 2, :], in0=src(k), scalar=g(k), in1=rstd[:, :],
                                             op0=ALU.mult, op1=ALU.mult).then_inc(y_ready, 1)
                    if k:
                        rest(k - 1)
                rest(KT - 1)

            vcol = lambda name: (lambda k: vec[:, VEC[name] + k:VEC[name] + k + 1])
            x_tile = lambda k: x[:, k, :]

            def post(name, gain_name, done):
                g = vcol(gain_name)

                def add(k):
                    dve.wait_ge(post_step, base + k + 1)
                    dve.tensor_tensor(x[:, k, :], x[:, k, :], normed[:, k % 2, :], ALU.add).then_inc(done, 1)

                base = 0 if name == "post2" else KT

                def step(k):
                    if k >= 2:
                        dve.wait_ge(done, k - 1)
                    dve.scalar_tensor_tensor(out=normed[:, k % 2, :], in0=facc[:, k, :], scalar=g(k), in1=rstd[:, :],
                                             op0=ALU.mult, op1=ALU.mult).then_inc(post_step, 1)
                    if k:
                        add(k - 1)
                    if k == KT - 1:
                        add(k)

                norm_in(name, None, None, step)

            def final(k):
                dve.scalar_tensor_tensor(out=x[:, k, :], in0=x[:, k, :], scalar=vcol("final_norm")(k), in1=rstd[:, :],
                                         op0=ALU.mult, op1=ALU.mult).then_inc(final_done, 1)

            dve.sem_inc(conv2_done, 4)
            dve.sem_inc(cvin_done, 4)
            dve.sem_inc(silu2_done, 4)
            norm_in("final", None, None, final)
            dve.wait_ge(final_done, KT)
            static_rest(MIX + 1)
            norm_in("pre2", x_tile, vcol("mix_pre"), None)
            dve.wait_ge(pos_landed, 16)
            dve.wait_ge(con_landed, 16)
            R = slice(64, 128)
            a0, a1, a2, a3 = (cv[R, k, :] for k in range(4))
            TURN = 2.0 * np.pi
            C1 = 6.28125
            C2 = float(np.float32(np.round((TURN - C1) * 2 ** 20) / 2 ** 20))
            C3 = float(TURN - C1 - C2)
            MAGIC = 1.5 * 2 ** 23
            link(dve.tensor_copy(a1, pos_i[R, :]))
            link(dve.tensor_scalar(a1, a1, ccol("freq", 64, 128), None, ALU.mult))
            link(dve.tensor_scalar(a2, a1, 1.0 / TURN, ccol("turn", 64, 128), ALU.mult, ALU.add))
            link(dve.tensor_scalar(a2, a2, MAGIC, None, ALU.add))
            link(dve.tensor_scalar(a2, a2, -MAGIC, None, ALU.add))
            for step in (C1, C2, C3):
                link(dve.scalar_tensor_tensor(out=a1, in0=a2, scalar=-step, in1=a1, op0=ALU.mult, op1=ALU.add))
            link(dve.tensor_scalar(a1, a1, ccol("phase", 64, 128), float(np.float32(3.1415925)), ALU.add, ALU.min))
            dve.tensor_scalar(a3, a1, float(np.float32(-3.1415925)), None, ALU.max).then_inc(trig_ready, 1)
            dve.wait_ge(trig_done, 1)
            link(dve.tensor_scalar(csn[R, :], csn[R, :], ccol("sign", 64, 128), None, ALU.mult))
            n = MIX
            link(dve.memset(cvin[:, :, 0:3], 0.0))
            taps = lambda k, t: vec[:, bass.ds(t + (VEC["conv_w_2"] + k * NCONV), 1)]
            with dve.Fori(0, 3) as i:
                for j in range(2):
                    rest_slab(i * 2 + (n + j + 2), n + j)
                    for m in range(2):
                        c = 2 * j + m
                        t = i * 4 + c
                        dve.wait_ge(cvin_done, i * 4 + (c + 5))
                        dve.wait_ge(silu2_done, i * 4 + (c + 1))
                        dve.tensor_scalar(cv[:, c, :], cvin[:, c, 0:T], taps(0, t), None, ALU.mult).then_inc(conv2_step, 1)
                        for k in range(1, 4):
                            dve.wait_ge(conv2_step, i * 12 + (3 * c + k))
                            dve.scalar_tensor_tensor(out=cv[:, c, :], in0=cvin[:, c, k:k + T], scalar=taps(k, t), in1=cv[:, c, :],
                                                     op0=ALU.mult, op1=ALU.add).then_inc(conv2_step if k < 3 else conv2_done, 1)
            for j in range(4):
                static_rest(n + 8 + j)
            dve.wait_ge(slab_done, n + 10)
            dve.tensor_tensor(normed[64:96, 0, :], PS[64:96, 7, :], csn[64:96, :], ALU.mult).then_inc(trig_step, 1)
            dve.tensor_tensor(normed[64:96, 1, :], PS[96:128, 7, :], csn[96:128, :], ALU.mult).then_inc(trig_step, 1)
            dve.wait_ge(trig_step, 2)
            dve.tensor_tensor(krope[64:96, :], normed[64:96, 0, :], normed[64:96, 1, :], ALU.add).then_inc(krope_done, 1)
            link(dve.tensor_copy(ab[:, :, :], PS[:, 0, 0:TT * 8].rearrange("p (t e) -> p t e", t=TT)))
            dve.sem_inc(ab_done, 1)
            for k in range(3):
                if k != 1:
                    dve.wait_ge(mstd_done, k // 2 + 1)
                    link(dve.reciprocal(mstd[:, k // 2, :], mstd[:, k // 2, :]))
                g = vcol("q_norm")(k) if k < 2 else vcol("kv_norm")(0)
                dve.scalar_tensor_tensor(out=cqr[:, k, :], in0=cqr[:, k, :], scalar=g, in1=mstd[:, k // 2, :],
                                         op0=ALU.mult, op1=ALU.mult).then_inc(mc_ready, 1)
            dve.wait_ge(heads_landed, 16)
            per = lambda ap: ap.unsqueeze(1).to_broadcast([P, TT, GH])
            link(dve.tensor_tensor(cols[:, GL, :, :], ab[:, :, 0:GH], per(heads_c[:, GH:2 * GH]), ALU.add))
            link(dve.tensor_scalar(cols[:, KD, :, :], cols[:, GL, :, :], 0.0, None, ALU.max))
            dve.scalar_tensor_tensor(out=cols[:, TMP, :, :], in0=cols[:, KD, :, :], scalar=-2.0, in1=cols[:, GL, :, :],
                                     op0=ALU.mult, op1=ALU.add).then_inc(soft1, 1)
            dve.wait_ge(soft2, 3)
            link(dve.tensor_tensor(cols[:, EG, :, :], cols[:, KD, :, :], cols[:, EG, :, :], ALU.add))
            dve.scalar_tensor_tensor(out=rowsrc[:, :, 0:GH], in0=cols[:, EG, :, :], scalar=-1.0, in1=per(small[:, 0, :]),
                                     op0=ALU.mult, op1=ALU.mult).then_inc(cols_done, 1)
            for k in range(3):
                dve.wait_ge(mc_hi_done, k + 1)
                dve.tensor_tensor(mc_lo[:, k, :], cqr[:, k, :], mc_hi[:, k, :].bitcast(F32), ALU.subtract).then_inc(mc_lo_done, 1)
            dve.wait_ge(beta1, 1)
            link(dve.tensor_scalar(cols[:, BETA, :, :], cols[:, BETA, :, :], 1.0, None, ALU.add))
            link(dve.reciprocal(cols[:, BETA, :, :], cols[:, BETA, :, :]))
            dve.wait_ge(ssd_done, 1)
            link(dve.reciprocal(ssqk[:, :, :], ssqk[:, :, :]))
            link(dve.tensor_scalar(rowsrc[:, :, 2 * GH:3 * GH], ssqk[:, :, 0:GH], float(P) ** -0.5, None, ALU.mult))
            link(dve.tensor_copy(cols[:, RK, :, :], ssqk[:, :, GH:2 * GH]))
            link(dve.tensor_tensor(rowsrc[:, :, GH:2 * GH], cols[:, BETA, :, :], cols[:, RK, :, :], ALU.mult))
            dve.wait_ge(gcum_ready, 1)
            dve.tensor_copy(cols[:, GCOL, :, :], PS[:, 2, 0:TT * GH].rearrange("p (c h) -> p c h", c=TT)).then_inc(cols_done, 1)
            def head_rope(h):
                dve.wait_ge(q_ready, h + 1)
                if h:
                    dve.wait_ge(qr_done, h)
                if h >= 2:
                    dve.wait_ge(ms_ready, 4 * (h - 1))
                dve.tensor_tensor(normed[64:96, 0, :], PS[64:96, 0, :], csn[64:96, :], ALU.mult).then_inc(trig_step, 1)
                dve.tensor_tensor(normed[64:96, 1, :], PS[96:128, 0, :], csn[96:128, :], ALU.mult).then_inc(trig_step, 1)
                dve.wait_ge(trig_step, 2 * h + 4)
                dve.tensor_tensor(qh[64:96, h % 2, :], normed[64:96, 0, :], normed[64:96, 1, :], ALU.add).then_inc(qr_done, 1)

            def row_max(h, t):
                g = 4 * h + t
                dve.wait_ge(ms_ready, g + 1)
                if h:
                    dve.wait_ge(exp_done, g - 3)
                link(dve.tensor_reduce(small[:, 0, t:t + 1], PS[:, 2 + t, 0:(t + 1) * P], AX.X, ALU.max))
                dve.tensor_scalar(small[:, 1, t:t + 1], small[:, 0, t:t + 1], -(QK ** -0.5), None, ALU.mult).then_inc(nmx_done, 1)

            def weigh(h, t):
                dve.wait_ge(exp_done, 4 * h + t + 1)
                link(dve.reciprocal(small[:, 2, t:t + 1], small[:, 2, t:t + 1]))
                p = pr[t][:, 0:(t + 1) * P]
                dve.tensor_scalar(p, p, small[:, 2, t:t + 1], None, ALU.mult).then_inc(p_ready, 1)

            dve.wait_ge(krope_done, 1)
            head_rope(0)
            for h in range(MH + 1):
                for t in range(TT):
                    if h < MH:
                        row_max(h, t)
                if h == 0:
                    dve.wait_ge(soft2, 4)
                    link(dve.tensor_tensor(cols[:, KBS, :, :], rowsrc[:, :, GH:2 * GH], cols[:, EG, :, :], ALU.mult))
                if h + 1 < MH:
                    head_rope(h + 1)
                for t in range(TT):
                    if h < MH:
                        weigh(h, t)
                if h and h % 2 == 0:
                    dve.wait_ge(mo_hi_done, h // 2)
                    dve.tensor_tensor(act_lo[:, 3 + h // 2, :], bank(7), act_hi[:, 3 + h // 2, :].bitcast(F32),
                                      ALU.subtract).then_inc(mo_lo_done, 1)

            dve.wait_ge(o2_ready, MH)
            wide = lambda ap: ap.unsqueeze(1).to_broadcast([P, GH, P])
            level = lambda s: wide(con[:, CON["levels"] + s * P:CON["levels"] + (s + 1) * P])

            def spread(c):
                dve.tensor_copy(bcs[:, :, :], rowsrc[:, c, :].unsqueeze(2).to_broadcast([P, 3 * GH, P])).then_inc(bcs_done, 1)

            spread(0)
            for c in range(TT):
                dve.wait_ge(rows_ready, c + 1)
                link(dve.tensor_copy(cols[:, GL, c, :], hb(bank(0))[:, :, P - 1]))
                dve.tensor_tensor(cols[:, KD, c, :], cols[:, GL, c, :], cols[:, GCOL, c, :], ALU.subtract).then_inc(kd_raw, 1)
                if c:
                    dve.wait_ge(ptm_done, GH * c)
                for h in range(GH):
                    dve.scalar_tensor_tensor(out=ex[:, hs(h)], in0=PS[:, 0, hs(h)], scalar=col(GCOL, c, h), in1=cc("causal"),
                                             op0=ALU.subtract, op1=ALU.add).then_inc(eraw_done, 1)
                if c + 1 < TT:
                    spread(c + 1)
                dve.wait_ge(kd_exp, 3 * c + 2)
                link(dve.tensor_tensor(cols[:, KDS, c, :], cols[:, KDS, c, :], cols[:, RK, c, :], ALU.mult))
                dve.sem_inc(kd_done, 1)
                dve.wait_ge(kq_ready, c + 1)
                dve.wait_ge(e_done, c + 1)
                for h in range(GH):
                    dve.scalar_tensor_tensor(out=mt[:, c, hs(h)], in0=PS[:, 3, hs(h)], scalar=col(RK, c, h), in1=ex[:, hs(h)],
                                             op0=ALU.mult, op1=ALU.mult).then_inc(mt_done, 1)
                for h in range(GH):
                    dve.scalar_tensor_tensor(out=ptm[:, c, hs(h)], in0=PS[:, 4, hs(h)], scalar=col(RK, c, h), in1=ex[:, hs(h)],
                                             op0=ALU.mult, op1=ALU.mult).then_inc(ptm_done, 1)
                dve.wait_ge(kd_exp, 3 * c + 3)
                link(dve.tensor_tensor(egrow[:, :], egrow[:, :], bank(2), ALU.mult))
                dve.wait_ge(ptm_done, GH * (c + 1))
                link(dve.tensor_tensor(ptm[:, c, :], ptm[:, c, :], bank(2), ALU.mult))
                dve.wait_ge(mt_done, GH * (c + 1))
                dve.tensor_tensor(mt[:, c, :], mt[:, c, :], bank(1), ALU.mult).then_inc(rows_used, 1)
                dve.tensor_tensor(qkv[:, 0:GH, c * P:(c + 1) * P], qkv[:, 0:GH, c * P:(c + 1) * P], hb(egrow[:, :]),
                                  ALU.mult).then_inc(qdec_done, 1)
                dve.wait_ge(rows_used, c + 1)
                link(dve.tensor_tensor(hb(gy[:, c, :]), hb(mt[:, c, :]), level(0), ALU.mult))
                dve.tensor_tensor(hb(gy[:, c, :]), wide(cc("ident")), hb(gy[:, c, :]), ALU.subtract).then_inc(y0_done, 1)

            def mask_level(g):
                if g >= 2:
                    dve.wait_ge(lp_ready, g - 1)
                dve.tensor_tensor(hb(lv[:, g % 2, :]), hb(mt[:, g % TT, :]), level(g // TT + 1), ALU.mult).then_inc(lv_done, 1)

            G = (LEVELS - 1) * TT
            mask_level(0)
            mask_level(1)
            dve.wait_ge(y0_done, TT)
            dve.wait_ge(x0_done, TT)
            for g in range(G):
                if g in (4, 8):
                    static_rest(n + 11 + g // 4)
                if g + 2 < G:
                    mask_level(g + 2)
                c = g % TT
                dve.wait_ge(xx_ready, g + 1)
                if g >= TT:
                    dve.wait_ge(xy_done, 2 * (g - TT + 1))
                dve.tensor_tensor(gx[:, c, :], gx[:, c, :], bank(2 + g % 2), ALU.subtract).then_inc(xy_done, 1)
                dve.tensor_tensor(gy[:, c, :], gy[:, c, :], bank(4 + g % 2), ALU.subtract).then_inc(xy_done, 1)
            for c in range(TT):
                dve.wait_ge(uw_ready, c + 1)
                dve.tensor_copy(gp[:, c, :], bank(7)).then_inc(wt_done, 1)
            dve.wait_ge(u_done, TT)
            def out_norm(c):
                at = oT[:, :, c * P:(c + 1) * P]
                dve.wait_ge(gstd_done, c + 1)
                dve.wait_ge(o3_done, c + 1)
                link(dve.reciprocal(gstd[:, c, :], gstd[:, c, :]))
                link(dve.scalar_tensor_tensor(out=at, in0=at, scalar=vcol("gdn_out")(0), in1=hb(gstd[:, c, :]),
                                              op0=ALU.mult, op1=ALU.mult))
                dve.tensor_tensor(at, at, gate[:, :, c * P:(c + 1) * P], ALU.mult).then_inc(go_ready, 1)

            def out_lo(c):
                tile = slice(c * P, (c + 1) * P)
                dve.wait_ge(go_hi_done, c + 1)
                dve.tensor_tensor(act_lo[:, 0:GH, tile], oT[:, :, tile], act_hi[:, 0:GH, tile].bitcast(F32),
                                  ALU.subtract).then_inc(go_lo_done, 1)

            for c in range(TT):
                if c == 0:
                    dve.sem_inc(vn_done, 1)
                else:
                    dve.wait_ge(ws_ready, c)
                    dve.tensor_tensor(gx[:, c, :], gx[:, c, :], bank(0), ALU.subtract).then_inc(vn_done, 1)
                if c + 1 < TT:
                    dve.wait_ge(sup_ready, c + 1)
                    if c:
                        dve.wait_ge(o3_ready, c + 1)
                    for h in range(GH):
                        if c == 0:
                            ins = dve.tensor_copy(state[:, h, :], PS[:, 2, hs(h)])
                        else:
                            ins = dve.scalar_tensor_tensor(out=state[:, h, :], in0=state[:, h, :], scalar=col(EGL, c, h),
                                                           in1=PS[:, 2, hs(h)], op0=ALU.mult, op1=ALU.add)
                        ins.then_inc(state_done, 1)
                    dve.wait_ge(state_done, GH * (c + 1))
                if c:
                    out_norm(c - 1)
                if c >= 2:
                    out_lo(c - 2)
            out_norm(TT - 1)
            out_lo(TT - 2)
            out_lo(TT - 1)
            for j in range(3):
                static_rest(n + 14 + j)
                for k in range(max(2 * j, 1), 2 * j + 2):
                    gather("post2", k)
            post("post2", "mix_post", post_done)
            static_rest(n + 17)

            dve.sem_inc(relu_done, 4)
            dve.sem_inc(sqr_done, 2)
            dve.sem_inc(h2_lo_done, 2)
            norm_in("ffn2", x_tile, vcol("ffn_pre"), None)
            n, seen = FFN2, 0
            for c, tiles in enumerate(F2CH):
                with dve.Fori(0, tiles // 4) as i:
                    for j in range(2):
                        for m in range(2):
                            t = 2 * j + m
                            dve.wait_ge(relu_done, i * 4 + (seen + t + 5))
                            dve.wait_ge(h2_lo_done, i * 4 + (seen + t + 1))
                            dve.tensor_tensor(hraw2[:, m, :], sg2[:, m, :], sg2[:, m, :], ALU.mult).then_inc(sqr_done, 1)
                        rest_slab(i * 2 + (n + j + 2), n + j)
                        for m in range(2):
                            t = 2 * j + m
                            dve.wait_ge(h2_hi_done, i * 4 + (seen + t + 1))
                            at = bass.ds(i * 4 + t, 1)
                            dve.tensor_tensor(hid2_lo[:, at, :].rearrange("p o t -> p (o t)"), hraw2[:, m, :],
                                              hid2_hi[:, at, :].rearrange("p o t -> p (o t)").bitcast(F32),
                                              ALU.subtract).then_inc(h2_lo_done, 1)
                n += tiles // 2
                seen += tiles
                with dve.Fori(0, tiles // 4 - 1) as i:
                    rest_slab(i * 2 + (n + 2), n)
                    rest_slab(i * 2 + (n + 3), n + 1)
                n += tiles // 2
                static_rest(n)
                static_rest(n + 1)
            dve.wait_ge(f2_copied, KT)
            for s, b in enumerate(FIN):
                if s < KT - 1:
                    dve.wait_ge(tile_summed, (KT - 1) * 5 + s + 1)
                else:
                    dve.wait_ge(slab_done, N_SLABS)
                dve.tensor_tensor(facc[:, b, :], facc[:, b, :], bank(b), ALU.add).then_inc(f_done, 1)
                if 2 <= s <= 6:
                    gather("last", s - 1)
            dve.wait_ge(f_done, KT)
            post("last", "ffn_post", x_final)


def decay_tables():
    h = np.arange(RH, dtype=np.float64)
    lf = np.log1p(-np.exp2(-5.0 - h))[:, None, None]
    lb = np.log1p(-np.exp2(-5.5 - h))[:, None, None]
    dx = (np.arange(TOEP_X)[None, :] - (TT - 1) * P - np.arange(P)[:, None])[None]
    fwd = np.where(dx >= 0, np.exp(np.maximum(dx, 0) * lf), 0.0)
    bwd = np.where(dx <= 0, np.exp(np.maximum(-dx, 0) * lb), 0.0)
    dc = (np.arange(TOEP_C)[None, :] - (CT - 1) * P - np.arange(P)[:, None])[None]
    both = np.exp((dc + C) * lf) + np.exp((T - dc) * lb)
    tab = np.concatenate([fwd + bwd, both], axis=2) / np.sqrt(RD)
    return np.concatenate([tab, tab[-1:]], axis=0).astype(np.float32)


def rope1_table():
    n = RD // 4
    freq = 10000.0 ** (-np.arange(n, dtype=np.float32) / n)
    both = np.concatenate([freq, freq]).astype(np.float32)[:, None]
    sign = np.concatenate([np.ones(n), -np.ones(n)])[:, None]
    row = both * np.arange(T // GRID_W, dtype=np.float32)[None]
    col = both * np.arange(GRID_W, dtype=np.float32)[None]
    return np.concatenate([np.cos(row), sign * np.sin(row), np.cos(col), sign * np.sin(col)], axis=1).astype(np.float32)


def constant_table():
    i = np.arange(P)
    key, query = i[:, None], i[None, :]
    tab = np.zeros((P, N_CON), np.float64)

    def put(name, v):
        v = np.asarray(v, np.float64).reshape(P, -1)
        tab[:, CON[name]:CON[name] + v.shape[1]] = v

    put("ident", np.eye(P))
    put("upper", key <= query)
    put("causal", np.where(query >= key, 0.0, NEG))
    put("mask_q", (key == 0) & (query < 64))
    put("mask_k", np.where((key == 0) & (query >= 64), NEG, 0.0))
    levels = []
    for s in range(LEVELS):
        b = 2 ** s
        levels.append((query // b % 2 == 1) & (key // b == query // b - 1))
    put("levels", np.concatenate(levels, axis=1))
    inv = 10000.0 ** (-np.arange(0, ROPE, 2, dtype=np.float32) / ROPE)
    r = i - 64
    freq = np.where(r >= 0, inv[r % (ROPE // 2)], 0.0)
    cosine = (r >= 0) & (r < ROPE)
    put("freq", freq)
    put("turn", np.where(cosine, 0.25, 0.0))
    put("phase", np.where(cosine, np.pi / 2, 0.0))
    put("sign", np.where((r >= ROPE) & (r < ROPE + ROPE // 2), -1.0, 1.0))
    return tab.astype(np.float32)


def by_columns(w, c0):
    return w[:, c0:c0 + 256].reshape(KT, P, 256).transpose(1, 0, 2).reshape(P, SLAB)


def by_rows(w, r0):
    return w[r0:r0 + 256].reshape(2, P, D).transpose(1, 0, 2).reshape(P, SLAB)


def value_slab(w, r0, c0):
    return w[r0:r0 + 512, c0:c0 + 512].reshape(4, P, 512).transpose(1, 0, 2).reshape(P, SLAB)


def swiglu_slabs(w1, w3, w2):
    out, t0 = [], 0
    for tiles in FCH:
        for t in range(t0, t0 + tiles, 2):
            out += [by_columns(w1, t * P), by_columns(w3, t * P)]
        out += [by_rows(w2, t * P) for t in range(t0, t0 + tiles, 2)]
        t0 += tiles
    return out


def slab_stream(a):
    out = []
    w, wo = a["ret_w_qkvg"][0], a["ret_w_o"][0]
    for h in range(RH):
        out += [by_columns(w, h * RD), by_columns(w, D + h * RD)]
        out += [value_slab(w, r, 2 * D + h * RV) for r in (0, 512)]
        out += [by_columns(w, 4 * D + h * RV + c) for c in (0, 256)]
        out += [by_rows(wo, h * RV + r) for r in (0, 256)]
    out += swiglu_slabs(a["ffn_w1"][0], a["ffn_w3"][0], a["ffn_w2"][0])
    w, wo = a["conv_w_in"][0], a["conv_w_out"][0]
    for t in range(0, KT, 2):
        out += [by_columns(w, D + t * P), by_columns(w, 2 * D + t * P)]
    out += [by_columns(w, c) for c in range(0, D, 256)]
    out += [by_columns(wo, c) for c in range(0, D, 256)]
    out += swiglu_slabs(a["ffn_w1"][1], a["ffn_w3"][1], a["ffn_w2"][1])
    w = a["w_in_2"][0]
    g, swap = GH * P, np.r_[ROPE // 2:ROPE, 0:ROPE // 2]
    out += [by_columns(w, c) for c in range(0, 4 * g, 256)]
    ab, cq = w[:, 4 * g:4 * g + 2 * GH], w[:, 4 * g + 2 * GH:4 * g + 2 * GH + 256]
    ckv, kr = w[:, -(P + ROPE):-ROPE], w[:, -ROPE:]
    out.append(by_columns(cq, 0))
    blank = np.zeros((D, 64 - 2 * GH), np.float32)
    out.append(by_columns(np.concatenate([ckv, ab, blank, kr, kr[:, swap]], axis=1), 0))
    qu = a["w_q_up_2"][0].reshape(2 * P, MH, QK)
    out.append(by_rows(np.concatenate([qu, qu[:, :, NOPE:][:, :, swap]], axis=2).reshape(2 * P, D), 0))
    kv = a["w_kv_up_2"][0].reshape(P, MH, NOPE + MV)
    out.append(np.concatenate([kv[:, :, :NOPE].reshape(P, -1), kv[:, :, NOPE:].reshape(P, -1),
                               np.zeros((P, SLAB - D), np.float32)], axis=1))
    out += [by_columns(a["w_out_2"][0], c) for c in range(0, D, 256)]
    t0 = 0
    for tiles in F2CH:
        out += [by_columns(a["w_up_2"][0], t * P) for t in range(t0, t0 + tiles, 2)]
        out += [by_rows(a["w_down_2"][0], t * P) for t in range(t0, t0 + tiles, 2)]
        t0 += tiles
    return np.stack(out)


def feature_major(t):
    return np.ascontiguousarray(t.T.reshape(-1, P, t.shape[0]).transpose(1, 0, 2))


def vector_table(a):
    rows = [a["ada_b"].reshape(-1), a["c"].reshape(-1), a["c_ctx"], a["norm_mix"].reshape(-1),
            a["norm_ffn"].reshape(-1), a["final_norm"], a["mix_pre_norm_2"][0], a["mix_post_norm_2"][0],
            a["ffn_pre_norm_2"][0], a["ffn_post_norm_2"][0], a["conv_w"][0].reshape(-1), a["conv_w_2"][0].reshape(-1),
            a["gdn_out_norm_2"][0], a["q_norm_2"][0], a["kv_norm_2"][0]]
    return np.ascontiguousarray(np.concatenate(rows).reshape(-1, P).T)


def kernel(**inputs):
    import concourse.bacc as _bacc
    from concourse.bass_utils import run_bass_kernel_spmd as _run

    a = {k: np.asarray(v) for k, v in inputs.items()}
    arrays = {
        "slabs": slab_stream(a),
        "ada": np.stack([by_rows(a["ada_w"][l][:, u * D:(u + 1) * D], r * 256)
                         for l in range(2) for u in range(6) for r in range(4)]),
        "x_t": feature_major(a["x"][0]),
        "ctx_t": feature_major(a["ctx"][0]),
        "vecs": vector_table(a),
        "decay": decay_tables(),
        "rope1": rope1_table(),
        "consts": constant_table(),
        "positions": np.ascontiguousarray(np.broadcast_to(a["positions_2"], (P, T))),
        "per_head": np.ascontiguousarray(np.broadcast_to(
            np.concatenate([a["a_log_2"][0], a["dt_bias_2"][0]])[None], (P, 2 * GH))),
    }
    nc = _bacc.Bacc("TRN2", target_bir_lowering=False, num_devices=1)
    args = [nc.dram_tensor(name, v.shape, mybir.dt.from_np(v.dtype), kind="ExternalInput").ap()
            for name, v in arrays.items()]
    args.append(nc.dram_tensor("out_t", (P, KT, T), F32, kind="ExternalOutput").ap())
    build(nc, *args)
    r = _run(nc, [arrays], core_ids=[0])
    got = r.results[0]["out_t"]
    return np.ascontiguousarray(got.transpose(1, 0, 2).reshape(D, T).T)[None]
```
